# Optimizing a Trainium2 kernel written in Bass

```python
import jax, jax.numpy as jnp
from jax import lax
import numpy as np
import math

D_MODEL = 1024
BATCH = 1
SEQ = 256
DEPTH = 2

N_HEADS = 8
N_KV_HEADS = 2
HEAD_DIM = 64
ATTN_WIDTH = N_HEADS * HEAD_DIM
KV_WIDTH = N_KV_HEADS * HEAD_DIM
WINDOW = 128
ROT_DIM = HEAD_DIM // 4
ROPE_THETA = 500000.0
HGRN_HEADS = 4
HGRN_HEAD_DIM = 128
HGRN_WIDTH = HGRN_HEADS * HGRN_HEAD_DIM
CHUNK = 64
NORM_EPS = 1e-6
MASK_VALUE = -1e30
SPLITS = (ATTN_WIDTH, KV_WIDTH, KV_WIDTH, ATTN_WIDTH,
          HGRN_WIDTH, HGRN_WIDTH, HGRN_WIDTH, HGRN_WIDTH,
          D_MODEL, D_MODEL)
IN_WIDTH = 2 * ATTN_WIDTH + 2 * KV_WIDTH + 4 * HGRN_WIDTH + 2 * D_MODEL


def rms_norm(x, w):
    xf = x.astype(jnp.float32)
    y = xf * lax.rsqrt(jnp.mean(xf * xf, axis=-1, keepdims=True) + NORM_EPS)
    return (y * w.astype(jnp.float32)).astype(x.dtype)

def partial_rope(x, positions):
    half = ROT_DIM // 2
    inv_freq = jnp.power(ROPE_THETA, -jnp.arange(half, dtype=jnp.float32) * (2.0 / ROT_DIM))
    ang = positions.astype(jnp.float32)[..., None] * inv_freq
    cos = jnp.cos(ang)[:, :, None, :]
    sin = jnp.sin(ang)[:, :, None, :]
    xr = x[..., :ROT_DIM].astype(jnp.float32)
    x1, x2 = xr[..., :half], xr[..., half:]
    rot = jnp.concatenate([x1 * cos - x2 * sin, x2 * cos + x1 * sin], axis=-1)
    return jnp.concatenate([rot.astype(x.dtype), x[..., ROT_DIM:]], axis=-1)

def sliding_window_attention(q, k, v, sinks):
    B, T = q.shape[0], q.shape[1]
    nb = T // WINDOW
    G = N_HEADS // N_KV_HEADS
    qb = q.astype(jnp.float32).reshape(B, nb, WINDOW, N_KV_HEADS, G, HEAD_DIM) * (HEAD_DIM ** -0.5)

    def band(a):
        a = a.astype(jnp.float32).reshape(B, nb, WINDOW, N_KV_HEADS, HEAD_DIM)
        prev = jnp.pad(a[:, :-1], ((0, 0), (1, 0), (0, 0), (0, 0), (0, 0)))
        return jnp.concatenate([prev, a], axis=2)

    kb, vb = band(k), band(v)
    blk = jnp.arange(nb)[:, None]
    qpos = blk * WINDOW + jnp.arange(WINDOW)[None, :]
    kpos = (blk - 1) * WINDOW + jnp.arange(2 * WINDOW)[None, :]
    delta = qpos[:, :, None] - kpos[:, None, :]
    mask = (delta >= 0) & (delta < WINDOW) & (kpos[:, None, :] >= 0)
    s = jnp.einsum('bnqhgd,bnkhd->bhgnqk', qb, kb)
    s = jnp.where(mask, s, MASK_VALUE)
    sink = sinks.astype(jnp.float32).reshape(N_KV_HEADS, G)[None, :, :, None, None, None]
    m = jnp.maximum(jnp.max(s, axis=-1, keepdims=True), sink)
    p = jnp.exp(s - m)
    p = p / (jnp.sum(p, axis=-1, keepdims=True) + jnp.exp(sink - m))
    o = jnp.einsum('bhgnqk,bnkhd->bnqhgd', p, vb)
    return o.reshape(B, T, ATTN_WIDTH)

def hgrn2_recurrence(q, k, v, logf):
    B, T, H, Dk = q.shape
    Dv = v.shape[-1]
    n = T // CHUNK

    def chunks(a):
        return a.reshape(B, n, CHUNK, H, a.shape[-1]).transpose(1, 0, 3, 2, 4)

    causal = jnp.tril(jnp.ones((CHUNK, CHUNK), dtype=bool))[:, :, None]

    def step(S, blk):
        qc, kc, vc, gc = blk
        G = jnp.cumsum(gc, axis=-2)
        diff = G[:, :, :, None, :] - G[:, :, None, :, :]
        decay = jnp.exp(jnp.where(causal, diff, MASK_VALUE))
        scores = jnp.einsum('bhtd,bhsd,bhtsd->bhts', qc, kc, decay)
        o = (jnp.einsum('bhts,bhsv->bhtv', scores, vc)
             + jnp.einsum('bhtd,bhdv->bhtv', qc * jnp.exp(G), S))
        G_end = G[:, :, -1:, :]
        S = (S * jnp.exp(G_end)[:, :, 0, :, None]
             + jnp.einsum('bhsd,bhsv->bhdv', kc * jnp.exp(G_end - G), vc))
        return S, o

    S0 = jnp.zeros((B, H, Dk, Dv), jnp.float32)
    _, o = lax.scan(step, S0, (chunks(q), chunks(k), chunks(v), chunks(logf)))
    return o.transpose(1, 0, 3, 2, 4).reshape(B, T, H, Dv)

def first_inputs(seed: int = 0) -> dict:
    key = jax.random.key(seed)
    ks = jax.random.split(key, 12)
    f32 = jnp.float32
    x = jax.random.normal(ks[0], (BATCH, SEQ, D_MODEL), f32)
    offsets = jax.random.randint(ks[1], (BATCH, 1), 0, 1024, dtype=jnp.int32)
    positions = (jnp.arange(SEQ, dtype=jnp.int32)[None, :] + offsets).astype(jnp.int32)
    norm_w = 1.0 + 0.02 * jax.random.normal(ks[2], (DEPTH, D_MODEL), f32)
    w_in = jax.random.normal(ks[3], (DEPTH, D_MODEL, IN_WIDTH), f32) * D_MODEL ** -0.5
    attn_sinks = 0.5 * jax.random.normal(ks[4], (DEPTH, N_HEADS), f32)
    hgrn_norm_w = 1.0 + 0.02 * jax.random.normal(ks[5], (DEPTH, HGRN_HEAD_DIM), f32)
    w_up_attn = jax.random.normal(ks[6], (DEPTH, ATTN_WIDTH, D_MODEL), f32) * ATTN_WIDTH ** -0.5
    w_up_hgrn = jax.random.normal(ks[7], (DEPTH, HGRN_WIDTH, D_MODEL), f32) * HGRN_WIDTH ** -0.5
    w_out = jax.random.normal(ks[8], (DEPTH, D_MODEL, D_MODEL), f32) * D_MODEL ** -0.5
    lb_logits = 0.1 * jax.random.normal(ks[9], (DEPTH, HGRN_WIDTH), f32)
    final_norm_w = 1.0 + 0.02 * jax.random.normal(ks[10], (D_MODEL,), f32)
    return {'x': x, 'positions': positions, 'norm_w': norm_w, 'w_in': w_in,
            'attn_sinks': attn_sinks, 'hgrn_norm_w': hgrn_norm_w, 'w_up_attn': w_up_attn,
            'w_up_hgrn': w_up_hgrn, 'w_out': w_out, 'lb_logits': lb_logits,
            'final_norm_w': final_norm_w}

def first_block(x, positions, norm_w, w_in, attn_sinks, hgrn_norm_w, w_up_attn, w_up_hgrn,
              w_out, lb_logits, final_norm_w):
    B, T, _ = x.shape
    split_points = [int(s) for s in np.cumsum(SPLITS)[:-1]]
    lb_soft = jax.nn.softmax(lb_logits.astype(jnp.float32), axis=0)
    lb_all = jnp.cumsum(lb_soft, axis=0) - lb_soft[0]

    for layer in range(DEPTH):
        h = rms_norm(x, norm_w[layer])
        proj = h @ w_in[layer]
        (q, k, v, z_attn, q_h, f_h, i_h, g_h, gate_attn, gate_hgrn) = jnp.split(proj, split_points, axis=-1)

        q = partial_rope(q.reshape(B, T, N_HEADS, HEAD_DIM), positions)
        k = partial_rope(k.reshape(B, T, N_KV_HEADS, HEAD_DIM), positions)
        v = v.reshape(B, T, N_KV_HEADS, HEAD_DIM)
        a = sliding_window_attention(q, k, v, attn_sinks[layer]).astype(x.dtype) * jax.nn.silu(z_attn)

        lb = lb_all[layer]
        fx = f_h.astype(jnp.float32)
        logf = jnp.log(lb + (1.0 - lb) * jax.nn.sigmoid(fx))
        kin = (1.0 - lb) * jax.nn.sigmoid(-fx)
        qin = jax.nn.silu(q_h.astype(jnp.float32))
        heads = lambda t: t.reshape(B, T, HGRN_HEADS, HGRN_HEAD_DIM)
        o = hgrn2_recurrence(heads(qin), heads(kin), heads(i_h.astype(jnp.float32)), heads(logf))
        o = o * lax.rsqrt(jnp.mean(o * o, axis=-1, keepdims=True) + NORM_EPS) * hgrn_norm_w[layer].astype(jnp.float32)
        b = o.reshape(B, T, HGRN_WIDTH).astype(x.dtype) * jax.nn.silu(g_h)

        merged = (jax.nn.sigmoid(gate_attn) * (a @ w_up_attn[layer])
                  + jax.nn.sigmoid(gate_hgrn) * (b @ w_up_hgrn[layer]))
        x = x + merged @ w_out[layer]

    return rms_norm(x, final_norm_w)


N_MIXERS = 2
N_A = (DEPTH + 1) // 2
N_B = DEPTH // 2
A_HEADS = 16
A_QK_DIM = 64
A_V_DIM = 64
A_KV_RANK = 256
IDX_HEADS = 8
IDX_DIM = 64
TOPK_MAX = 256
A_SPLITS = [A_HEADS * A_QK_DIM,
            A_HEADS * A_QK_DIM + A_KV_RANK,
            A_HEADS * A_QK_DIM + A_KV_RANK + IDX_HEADS * IDX_DIM,
            A_HEADS * A_QK_DIM + A_KV_RANK + IDX_HEADS * IDX_DIM + IDX_DIM]
A_IN = A_SPLITS[-1] + IDX_HEADS
B_HEADS = 8
B_HEAD_DIM = 64
B_QK = 2 * B_HEADS * B_HEAD_DIM
B_IN = 3 * B_QK
REL_BUCKETS = 32
REL_MAX_DIST = 128
BIAS_HEADS = A_HEADS
D_FF = 4 * D_MODEL
Q_BLOCK = 128
LN_EPS = 1e-5
NEG = -1e30
DN_ALPHA = (2 * DEPTH) ** 0.25
DN_BETA = (8 * DEPTH) ** -0.25


def _layer_norm(x, g, b):
    xf = x.astype(jnp.float32)
    mu = jnp.mean(xf, -1, keepdims=True)
    var = jnp.mean(jnp.square(xf - mu), -1, keepdims=True)
    return ((xf - mu) * lax.rsqrt(var + LN_EPS)).astype(x.dtype) * g + b

def _rms_norm(x, g):
    xf = x.astype(jnp.float32)
    return (xf * lax.rsqrt(jnp.mean(xf * xf, -1, keepdims=True) + LN_EPS)).astype(x.dtype) * g

def _rel_bucket(dist):
    n = jnp.maximum(dist, 0)
    max_exact = REL_BUCKETS // 2
    nf = jnp.maximum(n, 1).astype(jnp.float32)
    large = max_exact + (jnp.log(nf / max_exact) / math.log(REL_MAX_DIST / max_exact)
                         * (REL_BUCKETS - max_exact)).astype(jnp.int32)
    large = jnp.minimum(large, REL_BUCKETS - 1)
    return jnp.where(n < max_exact, n, large)

def _to_blocks(a):
    B, S = a.shape[:2]
    return jnp.moveaxis(a.reshape(B, S // Q_BLOCK, Q_BLOCK, *a.shape[2:]), 1, 0)

def _from_blocks(a):
    nb, B, Q = a.shape[:3]
    return jnp.moveaxis(a, 0, 1).reshape(B, nb * Q, *a.shape[3:])

def _dsa_mixer(h, w_in, kv_norm, w_uk, w_uv, w_o, rel_bias):
    B, S, _ = h.shape
    topk = min(TOPK_MAX, S // 4)
    proj = h @ w_in
    q, ckv, iq, ik, iw = jnp.split(proj, A_SPLITS, axis=-1)
    q = q.reshape(B, S, A_HEADS, A_QK_DIM)
    ckv = _rms_norm(ckv, kv_norm)
    iq = iq.reshape(B, S, IDX_HEADS, IDX_DIM)
    iw = iw * (IDX_HEADS ** -0.5 * IDX_DIM ** -0.5)
    pos = jnp.arange(S, dtype=jnp.int32)

    def block(args):
        qb, iqb, iwb, tpos = args
        idx_logits = jnp.einsum('bqhd,bsd->bhqs', iqb, ik).astype(jnp.float32)
        score = jnp.einsum('bhqs,bqh->bqs', jax.nn.relu(idx_logits), iwb.astype(jnp.float32))
        causal = pos[None, :] <= tpos[:, None]
        score = jnp.where(causal[None], score, -jnp.inf)
        _, sel = lax.top_k(score, topk)
        valid = sel <= tpos[None, :, None]
        kv_sel = jax.vmap(lambda cb, ib: cb[ib])(ckv, sel)
        q_lat = jnp.einsum('bqhd,hdr->bqhr', qb, w_uk) * (A_QK_DIM ** -0.5)
        logits = jnp.einsum('bqhr,bqkr->bhqk', q_lat, kv_sel).astype(jnp.float32)
        bias = rel_bias[_rel_bucket(tpos[None, :, None] - sel)]
        logits = logits + jnp.transpose(bias, (0, 3, 1, 2))
        logits = jnp.where(valid[:, None], logits, NEG)
        p = jax.nn.softmax(logits, axis=-1).astype(h.dtype)
        o_lat = jnp.einsum('bhqk,bqkr->bqhr', p, kv_sel)
        return jnp.einsum('bqhr,hrd->bqhd', o_lat, w_uv)

    o = lax.map(block, (_to_blocks(q), _to_blocks(iq), _to_blocks(iw),
                        pos.reshape(S // Q_BLOCK, Q_BLOCK)))
    o = _from_blocks(o)
    return o.reshape(B, S, A_HEADS * A_V_DIM) @ w_o

def _diff_mixer(h, w_in, lam, subln_g, w_o, rel_bias, layer_idx):
    B, S, _ = h.shape
    lam_init = 0.8 - 0.6 * math.exp(-0.3 * layer_idx)
    proj = h @ w_in
    q, k, v = jnp.split(proj, 3, axis=-1)
    q = q.reshape(B, S, B_HEADS, 2, B_HEAD_DIM) * (B_HEAD_DIM ** -0.5)
    k = k.reshape(B, S, B_HEADS, 2, B_HEAD_DIM)
    v = v.reshape(B, S, B_HEADS, 2 * B_HEAD_DIM)
    lam_f = lam.astype(jnp.float32)
    lam_full = (jnp.exp(jnp.sum(lam_f[0] * lam_f[1])) - jnp.exp(jnp.sum(lam_f[2] * lam_f[3]))
                + lam_init)
    pos = jnp.arange(S, dtype=jnp.int32)

    def block(args):
        qb, tpos = args
        logits = jnp.einsum('bqhmd,bshmd->bhmqs', qb, k).astype(jnp.float32)
        bias = rel_bias[_rel_bucket(tpos[:, None] - pos[None, :])]
        bias = jnp.transpose(bias.reshape(Q_BLOCK, S, B_HEADS, 2), (2, 3, 0, 1))
        causal = pos[None, :] <= tpos[:, None]
        logits = jnp.where(causal, logits + bias, NEG)
        p = jax.nn.softmax(logits, axis=-1)
        a = p[:, :, 0] - lam_full * p[:, :, 1]
        return jnp.einsum('bhqs,bshe->bqhe', a.astype(h.dtype), v)

    o = _from_blocks(lax.map(block, (_to_blocks(q), pos.reshape(S // Q_BLOCK, Q_BLOCK))))
    o = _rms_norm(o, subln_g) * (1.0 - lam_init)
    return o.reshape(B, S, B_HEADS * 2 * B_HEAD_DIM) @ w_o

def _sqrelu_mlp(h, w1, w2):
    return jnp.square(jax.nn.relu(h @ w1)) @ w2

def second_inputs(seed: int = 0) -> dict:
    key = jax.random.key(seed)
    ks = jax.random.split(key, 20)
    nrm = lambda k, shape, s: jax.random.normal(k, shape, jnp.float32) * s
    D = D_MODEL
    b_w_in = nrm(ks[10], (N_B, D, B_IN), D ** -0.5)
    b_w_in = b_w_in.at[..., 2 * B_QK:].multiply(DN_BETA)
    return {
        'x': nrm(ks[0], (BATCH, SEQ, D), 1.0),
        'c': nrm(ks[1], (BATCH, D), 1.0),
        'rel_bias': nrm(ks[2], (REL_BUCKETS, BIAS_HEADS), 0.5),
        'ada_w': nrm(ks[3], (DEPTH, D, 6 * D), 0.1 * D ** -0.5),
        'ada_b': nrm(ks[4], (DEPTH, 6 * D), 0.01),
        'ln_g': 1.0 + nrm(ks[5], (DEPTH, 2, D), 0.02),
        'ln_b': nrm(ks[6], (DEPTH, 2, D), 0.02),
        'a_w_in': nrm(ks[7], (N_A, D, A_IN), D ** -0.5),
        'a_kv_norm': 1.0 + nrm(ks[8], (N_A, A_KV_RANK), 0.02),
        'a_w_uk': nrm(ks[9], (N_A, A_HEADS, A_QK_DIM, A_KV_RANK), A_KV_RANK ** -0.5),
        'a_w_uv': nrm(ks[11], (N_A, A_HEADS, A_KV_RANK, A_V_DIM), DN_BETA * A_KV_RANK ** -0.5),
        'a_w_o': nrm(ks[12], (N_A, A_HEADS * A_V_DIM, D), DN_BETA * (A_HEADS * A_V_DIM) ** -0.5),
        'b_w_in': b_w_in,
        'b_lambda': nrm(ks[13], (N_B, 4, B_HEAD_DIM), 0.1),
        'b_subln': 1.0 + nrm(ks[14], (N_B, 2 * B_HEAD_DIM), 0.02),
        'b_w_o': nrm(ks[15], (N_B, B_QK, D), DN_BETA * B_QK ** -0.5),
        'mlp_w1': nrm(ks[16], (DEPTH, D, D_FF), D ** -0.5),
        'mlp_w2': nrm(ks[17], (DEPTH, D_FF, D), DN_BETA * D_FF ** -0.5),
    }

def second_block(x, c, rel_bias, ada_w, ada_b, ln_g, ln_b,
              a_w_in, a_kv_norm, a_w_uk, a_w_uv, a_w_o,
              b_w_in, b_lambda, b_subln, b_w_o,
              mlp_w1, mlp_w2):
    mod = jnp.einsum('bd,lde->lbe', jax.nn.silu(c), ada_w) + ada_b[:, None]
    for i in range(DEPTH):
        sh_t, sc_t, g_t, sh_c, sc_c, g_c = [m[:, None] for m in jnp.split(mod[i], 6, axis=-1)]
        h = x * (1.0 + sc_t) + sh_t
        j = i // N_MIXERS
        if i % N_MIXERS == 0:
            y = _dsa_mixer(h, a_w_in[j], a_kv_norm[j], a_w_uk[j], a_w_uv[j], a_w_o[j], rel_bias)
        else:
            y = _diff_mixer(h, b_w_in[j], b_lambda[j], b_subln[j], b_w_o[j], rel_bias, i)
        x = _layer_norm(DN_ALPHA * x + (1.0 + g_t) * y, ln_g[i, 0], ln_b[i, 0])
        h = x * (1.0 + sc_c) + sh_c
        y = _sqrelu_mlp(h, mlp_w1[i], mlp_w2[i])
        x = _layer_norm(DN_ALPHA * x + (1.0 + g_c) * y, ln_g[i, 1], ln_b[i, 1])
    return x


def setup_inputs(seed=0):
    out = dict(first_inputs(seed))
    for name, value in second_inputs(seed + 1).items():
        if name != "x":
            out[name + "_2"] = value
    return out


def reference(
    x, positions, norm_w, w_in, attn_sinks, hgrn_norm_w, w_up_attn, w_up_hgrn, w_out, lb_logits,
    final_norm_w, c_2, rel_bias_2, ada_w_2, ada_b_2, ln_g_2, ln_b_2, a_w_in_2, a_kv_norm_2,
    a_w_uk_2, a_w_uv_2, a_w_o_2, b_w_in_2, b_lambda_2, b_subln_2, b_w_o_2, mlp_w1_2, mlp_w2_2,
):
    x = first_block(
        x, positions, norm_w, w_in, attn_sinks, hgrn_norm_w, w_up_attn, w_up_hgrn, w_out,
        lb_logits, final_norm_w,
    )
    return second_block(
        x, c_2, rel_bias_2, ada_w_2, ada_b_2, ln_g_2, ln_b_2, a_w_in_2, a_kv_norm_2, a_w_uk_2,
        a_w_uv_2, a_w_o_2, b_w_in_2, b_lambda_2, b_subln_2, b_w_o_2, mlp_w1_2, mlp_w2_2,
    )


_drawn_inputs = setup_inputs


def setup_inputs(seed=0):
    import zlib

    import numpy as np

    out = dict(_drawn_inputs(seed))
    spreads = {}
    factors = {'norm_w': 3.656,
     'attn_sinks': 8.0,
     'hgrn_norm_w': 5.477,
     'lb_logits': 8.0,
     'ada_b_2': 3.616,
     'a_kv_norm_2': 8.0,
     'b_subln_2': 8.0}
    for name, (base, spread) in spreads.items():
        noise = np.random.default_rng([zlib.crc32(name.encode()), seed]).standard_normal(out[name].shape)
        drawn = base * np.exp(spread * noise) if base else spread * noise
        out[name] = __import__('jax').numpy.asarray(drawn.astype(out[name].dtype))
    for name, factor in factors.items():
        out[name] = (out[name] * factor).astype(out[name].dtype)
    return out
```

```python
from contextlib import ExitStack

import numpy as np

import concourse.bass as bass
from concourse import mybir

ALU = mybir.AluOpType
ACT = mybir.ActivationFunctionType
AX = mybir.AxisListType
F32 = mybir.dt.float32
I32 = mybir.dt.int32

P = 128
T = 256
NT = T // P
D = 1024
KT = D // P
HD = 64
HALF = 512
EPS = 1e-6
LN_EPS = 1e-5
NEG = -1e30
LOWEST = -3e38
TOPK = 64
ALPHA = 4 ** 0.25
LAM_INIT = 0.8 - 0.6 * float(np.exp(-0.3))
RING = 6
NBUCKET = 32
DIST = 3 * P - 1
ROPE_HALF = 8
QUAD = 4
LEVELS = 8
CHUNK = 64
TURN = float(2 * np.pi)
TURN_PARTS = [6.28125, 0.0019350051879882812, 3.0199159819567e-07]
ROUNDER = 1.5 * 2.0 ** 23
SIN_MAX = 3.1415925
Q0, K0, V0, Z0, QH0, F0, I0, G0, GA0, GH0 = 0, 512, 640, 768, 1280, 1792, 2304, 2816, 3328, 4352


def bucket_onehot():
    edges = list(range(16)) + [int(np.ceil(16 * 8 ** (k / 16) - 1e-9)) for k in range(16)] + [T]
    table = np.zeros((NBUCKET + 1, DIST), np.float32)
    for b in range(NBUCKET):
        table[b, edges[b] + P - 1:edges[b + 1] + P - 1] = 1.0
    table[0, :P - 1] = 1.0
    table[NBUCKET, :P - 1] = NEG
    return table


def build_program(nc, I, out):
    with ExitStack() as ctx:
        def sb(name, shape, dt=F32):
            return ctx.enter_context(nc.sbuf_tensor(name, shape, dt))

        sems = {}

        def S(name):
            if name not in sems:
                sems[name] = ctx.enter_context(nc.semaphore(name))
            return sems[name]

        lin_ps = ctx.enter_context(nc.psum_tensor("lin_ps", [P, 4, HALF], F32))
        tmp_ps = ctx.enter_context(nc.psum_tensor("tmp_ps", [P, 4, HALF], F32))

        ring = sb("ring", [P, RING, 4, HALF])
        x = sb("x", [P, NT, D])
        hT = sb("hT", [P, KT, T])
        ident = sb("ident", [P, P])
        ones = sb("ones", [P, P])
        band = sb("band", [P, T])
        levelmask = sb("levelmask", [P, LEVELS, P])
        chunkmask = sb("chunkmask", [P, 4 * T])
        pairx = sb("pairx", [P, 2, P], I32)
        stackA = sb("stackA", [P, P])
        stackB = sb("stackB", [5, P])
        colA = sb("colA", [P, P])
        colB = sb("colB", [P, 5])
        sinks = sb("sinks", [P, 16])
        lamb = sb("lamb", [P, 4, HD])
        posi = sb("posi", [P, NT], I32)
        posf = sb("posf", [P, NT])
        invf = sb("invf", [P, ROPE_HALF])
        ang = sb("ang", [P, NT, 2, ROPE_HALF])
        angk = sb("angk", [P, NT, 2, ROPE_HALF])
        trig = sb("trig", [P, NT, 2, ROPE_HALF])
        lbw = sb("lbw", [P, 6, 4])
        lams = sb("lams", [P, 8])
        csil = sb("csil", [P, KT])
        csb = sb("csb", [P, KT, P])
        modc = sb("modc", [P, 2, 4, KT])
        gmod = sb("gmod", [P, 4, D])
        relT = sb("relT", [NBUCKET + 1, 16])
        onehot = sb("onehot", [NBUCKET + 1, DIST])
        relvec = sb("relvec", [16, DIST])
        lnp = sb("lnp", [P, 2, D])
        st = sb("st", [P, 3, 2, 8])
        bns = sb("bns", [P, NT, 2, 6])
        mv = sb("mv", [P, NT, 2])
        qst = sb("qst", [P, 8, 6, QUAD])
        rden = sb("rden", [P, NT, 16])
        ropet = sb("ropet", [P, 4, 10, ROPE_HALF])
        hs = sb("hs", [P, NT, D])
        iw = sb("iw", [P, NT, 8])
        top8 = sb("top8", [P, 8])
        arena = sb("arena", [P, 20 * 1024])
        scratch = nc.dram_tensor("relvec_dram", (16, DIST), F32).ap()

        def at(k, *shape):
            n = int(np.prod(shape))
            v = arena[:, int(k * 1024):int(k * 1024) + n]
            names = " ".join(f"d{j}" for j in range(len(shape)))
            return v if len(shape) == 1 else v.rearrange(
                f"p ({names}) -> p {names}", **{f"d{j}": s for j, s in enumerate(shape)})

        qkv = at(0, NT, 768)
        zs = at(1.5, NT, HALF)
        ga = at(2.5, NT, D)
        gh = at(4.5, NT, D)
        vh = at(6.5, NT, HALF)
        zg = at(7.5, NT, HALF)
        qin = at(8.5, 4, T)
        kin = at(9.5, 4, T)
        G = at(10.5, 4, T)
        decay = [at(11.5, 4, T), at(12.5, 4, T)]
        scor = at(13.5, 8, P)
        cross = at(14.5, 4, P)
        kdup = at(15, NT, 2, 2, HD)
        Pq = [at(15.5, QUAD, T), at(16.5, QUAD, T)]
        pT = [at(17.5, QUAD * T), at(18.5, QUAD * T)]
        kTd = at(19.5, 2, T)
        levelge = at(0, LEVELS + 1, P)
        qTa, aT, bT = qin, kin, G
        gate_min, gate_max, gate_p, gate_n, gate_lnsum = decay[0], decay[1], at(13.5, 4, T), kin, G
        qT = at(0, KT, T)
        kT = at(2, KT, T)
        vv = at(4, NT, D)
        iqT = at(6, 4, T)
        ikT = at(7, T)
        ckv = at(7.25, NT, T)
        ckvT = at(7.75, 2, T)
        wukT = at(8.25, 2, D)
        isc = at(10.25, NT, T)
        iwk = at(10.75, NT, T)
        Mbias = at(11.25, 16, T)
        hb = [at(6, QUAD, T), at(7, QUAD, T)]
        osq = at(6, NT, D)

        done = {}
        turn_tmp, turn_lin = {}, {}
        units = []
        count = {}

        def bump(name, n=1):
            count[name] = count.get(name, 0) + n
            return count[name]

        def read_of(name):
            which, n = ("tmp", turn_tmp[name]) if name in turn_tmp else ("lin", turn_lin[name])
            return S(f"{which}_read{n % 2}"), n // 2 + 1

        def win(w, c0, n, k0=0):
            return w[k0 * P:(k0 + 4) * P, c0:c0 + n].rearrange("(k p) n -> p k n", p=P)

        block = ctx.enter_context(nc.Block())

        @block.tensor
        def _(pe):
            pending = [0]

            def take(*parts):
                n = len(units)
                s = n % RING
                landed = 16 * len(parts) + (units[n - RING]["landed"] if n >= RING else 0)
                pending[0] += 1
                units.append({"parts": parts, "landed": landed})
                pe.wait_ge(S(f"w_landed{s}"), landed)
                return ring[:, s]

            def used(ins):
                n, pending[0] = pending[0], 0
                ins.then_inc(S("w_used"), n)
                return S("w_used"), bump("w_used", n)

            def wait_read(*names):
                for name in names:
                    pe.wait_ge(*read_of(name))

            def open_tmp(name):
                n = len(turn_tmp)
                turn_tmp[name] = n
                if n >= 2:
                    pe.wait_ge(S(f"tmp_read{n % 2}"), n // 2)
                return tmp_ps[:, 2 * (n % 2):2 * (n % 2) + 2, :]

            def close_tmp(ins, name):
                ins.then_inc(S("tmp_full"), 1)
                done[name] = (S("tmp_full"), bump("tmp_full"))

            def open_lin(name):
                n = len(turn_lin)
                turn_lin[name] = n
                if n >= 2:
                    pe.wait_ge(S(f"lin_read{n % 2}"), n // 2)
                return lin_ps[:, 2 * (n % 2):2 * (n % 2) + 2, :]

            def linear_tok(name, w, c0, n, src, kts=KT, first=True):
                ps = open_lin(name)
                for k0 in range(0, kts, 4):
                    slot = take((slice(0, n), win(w, c0, n, k0)))
                    for k in range(4):
                        for i in range(NT):
                            mm = pe.matmul(ps[:, i, 0:n], src[:, k0 + k, i * P:(i + 1) * P], slot[:, k, 0:n],
                                           start=(k0 + k == 0), stop=(k0 + k == kts - 1))
                    done[name] = used(mm)

            def feat_unit(ps, slot, k0, src, cols=4):
                for k in range(4):
                    for c in range(cols):
                        mm = pe.matmul(ps[:, c // 2, (c % 2) * T:(c % 2) * T + T], slot[:, k, c * P:(c + 1) * P],
                                       src[:, k0 + k, :], start=(k0 + k == 0 and c % 2 == 0),
                                       stop=(k0 + k == KT - 1), skip_group_check=True)
                return mm

            def linear_feat(name, w, c0, src):
                ps = open_lin(name)
                for k0 in (0, 4):
                    slot = take((slice(0, HALF), win(w, c0, HALF, k0)))
                    done[name] = used(feat_unit(ps, slot, k0, src))

            def transposes(name, pieces):
                ps = open_tmp(name).rearrange("p a b -> p (a b)")
                for n, piece in enumerate(pieces):
                    mm = pe.transpose(ps[:, n * P:(n + 1) * P], piece, ident[:])
                close_tmp(mm, name)

            def feature_major(name, src, kts=KT):
                for h in range(kts // 4):
                    transposes(f"{name}{h}", [src[:, i, k * P:(k + 1) * P]
                                              for k in range(4 * h, 4 * h + 4) for i in range(NT)])

            def ada(layer, n):
                name = f"ada{layer}_{n}"
                ps = open_lin(name)
                w = I["ada_w_2"][layer]
                if n // 2 in (2, 5):
                    for k0 in (0, 4):
                        slot = take((slice(0, HALF), win(w, n * HALF, HALF, k0)))
                        for k in range(4):
                            mm = pe.matmul(ps[:, 0, :], csb[:, k0 + k, :], slot[:, k, :],
                                           start=(k0 + k == 0), stop=(k0 + k == KT - 1))
                        done[name] = used(mm)
                    return
                slots = [take((slice(0, HALF), win(w, n * HALF, HALF, k0))) for k0 in (0, 4)]
                for c in range(4):
                    for k in range(KT):
                        mm = pe.matmul(ps[:, 0, c:c + 1], slots[k // 4][:, k % 4, c * P:(c + 1) * P],
                                       csil[:, k:k + 1], start=(k == 0), stop=(k == KT - 1))
                done[name] = used(mm)

            def attention(name, quads, q, k, v, vw, per, ocols):
                def scores(n):
                    i, g = quads[n]
                    W = P * (i + 1)
                    ps = open_tmp(f"{name}s{n}")
                    for j in range(2):
                        for a in range(2):
                            mm = pe.matmul(ps[:, a, j * W:(j + 1) * W], q(g, j, a)[:, i * P:(i + 1) * P],
                                           k(g, j, a)[:, 0:W], start=True, stop=True)
                    close_tmp(mm, f"{name}s{n}")

                def turned(n):
                    i, g = quads[n]
                    pe.wait_ge(S(f"{name}prob"), n + 1)
                    transposes(f"{name}p{n}", [Pq[n % 2][:, s, b * P:(b + 1) * P]
                                               for s in range(per) for b in range(i + 1)])

                def product(n):
                    i, g = quads[n]
                    wait_read(f"{name}p{n}")
                    if g == 0 and (i == 0 or ocols == D):
                        product.ps = open_lin(f"{name}o{i}")
                    ps = product.ps
                    for s in range(per):
                        head = g * per + (2 * (s % 2) + s // 2 if per == QUAD else s)
                        o = ps[:, i, head * vw:(head + 1) * vw] if ocols == HALF else \
                            ps.rearrange("p a b -> p (a b)")[:, head * vw:(head + 1) * vw]
                        for b in range(i + 1):
                            blk = s * (i + 1) + b
                            mm = pe.matmul(o, pT[n % 2][:, blk * P:(blk + 1) * P], v(b, head),
                                           start=(b == 0), stop=(b == i))
                    mm.then_inc(S("att_pv"), 1)
                    done[f"{name}o{i}"] = done[f"{name}pv{n}"] = (S("att_pv"), bump("att_pv"))

                for n in range(len(quads) + 2):
                    if n < len(quads):
                        scores(n)
                    if 1 <= n <= len(quads):
                        turned(n - 1)
                    if n >= 2:
                        product(n - 2)

            pe.wait_ge(S("ident"), 1)
            pe.wait_ge(S("small_landed"), 16 * 8)
            ps = open_tmp("cols")
            pe.transpose(ps[:, 0, 0:P], stackA[:], ident[:])
            close_tmp(pe.transpose(ps[:, 0, P:P + 5], stackB[:], ident[0:5, 0:5]), "cols")
            ps = open_tmp("relvec")
            pe.wait_ge(S("rel_landed"), 32)
            close_tmp(pe.matmul(ps[0:16, 0, 0:DIST], relT[:], onehot[:], start=True, stop=True), "relvec")

            holes = [(layer, n) for layer in range(2) for n in range(12)]

            def fill(n):
                if len(holes) == 24 and n:
                    pe.wait_ge(S("cond_ready"), 1)
                for _ in range(n):
                    if holes:
                        ada(*holes.pop(0))

            quads_a = [(i, g) for i in range(NT) for g in range(2)]
            for L in range(2):
                w = I["w_in"][L]
                fill(1)
                pe.wait_ge(S("f_scaled"), L + 1)
                feature_major(f"f{L}hT", hs)
                wait_read(f"f{L}hT0", f"f{L}hT1")
                linear_feat(f"f{L}f", w, F0, hT)
                linear_feat(f"f{L}qh", w, QH0, hT)
                linear_tok(f"f{L}kv", w, K0, 256, hT)
                linear_tok(f"f{L}q", w, Q0, HALF, hT)
                linear_tok(f"f{L}i", w, I0, HALF, hT)
                pe.wait_ge(S("f_rope"), L + 1)
                transposes(f"f{L}kT", [kdup[:, i, g].rearrange("p a d -> p (a d)") for g in range(2) for i in range(NT)])
                linear_tok(f"f{L}z", w, Z0, HALF, hT)
                linear_tok(f"f{L}g", w, G0, HALF, hT)
                for lv in range(LEVELS + 1):
                    name = f"f{L}lv{lv}"
                    ps = open_tmp(name).rearrange("p a b -> p (a b)")
                    pe.wait_ge(S("level_ready"), (LEVELS + 1) * L + lv + 1)
                    left, right = (kin, qin) if lv == 0 else (decay[lv % 2], decay[lv % 2])
                    for n in range(4 if lv == LEVELS else 8):
                        if lv == LEVELS:
                            a, b = left[:, n, 0:P], right[:, n, P:T]
                        else:
                            cut = slice((n % 2) * P, (n % 2) * P + P)
                            a, b = left[:, n // 2, cut], right[:, n // 2, cut]
                        mm = pe.matmul(ps[:, n * P:(n + 1) * P], a, b, start=True, stop=True)
                    close_tmp(mm, name)
                    if lv in (2, 4, 6, 7):
                        c = {2: (GA0, "ga0"), 4: (GA0 + HALF, "ga1"), 6: (GH0, "gh0"), 7: (GH0 + HALF, "gh1")}[lv]
                        linear_tok(f"f{L}{c[1]}", w, c[0], HALF, hT)
                transposes(f"f{L}qT", [qkv[:, i, k * P:(k + 1) * P] for k in range(4) for i in range(NT)])
                ps = open_lin(f"f{L}ho")
                wait_read(f"f{L}lv{LEVELS - 1}", f"f{L}lv{LEVELS}")
                for h in range(4):
                    cols = slice(h * P, (h + 1) * P)
                    pe.matmul(ps[:, 0, cols], scor[:, 2 * h, :], vh[:, 0, cols], start=True, stop=True)
                    pe.matmul(ps[:, 1, cols], cross[:, h, :], vh[:, 0, cols], start=True, stop=False)
                    mm = pe.matmul(ps[:, 1, cols], scor[:, 2 * h + 1, :], vh[:, 1, cols], start=False, stop=True)
                mm.then_inc(S("hgrn_out"), 1)
                done[f"f{L}ho"] = (S("hgrn_out"), bump("hgrn_out"))
                wait_read(f"f{L}kT", f"f{L}qT")
                attention(f"f{L}a", quads_a,
                          lambda g, j, a: qTa[a * HD:(a + 1) * HD, 2 * g + j, :],
                          lambda g, j, a: kTd[a * HD:(a + 1) * HD, g, :],
                          lambda b, head: qkv[:, b, 640 + (head // 4) * HD:640 + (head // 4 + 1) * HD],
                          HD, QUAD, HALF)
                fill(3)
                pe.wait_ge(S("f_b"), L + 1)
                feature_major(f"f{L}bT", hs[:, :, HALF:D], 4)
                pe.wait_ge(S("f_a"), L + 1)
                feature_major(f"f{L}aT", hs[:, :, 0:HALF], 4)
                wait_read(f"f{L}bT0", f"f{L}aT0")
                for c in range(2):
                    linear_tok(f"f{L}ua{c}", I["w_up_attn"][L], c * HALF, HALF, aT, kts=4)
                    linear_tok(f"f{L}uh{c}", I["w_up_hgrn"][L], c * HALF, HALF, bT, kts=4)
                fill(2)
                pe.wait_ge(S("f_merged"), L + 1)
                feature_major(f"f{L}mT", hs)
                wait_read(f"f{L}mT0", f"f{L}mT1")
                for c in range(2):
                    linear_tok(f"f{L}out{c}", I["w_out"][L], c * HALF, HALF, hT)
            fill(len(holes))

            def mixed(name):
                pe.wait_ge(S(f"{name}x"), 1)
                feature_major(f"{name}hT", x)
                wait_read(f"{name}hT0", f"{name}hT1")

            def project(name, w):
                feature_major(f"{name}oT", hs)
                wait_read(f"{name}oT0", f"{name}oT1")
                for c in range(2):
                    linear_tok(f"{name}y{c}", w, c * HALF, HALF, hT)

            def mlp(name, w1, w2):
                mixed(name)
                groups = 8
                ys = None
                for g in range(groups + 1):
                    if g < groups:
                        ps = open_tmp(f"{name}u{g}")
                        for k0 in (0, 4):
                            slot = take((slice(0, HALF), win(w1, g * HALF, HALF, k0)))
                            mm = feat_unit(ps, slot, k0, hT)
                            if k0 == 0:
                                used(mm)
                        close_tmp(mm, f"{name}u{g}")
                    if g == 1:
                        ys = [open_lin(f"{name}y{c}") for c in range(2)]
                    if g >= 1:
                        pe.wait_ge(S(f"{name}act"), g)
                        for c in range(2):
                            slot = take((slice(0, HALF), win(w2, c * HALF, HALF, 4 * (g - 1))))
                            for k in range(4):
                                for i in range(NT):
                                    mm = pe.matmul(ys[c][:, i, :], hb[(g - 1) % 2][:, k, i * P:(i + 1) * P],
                                                   slot[:, k, :], start=(g == 1 and k == 0),
                                                   stop=(g == groups and k == 3), skip_group_check=True)
                            done[f"{name}y{c}"] = used(mm)
                            if c == 1:
                                done[f"{name}hb{g - 1}"] = done[f"{name}y{c}"]

            quads_16 = [(i, g) for i in range(NT) for g in range(4)]

            w = I["a_w_in_2"][0]
            mixed("s0")
            ps = open_lin("s0misc")
            psk = open_tmp("s0ik")
            for k0 in (0, 4):
                slot = take((slice(0, T), win(w, 1024, T, k0)), (slice(T, T + 8), win(w, 1856, 8, k0)),
                            (slice(384, 448), win(w, 1792, HD, k0)), (slice(448, 512), win(w, 1792, HD, k0)))
                for k in range(4):
                    for i in range(NT):
                        pe.matmul(ps[:, i, 0:T + 8], hT[:, k0 + k, i * P:(i + 1) * P], slot[:, k, 0:T + 8],
                                  start=(k0 + k == 0), stop=(k0 + k == KT - 1))
                    mm = pe.matmul(psk[:, 0, 0:T], slot[:, k, 384:512], hT[:, k0 + k, :],
                                   start=(k0 + k == 0), stop=(k0 + k == KT - 1))
                done["s0misc"] = done["s0ik"] = used(mm)
            linear_feat("s0iq", w, 1280, hT)
            wait_read("s0ik", "s0iq")
            for i in range(NT):
                for g in range(2):
                    W = P * (i + 1)
                    ps = open_tmp(f"s0idx{i}{g}")
                    for j in range(2):
                        for a in range(2):
                            rows = slice(a * HD, (a + 1) * HD)
                            mm = pe.matmul(ps[:, a, j * W:(j + 1) * W], iqT[rows, 2 * g + j, i * P:(i + 1) * P],
                                           ikT[rows, 0:W], start=True, stop=True)
                    close_tmp(mm, f"s0idx{i}{g}")
                if i == 0:
                    linear_feat("s0q0", w, 0, hT)
            linear_feat("s0q1", w, HALF, hT)
            pe.wait_ge(S("s0ckvn"), 1)
            transposes("s0ckvT", [ckv[:, i, r * P:(r + 1) * P] for r in range(2) for i in range(NT)])
            slot = take((slice(0, HALF), I["a_w_uk_2"][0].rearrange("h d r -> (h d) r").rearrange(
                "(k p) r -> p k r", p=P)))
            uk = slot.rearrange("p a b -> p (a b)").rearrange("p (k r) -> p k r", k=KT)
            for r in range(2):
                ps = open_tmp(f"s0wuk{r}").rearrange("p a b -> p (a b)")
                for k in range(KT):
                    mm = pe.transpose(ps[:, k * P:(k + 1) * P], uk[:, k, r * P:(r + 1) * P], ident[:])
                close_tmp(mm, f"s0wuk{r}")
            wait_read("s0ckvT")
            slot = take((0, "wuv"), (1, "wuv"))
            uv = slot.rearrange("p a b -> p (a b)").rearrange("p (r n) -> p r n", r=2)
            for i in range(NT):
                ps = open_lin(f"s0v{i}")
                for c in range(2):
                    for r in range(2):
                        mm = pe.matmul(ps[:, c, :], ckvT[:, r, i * P:(i + 1) * P], uv[:, r, c * HALF:(c + 1) * HALF],
                                       start=(r == 0), stop=(r == 1))
                if i == 0:
                    mm.then_inc(S("s0v0_full"), 1)
                    done["s0v0"] = (S("s0v0_full"), 1)
                else:
                    done["s0v1"] = used(mm)
            wait_read("s0wuk0", "s0wuk1")
            for h in range(2):
                ps = open_tmp(f"s0k{h}")
                for c in range(4):
                    for r in range(2):
                        mm = pe.matmul(ps[:, c // 2, (c % 2) * T:(c % 2) * T + T],
                                       wukT[:, r, (4 * h + c) * P:(4 * h + c + 1) * P], ckvT[:, r, :],
                                       start=(r == 0), stop=(r == 1))
                close_tmp(mm, f"s0k{h}")
            wait_read("s0q0", "s0q1", "s0k0", "s0k1", "s0v0", "s0v1")
            heads = (lambda t: lambda g, j, a: t[a * HD:(a + 1) * HD, 2 * g + j, :])
            attention("s0", quads_16, heads(qT), heads(kT),
                      lambda b, head: vv[:, b, head * HD:(head + 1) * HD], HD, QUAD, D)
            wait_read("s0o0", "s0o1")
            project("s0", I["a_w_o_2"][0])
            mlp("s1", I["mlp_w1_2"][0], I["mlp_w2_2"][0])

            w = I["b_w_in_2"][0]
            mixed("s2")
            for n in range(2):
                linear_feat(f"s2q{n}", w, n * HALF, hT)
                linear_feat(f"s2k{n}", w, D + n * HALF, hT)
            for n in range(2):
                linear_tok(f"s2v{n}", w, 2 * D + n * HALF, HALF, hT)
            wait_read(*(f"s2{part}{n}" for part in "qkv" for n in range(2)))
            attention("s2", quads_16, heads(qT), heads(kT),
                      lambda b, head: vv[:, b, head * P:(head + 1) * P], P, 2, D)
            pe.wait_ge(S("s2o"), 1)
            project("s2", I["b_w_o_2"][0])
            mlp("s3", I["mlp_w1_2"][1], I["mlp_w2_2"][1])

        def full_tmp(eng, name):
            eng.wait_ge(*done[name])
            n = turn_tmp[name]
            return tmp_ps[:, 2 * (n % 2):2 * (n % 2) + 2, :]

        def full_lin(eng, name):
            eng.wait_ge(*done[name])
            n = turn_lin[name]
            return lin_ps[:, 2 * (n % 2):2 * (n % 2) + 2, :]

        def read(ins, name):
            ins.then_inc(read_of(name)[0], 1)

        def flat(v):
            return v.rearrange("p a b -> p (a b)")

        @block.sync
        def _(sp):
            released = 0
            for n, unit in enumerate(units):
                if n >= RING:
                    sp.wait_ge(S("w_used"), n - RING + 1)
                slot = ring[:, n % RING]
                for cols, src in unit["parts"]:
                    if isinstance(src, str):
                        r = cols
                        dst = slot.rearrange("p a b -> p (a b)")[:, r * D:(r + 1) * D].rearrange(
                            "p (h d) -> p h d", h=16)
                        sp.dma_start(dst, I["a_w_uv_2"][0, :, r * P:(r + 1) * P, :].rearrange(
                            "h p d -> p h d")).then_inc(S(f"w_landed{n % RING}"), 16)
                    elif src.shape[1] == KT:
                        sp.dma_start(slot.rearrange("p a b -> p (a b)").rearrange("p (k r) -> p k r", k=KT),
                                     src).then_inc(S(f"w_landed{n % RING}"), 16)
                    else:
                        sp.dma_start(slot[:, :, cols], src).then_inc(S(f"w_landed{n % RING}"), 16)
            sp.wait_ge(S("s4x"), 1)
            sp.dma_start(out.rearrange("b (i p) d -> p (b i) d", p=P), x[:]).then_inc(S("out_written"), 16)
            sp.wait_ge(S("out_written"), 16)

        @block.gpsimd
        def _(pool):
            def step(ins):
                ins.then_inc(S("pool_step"), 1)
                pool.wait_ge(S("pool_step"), bump("pool_step"))

            step(pool.memset(ident[:], 0.0))
            pool.affine_select(out=ident[:], in_=ident[:], compare_op=ALU.not_equal, fill=1.0, base=0,
                               pattern=[[-1, P]], channel_multiplier=1).then_inc(S("ident"), 1)
            pool.memset(ones[:], 1.0).then_inc(S("ones"), 1)
            step(pool.memset(band[:], 0.0))
            step(pool.affine_select(out=band[:, 0:P], in_=band[:, 0:P], compare_op=ALU.is_gt, fill=NEG, base=0,
                                    pattern=[[1, P]], channel_multiplier=-1))
            pool.affine_select(out=band[:, P:T], in_=band[:, P:T], compare_op=ALU.is_ge, fill=NEG, base=0,
                               pattern=[[-1, P]], channel_multiplier=1).then_inc(S("band"), 1)
            step(pool.iota(pairx[:, 0, :], pattern=[[0, P]], base=0, channel_multiplier=1))
            pool.iota(pairx[:, 1, :], pattern=[[1, P]], base=0, channel_multiplier=0).then_inc(S("pairs"), 1)
            step(pool.memset(chunkmask[:], 1.0))
            pool.memset(chunkmask[:].rearrange("p (c t) -> p c t", t=CHUNK)[:, :, 0:1], 0.0).then_inc(S("chunkmask"), 1)
            for j in range(ROPE_HALF):
                ins = pool.memset(invf[:, j:j + 1], float(np.float32(500000.0) ** np.float32(-j * 0.125)))
            ins.then_inc(S("invf"), 1)
            step(pool.memset(relT[:], 1.0))
            pool.dma_start(relT[0:NBUCKET, :], I["rel_bias_2"]).then_inc(S("rel_landed"), 16)
            pool.dma_start(onehot[:], I["onehot"]).then_inc(S("rel_landed"), 16)
            for n, (layer, section) in enumerate([(0, 2), (0, 5), (1, 2), (1, 5)]):
                pool.dma_start(gmod[:, n, :], I["ada_b_2"][layer, section * D:(section + 1) * D].partition_broadcast(P)
                               ).then_inc(S("gbias_landed"), 16)
            pool.dma_start(lnp[:, 0, :], I["final_norm_w"].partition_broadcast(P)).then_inc(S("lnp_landed"), 32)
            pool.wait_ge(S("levels_both"), 1)
            pool.affine_select(out=levelmask[:, 1:, :], in_=levelmask[:, 1:, :], compare_op=ALU.is_gt, fill=0.0,
                               base=0, pattern=[[0, LEVELS - 1], [1, P]], channel_multiplier=-1
                               ).then_inc(S("levels"), 1)
            pool.wait_ge(*read_of("relvec"))
            pool.dma_start(scratch, relvec[:]).then_inc(S("scratch_written"), 16)
            pool.wait_ge(S("scratch_written"), 16)
            pool.wait_ge(*read_of("f1out1"))
            pool.dma_start(Mbias[:], bass.AP(scratch.tensor, 0, [[1, P], [DIST, 16], [1, T]])
                           ).then_inc(S("Mbias"), 16)
            for n in range(4):
                pool.wait_ge(S(f"s{n}x"), 1)
                for j, v in enumerate((I["ln_g_2"], I["ln_b_2"])):
                    pool.dma_start(lnp[:, j, :], v[n // 2, n % 2].partition_broadcast(P)
                                   ).then_inc(S("lnp_landed"), 16)
                if n == 0:
                    pool.wait_ge(S("s0idx_used"), 4)
                    for i in range(NT):
                        v = isc[:, i, 0:P * (i + 1)]
                        ins = pool.affine_select(out=v, in_=v, compare_op=ALU.is_ge, fill=LOWEST, base=P * i,
                                                 pattern=[[-1, P * (i + 1)]], channel_multiplier=1)
                    ins.then_inc(S("s0causal"), 1)

        @block.scalar
        def _(act):
            def step(ins):
                ins.then_inc(S("act_step"), 1)
                act.wait_ge(S("act_step"), bump("act_step"))

            act.dma_start(x[:], I["x"].rearrange("b (i p) d -> p (b i) d", p=P)).then_inc(S("x_landed"), 16)
            rows = 0
            for v in (I["norm_w"].rearrange("l (k p) -> (l k) p", p=P),
                      I["lb_logits"].rearrange("l (k p) -> (l k) p", p=P),
                      I["ada_b_2"].rearrange("l (k p) -> (l k) p", p=P),
                      I["c_2"].rearrange("b (k p) -> (b k) p", p=P)):
                act.dma_start(stackA[rows:rows + v.shape[0], :], v).then_inc(S("small_landed"), 16)
                rows += v.shape[0]
            rows = 0
            for v in (I["a_kv_norm_2"].rearrange("l (k p) -> (l k) p", p=P), I["b_subln_2"], I["hgrn_norm_w"]):
                act.dma_start(stackB[rows:rows + v.shape[0], :], v).then_inc(S("small_landed"), 16)
                rows += v.shape[0]
            act.dma_start(posi[:], I["positions"].rearrange("b (i p) -> p (b i)", p=P),
                          allow_slow_non_contiguous=True).then_inc(S("small_landed"), 16)
            act.dma_start(sinks[:], I["attn_sinks"].rearrange("l h -> (l h)").partition_broadcast(P)
                          ).then_inc(S("sinks_landed"), 16)
            act.dma_start(lamb[:].rearrange("p a d -> p (a d)"),
                          I["b_lambda_2"].rearrange("l a d -> (l a d)").partition_broadcast(P)
                          ).then_inc(S("lamb_landed"), 16)

            def squares(name, ready):
                act.wait_ge(*ready)
                for i in range(NT):
                    ins = act.activation(hs[:, i, :], x[:, i, :], ACT.Square, accum_out=st[:, 0, i, 0:1])
                ins.then_inc(S(f"{name}ss"), 1)

            def rough_rsqrt(name, v, y):
                act.wait_ge(S(f"{name}var"), 1)
                step(act.activation(y, v, ACT.Ln))
                act.activation(y, y, ACT.Exp, scale=-0.5).then_inc(S(f"{name}rough"), 1)

            def exps(name, n, W):
                act.wait_ge(S(f"{name}max"), n + 1)
                for s in range(QUAD):
                    ins = act.activation(Pq[n % 2][:, s, 0:W], Pq[n % 2][:, s, 0:W], ACT.Exp,
                                         bias=qst[:, n, 1, s:s + 1], accum_out=qst[:, n, 2, s:s + 1])
                return ins

            def attention(name, quads, per, sink=False):
                for n in range(len(quads) + 1):
                    if n < len(quads):
                        ins = exps(name, n, P * (quads[n][0] + 1))
                        if sink:
                            ins = act.activation(qst[:, n, 3, :], qst[:, n, 4, :], ACT.Exp)
                        ins.then_inc(S(f"{name}exp"), 1)
                    if n >= 1:
                        m = n - 1
                        ps = full_tmp(act, f"{name}p{m}")
                        if m >= 2:
                            act.wait_ge(*done[f"{name}pv{m - 2}"])
                        w = per * (quads[m][0] + 1) * P
                        read(act.copy(pT[m % 2][:, 0:w], flat(ps)[:, 0:w]), f"{name}p{m}")

            act.wait_ge(*read_of("cols"))
            act.activation(csil[:], colA[:, 120:128], ACT.Silu).then_inc(S("csil"), 1)
            act.wait_ge(S("angles"), 1)
            act.activation(trig[:], ang[:], ACT.Sin).then_inc(S("trig"), 1)
            act.wait_ge(S("lb_max"), 1)
            act.activation(lbw[:, 0:2, :], lbw[:, 0:2, :], ACT.Exp).then_inc(S("lb_exp"), 1)
            act.wait_ge(S("lam_dots"), 1)
            act.activation(lams[:, 0:2], lams[:, 0:2], ACT.Exp).then_inc(S("lam_exp"), 1)

            for L in range(2):
                squares(f"f{L}", (S("x_landed"), 16) if L == 0 else read_of("f0out1"))
                rough_rsqrt(f"f{L}", st[:, 1, :, 0], st[:, 2, :, 0])
                act.wait_ge(*read_of(f"f{L}f"))
                act.activation(gate_p[:], gate_min[:], ACT.Exp)
                act.activation(gate_n[:], gate_max[:], ACT.Exp, scale=-1.0).then_inc(S("f_pn"), 1)
                act.wait_ge(S("f_sum"), L + 1)
                ins = act.activation(gate_lnsum[:], gate_lnsum[:], ACT.Ln)
                if L == 1:
                    ins = act.activation(gate_p[:], gate_p[:], ACT.Ln)
                ins.then_inc(S("f_ln"), 1)
                act.wait_ge(S("f_kexp"), L + 1)
                act.activation(kin[:], gate_max[:], ACT.Exp, scale=-1.0).then_inc(S("f_kin"), 1)
                ps = full_lin(act, f"f{L}qh")
                read(act.activation(flat(qin), flat(ps), ACT.Silu), f"f{L}qh")
                ps = full_lin(act, f"f{L}kv")
                read(act.copy(qkv[:, :, K0:K0 + 256], ps[:, :, 0:256]), f"f{L}kv")
                ps = full_lin(act, f"f{L}q")
                read(act.mul(qkv[:, :, 0:HALF], ps, HD ** -0.5), f"f{L}q")
                ps = full_lin(act, f"f{L}i")
                read(act.copy(vh[:], ps), f"f{L}i")
                ps = full_lin(act, f"f{L}z")
                read(act.activation(zs[:], ps, ACT.Silu), f"f{L}z")
                ps = full_lin(act, f"f{L}g")
                read(act.activation(zg[:], ps, ACT.Silu), f"f{L}g")
                for lv in range(1, LEVELS + 1):
                    act.wait_ge(S("level_diff"), LEVELS * L + lv)
                    act.activation(decay[lv % 2][:], decay[lv % 2][:], ACT.Exp).then_inc(S("level_exp"), 1)
                    if lv in (3, 5, 7, 8):
                        g, c = {3: (ga, "ga0"), 5: (ga, "ga1"), 7: (gh, "gh0"), 8: (gh, "gh1")}[lv]
                        ps = full_lin(act, f"f{L}{c}")
                        half = slice(0, HALF) if c[-1] == "0" else slice(HALF, D)
                        read(act.activation(g[:, :, half], ps, ACT.Sigmoid), f"f{L}{c}")
                name = f"f{L}lv{LEVELS}"
                ps = full_tmp(act, name)
                read(act.copy(flat(cross), flat(ps)[:, 0:HALF]), name)
                ps = full_tmp(act, f"f{L}qT")
                act.wait_ge(S("level_ready"), (LEVELS + 1) * (L + 1))
                read(act.copy(flat(qTa), flat(ps)), f"f{L}qT")
                ps = full_lin(act, f"f{L}ho")
                act.activation(hs[:, :, 0:HALF], ps, ACT.Square).then_inc(S("f_hsq"), 1)
                rough_rsqrt(f"f{L}h", st[:, 1], st[:, 2])
                attention(f"f{L}a", [(i, g) for i in range(NT) for g in range(2)], QUAD, sink=True)

            squares("n", read_of("f1out1"))
            rough_rsqrt("n", st[:, 1, :, 0], st[:, 2, :, 0])

            def mixed(name, layer, j):
                ps = full_tmp(act, f"{name}hT0")
                act.wait_ge(S("mods_ready"), 1)
                for k in range(4):
                    ins = act.activation(hT[:, k, :], flat(ps)[:, k * T:(k + 1) * T], ACT.Identity,
                                         bias=modc[:, layer, 2 * j, k:k + 1], scale=modc[:, layer, 2 * j + 1, k:k + 1])
                read(ins, f"{name}hT0")

            def mlp(name, layer):
                mixed(name, layer, 1)
                for g in range(8):
                    ps = full_tmp(act, f"{name}u{g}")
                    if g >= 2:
                        act.wait_ge(*done[f"{name}hb{g - 2}"])
                    read(act.activation(flat(hb[g % 2]), flat(ps), ACT.Relu), f"{name}u{g}")
                rough_rsqrt(f"{name}ln", mv[:, :, 1], st[:, 2, :, 0])

            mixed("s0", 0, 0)
            ps = full_tmp(act, "s0ik")
            read(act.copy(ikT[:], ps[:, 0, 0:T]), "s0ik")
            ps = full_lin(act, "s0misc")
            act.copy(ckv[:], ps[:, :, 0:T]).then_inc(S("s0ckv"), 1)
            read(act.mul(iw[:], ps[:, :, T:T + 8], 8 ** -0.5 * HD ** -0.5), "s0misc")
            act.wait_ge(S("s0ckv"), 1)
            for i in range(NT):
                ins = act.activation(hs[:, i, 0:T], ckv[:, i, :], ACT.Square, accum_out=st[:, 0, i, 0:1])
            ins.then_inc(S("s0css"), 1)
            rough_rsqrt("s0c", st[:, 1, :, 0], st[:, 2, :, 0])
            ps = full_lin(act, "s0iq")
            read(act.copy(flat(iqT), flat(ps)), "s0iq")
            for i in range(NT):
                for g in range(2):
                    n = 2 * i + g
                    W = P * (i + 1)
                    ps = full_tmp(act, f"s0idx{i}{g}")
                    if n >= 2:
                        act.wait_ge(S("s0idx_used"), n - 1)
                    for a in range(2):
                        ins = act.activation(Pq[n % 2][:, 2 * a:2 * a + 2, 0:W],
                                             ps[:, a, 0:2 * W].rearrange("p (j w) -> p j w", j=2), ACT.Relu)
                    read(ins, f"s0idx{i}{g}")
                if i == 0:
                    ps = full_lin(act, "s0q0")
                    read(act.mul(flat(qT[:, 0:4, :]), flat(ps), HD ** -0.5), "s0q0")
            ps = full_lin(act, "s0q1")
            read(act.mul(flat(qT[:, 4:8, :]), flat(ps), HD ** -0.5), "s0q1")
            for r in range(2):
                ps = full_tmp(act, f"s0wuk{r}")
                read(act.copy(wukT[:, r, :], flat(ps)), f"s0wuk{r}")
            for i in range(NT):
                ps = full_lin(act, f"s0v{i}")
                read(act.copy(vv[:, i, :], flat(ps)), f"s0v{i}")
            for h in range(2):
                ps = full_tmp(act, f"s0k{h}")
                read(act.copy(flat(kT[:, 4 * h:4 * h + 4, :]), flat(ps)), f"s0k{h}")
            quads = [(i, g) for i in range(NT) for g in range(4)]
            attention("s0", quads, QUAD)
            rough_rsqrt("s0ln", mv[:, :, 1], st[:, 2, :, 0])
            mlp("s1", 0)
            mixed("s2", 1, 0)
            for n in range(2):
                for part, dst, scale in (("q", qT, HD ** -0.5), ("k", kT, 1.0)):
                    ps = full_lin(act, f"s2{part}{n}")
                    read(act.mul(flat(dst[:, 4 * n:4 * n + 4, :]), flat(ps), scale), f"s2{part}{n}")
            for n in range(2):
                ps = full_lin(act, f"s2v{n}")
                read(act.copy(vv[:, :, n * HALF:(n + 1) * HALF], ps), f"s2v{n}")
            attention("s2", quads, 2)
            for i in range(NT):
                act.wait_ge(*read_of(f"s2o{i}"))
                ins = act.activation(osq[:, i, :], hs[:, i, :], ACT.Square)
            ins.then_inc(S("s2osq"), 1)
            rough_rsqrt("s2h", st[:, 1], st[:, 2])
            rough_rsqrt("s2ln", mv[:, :, 1], st[:, 2, :, 0])
            mlp("s3", 1)

        @block.vector
        def _(dve):
            def step(ins):
                ins.then_inc(S("dve_step"), 1)
                dve.wait_ge(S("dve_step"), bump("dve_step"))

            def rsqrt(name, v, y, w):
                dve.wait_ge(S(f"{name}rough"), 1)
                step(dve.tensor_tensor(w, y, y, ALU.mult))
                step(dve.tensor_tensor(w, w, v, ALU.mult))
                step(dve.tensor_scalar(w, w, -0.5, 1.5, ALU.mult, ALU.add))
                step(dve.tensor_tensor(y, y, w, ALU.mult))

            def variance(name, ss, v, n, eps):
                dve.wait_ge(S(f"{name}ss"), 1)
                dve.tensor_scalar(v, ss, 1.0 / n, eps, ALU.mult, ALU.add).then_inc(S(f"{name}var"), 1)

            def turned(name, dst, cols, scale2=None):
                ps = flat(full_tmp(dve, name))
                for k, col in enumerate(cols):
                    ins = dve.tensor_scalar(dst[:, k, :], ps[:, k * T:(k + 1) * T], col, scale2, ALU.mult,
                                            ALU.mult if scale2 is not None else ALU.bypass)
                read(ins, name)

            dve.wait_ge(S("pairs"), 1)
            step(dve.tensor_tensor(pairx[:, 0, :], pairx[:, 0, :], pairx[:, 1, :], ALU.bitwise_xor))
            step(dve.tensor_copy(levelge[:, 0, :], pairx[:, 0, :]))
            for lv in range(1, LEVELS):
                dve.tensor_scalar(levelge[:, lv, :], levelge[:, 0, :], float(2 ** (lv - 1)), None, ALU.is_ge)
            step(dve.memset(levelge[:, LEVELS, :], 0.0))
            dve.tensor_scalar(levelmask[:, 0, :], levelge[:, 0, :], 0.0, None, ALU.is_equal)
            dve.tensor_tensor(levelmask[:, 1:, :], levelge[:, 1:LEVELS, :], levelge[:, 2:, :], ALU.subtract
                              ).then_inc(S("levels_both"), 1)
            ps = full_tmp(dve, "cols")
            dve.tensor_copy(colA[:], ps[:, 0, 0:P])
            read(dve.tensor_copy(colB[:], ps[:, 0, P:P + 5]), "cols")
            ps = full_tmp(dve, "relvec")
            read(dve.tensor_copy(relvec[:], ps[0:16, 0, 0:DIST]), "relvec")
            dve.wait_ge(S("small_landed"), 16 * 8)
            dve.wait_ge(S("invf"), 1)
            step(dve.tensor_copy(posf[:], posi[:]))
            for i in range(NT):
                for c in range(2):
                    ins = dve.tensor_scalar(ang[:, i, c, :], invf[:], posf[:, i:i + 1], None, ALU.mult)
            step(ins)
            for c in range(2):
                ins = dve.tensor_scalar(angk[:, :, c, :], ang[:, :, c, :], 1.0 / TURN, 0.25 * c, ALU.mult, ALU.add)
            step(ins)
            step(dve.tensor_scalar(angk[:], angk[:], ROUNDER, None, ALU.add))
            step(dve.tensor_scalar(angk[:], angk[:], -ROUNDER, None, ALU.add))
            for part in TURN_PARTS:
                step(dve.scalar_tensor_tensor(ang[:], angk[:], -part, ang[:], ALU.mult, ALU.add))
            step(dve.tensor_scalar(ang[:, :, 1, :], ang[:, :, 1, :], TURN / 4, None, ALU.add))
            dve.tensor_scalar(ang[:], ang[:], SIN_MAX, -SIN_MAX, ALU.min, ALU.max).then_inc(S("angles"), 1)
            step(dve.tensor_copy(lbw[:, 0:2, :], colA[:, 16:24].rearrange("p (l h) -> p l h", l=2)))
            step(dve.tensor_tensor(lbw[:, 2, :], lbw[:, 0, :], lbw[:, 1, :], ALU.max))
            dve.tensor_tensor(lbw[:, 0:2, :], lbw[:, 0:2, :], lbw[:, 2, :].unsqueeze(1).broadcast_to([P, 2, 4]),
                              ALU.subtract).then_inc(S("lb_max"), 1)
            dve.wait_ge(S("lb_exp"), 1)
            step(dve.tensor_tensor(lbw[:, 2, :], lbw[:, 0, :], lbw[:, 1, :], ALU.add))
            step(dve.reciprocal(lbw[:, 2, :], lbw[:, 2, :]))
            step(dve.tensor_tensor(lbw[:, 0:2, :], lbw[:, 0:2, :], lbw[:, 2, :].unsqueeze(1).broadcast_to([P, 2, 4]),
                                   ALU.mult))
            step(dve.tensor_tensor(lbw[:, 3, :], lbw[:, 0, :], lbw[:, 1, :], ALU.add))
            step(dve.tensor_tensor(lbw[:, 3, :], lbw[:, 3, :], lbw[:, 0, :], ALU.subtract))
            step(dve.tensor_scalar(lbw[:, 4, :], lbw[:, 3, :], -1.0, 1.0, ALU.mult, ALU.add))
            dve.wait_ge(S("lamb_landed"), 16)
            for n in range(2):
                step(dve.tensor_tensor(lamb[:, 2 * n, :], lamb[:, 2 * n, :], lamb[:, 2 * n + 1, :], ALU.mult))
                ins = dve.tensor_reduce(lams[:, n:n + 1], lamb[:, 2 * n, :], AX.X, ALU.add)
            ins.then_inc(S("lam_dots"), 1)
            dve.wait_ge(S("lam_exp"), 1)
            step(dve.tensor_tensor(lams[:, 2:3], lams[:, 1:2], lams[:, 0:1], ALU.subtract))
            step(dve.tensor_scalar(lams[:, 3:4], lams[:, 2:3], -LAM_INIT, None, ALU.add))
            dve.wait_ge(S("csil"), 1)
            dve.tensor_copy(csb[:], csil[:].unsqueeze(2).broadcast_to([P, KT, P])).then_inc(S("cond_ready"), 1)

            ada_order = [(layer, n) for layer in range(2) for n in range(12)]

            def fill(n):
                for _ in range(n):
                    layer, m = ada_order.pop(0)
                    section, half = m // 2, m % 2
                    name = f"ada{layer}_{m}"
                    ps = full_lin(dve, name)
                    if section in (2, 5):
                        g = gmod[:, 2 * layer + section // 4, half * HALF:(half + 1) * HALF]
                        dve.wait_ge(S("gbias_landed"), 64)
                        ins = dve.scalar_tensor_tensor(g, ps[:, 0, :], 1.0, g, ALU.add, ALU.add)
                    else:
                        scale = section in (1, 4)
                        bias = colA[:, 24 + 48 * layer + 4 * m:24 + 48 * layer + 4 * m + 4]
                        row = {0: 0, 1: 1, 3: 2, 4: 3}[section]
                        ins = dve.scalar_tensor_tensor(modc[:, layer, row, 4 * half:4 * half + 4], ps[:, 0, 0:4],
                                                       1.0 if scale else 0.0, bias, ALU.add, ALU.add)
                    read(ins, name)

            def softmax(name, n, quads, mask, sink=None):
                i, g = quads[n]
                W = P * (i + 1)
                ps = full_tmp(dve, f"{name}s{n}")
                if n >= 2:
                    dve.wait_ge(*done[f"{name}p{n - 2}"])
                buf = Pq[n % 2]
                for a in range(2):
                    ins = dve.tensor_tensor(buf[:, 2 * a:2 * a + 2, 0:W],
                                            ps[:, a, 0:2 * W].rearrange("p (j w) -> p j w", j=2),
                                            mask(i, g, a), ALU.add)
                read(ins, f"{name}s{n}")
                dve.wait_ge(*read_of(f"{name}s{n}"))
                return buf[:, :, 0:W]

            def maximum(name, n, g, scores, sink=None):
                step(dve.tensor_reduce(qst[:, n, 0, :], scores, AX.X, ALU.max))
                if sink is not None:
                    step(dve.tensor_tensor(qst[:, n, 0, :], qst[:, n, 0, :], sink, ALU.max))
                    dve.tensor_tensor(qst[:, n, 4, :], sink, qst[:, n, 0, :], ALU.subtract)
                dve.tensor_scalar(qst[:, n, 1, :], qst[:, n, 0, :], -1.0, None, ALU.mult
                                  ).then_inc(S(f"{name}max"), 1)

            def by_slot(v):
                return v.rearrange("p (j a) -> p a j", a=2)

            def slots(v):
                return v.rearrange("p (a j) -> p a j", a=2)

            for L in range(2):
                fill(1)
                variance(f"f{L}", st[:, 0, :, 0], st[:, 1, :, 0], D, EPS)
                rsqrt(f"f{L}", st[:, 1, :, 0], st[:, 2, :, 0], st[:, 0, :, 0])
                for i in range(NT):
                    ins = dve.tensor_scalar(hs[:, i, :], x[:, i, :], st[:, 2, i, 0:1], None, ALU.mult)
                ins.then_inc(S("f_scaled"), 1)
                for h in range(2):
                    turned(f"f{L}hT{h}", hT[:, 4 * h:4 * h + 4, :],
                           [colA[:, 8 * L + k:8 * L + k + 1] for k in range(4 * h, 4 * h + 4)])
                ps = full_lin(dve, f"f{L}f")
                dve.tensor_scalar(flat(gate_min), flat(ps), 0.0, None, ALU.min)
                read(dve.tensor_scalar(flat(gate_max), flat(ps), 0.0, None, ALU.max), f"f{L}f")
                dve.wait_ge(S("f_pn"), L + 1)
                if L == 1:
                    step(dve.tensor_tensor(flat(gate_lnsum), flat(gate_p), flat(gate_n), ALU.add))
                    for h in range(4):
                        ins = dve.scalar_tensor_tensor(gate_p[:, h, :], gate_n[:, h, :], lbw[:, 3, h:h + 1],
                                                       gate_p[:, h, :], ALU.mult, ALU.add)
                    ins.then_inc(S("f_sum"), 1)
                else:
                    dve.tensor_tensor(flat(gate_lnsum), flat(gate_p), flat(gate_n), ALU.add
                                      ).then_inc(S("f_sum"), 1)
                dve.wait_ge(S("f_ln"), L + 1)
                step(dve.tensor_tensor(flat(gate_p), flat(gate_p if L else gate_min), flat(gate_lnsum), ALU.subtract))
                dve.tensor_tensor(flat(gate_max), flat(gate_max), flat(gate_lnsum), ALU.add
                                  ).then_inc(S("f_kexp"), 1)
                dve.wait_ge(S("chunkmask"), 1)
                dve.wait_ge(S("f_kexp"), L + 1)
                step(dve.tensor_tensor_scan(flat(G), chunkmask[:], flat(gate_p), 0.0, ALU.mult, ALU.add))
                dve.wait_ge(S("f_kin"), L + 1)
                ins = dve.memset(flat(scor), 0.0)
                if L == 1:
                    for h in range(4):
                        ins = dve.tensor_scalar(kin[:, h, :], kin[:, h, :], lbw[:, 4, h:h + 1], None, ALU.mult)
                step(ins)
                dve.wait_ge(*read_of(f"f{L}kv"))
                dve.wait_ge(*read_of(f"f{L}q"))
                dve.wait_ge(S("trig"), 1)
                for i in range(NT):
                    heads = qkv[:, i, 0:640].rearrange("p (h d) -> p h d", h=10)
                    x1, x2 = heads[:, :, 0:ROPE_HALF], heads[:, :, ROPE_HALF:2 * ROPE_HALF]
                    sin, cos = (trig[:, i, c, :].unsqueeze(1).broadcast_to([P, 10, ROPE_HALF]) for c in range(2))
                    dve.tensor_tensor(ropet[:, 0], x1, cos, ALU.mult)
                    dve.tensor_tensor(ropet[:, 1], x2, sin, ALU.mult)
                    dve.tensor_tensor(ropet[:, 2], x2, cos, ALU.mult)
                    step(dve.tensor_tensor(ropet[:, 3], x1, sin, ALU.mult))
                    dve.tensor_tensor(x1, ropet[:, 0], ropet[:, 1], ALU.subtract)
                    step(dve.tensor_tensor(x2, ropet[:, 2], ropet[:, 3], ALU.add))
                for i in range(NT):
                    for a in range(2):
                        ins = dve.tensor_copy(kdup[:, i, :, a, :], qkv[:, i, K0:V0].rearrange("p (g d) -> p g d", g=2))
                ins.then_inc(S("f_rope"), 1)
                dve.wait_ge(*read_of(f"f{L}qh"))
                dve.nop().then_inc(S("level_ready"), 1)
                ps = full_tmp(dve, f"f{L}kT")
                read(dve.tensor_copy(flat(kTd), flat(ps)[:, 0:2 * T]), f"f{L}kT")

                def differences(lv):
                    buf = decay[lv % 2]
                    if lv >= 3:
                        dve.wait_ge(*done[f"f{L}lv{lv - 2}"])
                    if lv < LEVELS:
                        b = 2 ** (lv - 1)
                        g = flat(G).rearrange("p (n h b) -> p n h b", h=2, b=b)
                        d = flat(buf).rearrange("p (n h b) -> p n h b", h=2, b=b)
                        ref = g[:, :, 0, b - 1:b].broadcast_to([P, 4 * T // (2 * b), b])
                        if 2 * b <= CHUNK:
                            dve.tensor_tensor(d[:, :, 1, :], g[:, :, 1, :], ref, ALU.subtract)
                        else:
                            dve.tensor_copy(d[:, :, 1, :], g[:, :, 1, :])
                        ins = dve.tensor_tensor(d[:, :, 0, :], ref, g[:, :, 0, :], ALU.subtract)
                    else:
                        g = G.rearrange("p h (c t) -> p h c t", c=4)
                        d = buf.rearrange("p h (c t) -> p h c t", c=4)

                        def end(c):
                            return g[:, :, c, CHUNK - 1:CHUNK].broadcast_to([P, 4, CHUNK])

                        dve.tensor_copy(d[:, :, 2, :], g[:, :, 2, :])
                        dve.tensor_tensor(d[:, :, 3, :], g[:, :, 3, :], end(2), ALU.add)
                        dve.tensor_tensor(d[:, :, 1, :], end(1), g[:, :, 1, :], ALU.subtract)
                        step(dve.tensor_tensor(d[:, :, 0, :], end(0), g[:, :, 0, :], ALU.subtract))
                        ins = dve.tensor_tensor(d[:, :, 0, :], d[:, :, 0, :], end(1), ALU.add)
                    ins.then_inc(S("level_diff"), 1)

                def factors(lv):
                    dve.wait_ge(S("level_exp"), LEVELS * L + lv)
                    b = 2 ** (lv - 1)
                    d, q, k = (flat(v).rearrange("p (n h b) -> p n h b", h=2, b=b) for v in (decay[lv % 2], qin, kin))
                    dve.tensor_tensor(d[:, :, 1, :], d[:, :, 1, :], q[:, :, 1, :], ALU.mult)
                    dve.tensor_tensor(d[:, :, 0, :], d[:, :, 0, :], k[:, :, 0, :], ALU.mult
                                      ).then_inc(S("level_ready"), 1)

                def gather(lv):
                    ps = flat(full_tmp(dve, f"f{L}lv{lv}"))
                    if lv == 0:
                        dve.wait_ge(S("levels"), 1)
                    else:
                        dve.wait_ge(*read_of(f"f{L}lv{lv - 1}"))
                    read(dve.copy_predicated(scor[:], levelmask[:, lv, :].bitcast(I32).unsqueeze(1).broadcast_to([P, 8, P]),
                                             ps.rearrange("p (n t) -> p n t", n=8)), f"f{L}lv{lv}")

                differences(1)
                for lv in range(1, LEVELS + 1):
                    if lv < LEVELS:
                        differences(lv + 1)
                    factors(lv)
                    gather(lv - 1)
                dve.wait_ge(S("f_hsq"), L + 1)
                if L == 0:
                    dve.memset(st[:, 0, :, 4:8], 1.0)
                dve.tensor_reduce(st[:, 0, :, 0:4], hs[:, :, 0:HALF].rearrange("p i (h d) -> p i h d", h=4),
                                  AX.X, ALU.add).then_inc(S(f"f{L}hss"), 1)
                variance(f"f{L}h", st[:, 0], st[:, 1], P, EPS)
                rsqrt(f"f{L}h", st[:, 1], st[:, 2], st[:, 0])
                ps = full_lin(dve, f"f{L}ho")
                for i in range(NT):
                    ins = dve.tensor_tensor(hs[:, i, HALF:D].rearrange("p (h d) -> p h d", h=4),
                                            ps[:, i, :].rearrange("p (h d) -> p h d", h=4),
                                            st[:, 2, i, 0:4].unsqueeze(2).broadcast_to([P, 4, P]), ALU.mult)
                read(ins, f"f{L}ho")
                dve.wait_ge(*read_of(f"f{L}ho"))
                dve.wait_ge(*read_of(f"f{L}g"))
                dve.tensor_tensor(hs[:, :, HALF:D], hs[:, :, HALF:D], zg[:], ALU.mult).then_inc(S("f_b"), 1)
                quads = [(i, g) for i in range(NT) for g in range(2)]
                name = f"f{L}a"
                dve.wait_ge(S("band"), 1)
                dve.wait_ge(S("sinks_landed"), 16)

                def window(i, g, a):
                    m = band[:] if i else band[:, P:T]
                    return m.unsqueeze(1).broadcast_to([P, 2, P * (i + 1)])

                def total(n):
                    i, g = quads[n]
                    dve.wait_ge(S(f"{name}exp"), n + 1)
                    step(dve.tensor_tensor(qst[:, n, 2, :], qst[:, n, 2, :], qst[:, n, 3, :], ALU.add))
                    dve.reciprocal(by_slot(rden[:, i, 4 * g:4 * g + 4]), slots(qst[:, n, 2, :])
                                   ).then_inc(S(f"{name}prob"), 1)

                for n, (i, g) in enumerate(quads):
                    sink = by_slot(sinks[:, 8 * L + 4 * g:8 * L + 4 * g + 4])
                    scores = softmax(name, n, quads, window)
                    maximum(name, n, g, scores, sink)
                    if n >= 1:
                        total(n - 1)
                total(3)
                dve.wait_ge(S(f"{name}prob"), 4)
                dve.wait_ge(*done[f"{name}o1"])
                ps = full_lin(dve, f"{name}o0")
                for i in range(NT):
                    ins = dve.tensor_tensor(hs[:, i, 0:HALF].rearrange("p (h d) -> p h d", h=8),
                                            ps[:, i, :].rearrange("p (h d) -> p h d", h=8),
                                            rden[:, i, 0:8].unsqueeze(2).broadcast_to([P, 8, HD]), ALU.mult)
                read(ins, f"{name}o0")
                dve.wait_ge(*read_of(f"{name}o0"))
                dve.wait_ge(*read_of(f"f{L}z"))
                dve.tensor_tensor(hs[:, :, 0:HALF], hs[:, :, 0:HALF], zs[:], ALU.mult).then_inc(S("f_a"), 1)
                fill(3)
                turned(f"f{L}bT0", bT, [colB[:, 3 + L:4 + L]] * 4)
                ps = full_tmp(dve, f"f{L}aT0")
                read(dve.tensor_copy(flat(aT), flat(ps)), f"f{L}aT0")
                dve.wait_ge(*read_of(f"f{L}gh0"))
                dve.wait_ge(*read_of(f"f{L}gh1"))
                for c in range(2):
                    cols = slice(c * HALF, (c + 1) * HALF)
                    ps = full_lin(dve, f"f{L}ua{c}")
                    read(dve.tensor_tensor(hs[:, :, cols], ps, ga[:, :, cols], ALU.mult), f"f{L}ua{c}")
                    ps = full_lin(dve, f"f{L}uh{c}")
                    read(dve.tensor_tensor(gh[:, :, cols], ps, gh[:, :, cols], ALU.mult), f"f{L}uh{c}")
                    dve.wait_ge(*read_of(f"f{L}ua{c}"))
                    dve.wait_ge(*read_of(f"f{L}uh{c}"))
                    ins = dve.tensor_tensor(hs[:, :, cols], hs[:, :, cols], gh[:, :, cols], ALU.add)
                ins.then_inc(S("f_merged"), 1)
                fill(2)
                for h in range(2):
                    ps = full_tmp(dve, f"f{L}mT{h}")
                    read(dve.tensor_copy(flat(hT[:, 4 * h:4 * h + 4, :]), flat(ps)), f"f{L}mT{h}")
                for c in range(2):
                    cols = slice(c * HALF, (c + 1) * HALF)
                    ps = full_lin(dve, f"f{L}out{c}")
                    read(dve.tensor_tensor(x[:, :, cols], x[:, :, cols], ps, ALU.add), f"f{L}out{c}")
            fill(len(ada_order))
            dve.nop().then_inc(S("mods_ready"), 1)

            variance("n", st[:, 0, :, 0], st[:, 1, :, 0], D, EPS)
            rsqrt("n", st[:, 1, :, 0], st[:, 2, :, 0], st[:, 0, :, 0])
            dve.wait_ge(S("lnp_landed"), 32)
            for i in range(NT):
                ins = dve.scalar_tensor_tensor(x[:, i, :], x[:, i, :], st[:, 2, i, 0:1], lnp[:, 0, :],
                                               ALU.mult, ALU.mult)
            ins.then_inc(S("s0x"), 1)

            def mixed(name, layer, j):
                ps = flat(full_tmp(dve, f"{name}hT1"))
                for k in range(4):
                    ins = dve.tensor_scalar(hT[:, 4 + k, :], ps[:, k * T:(k + 1) * T],
                                            modc[:, layer, 2 * j + 1, 4 + k:5 + k], modc[:, layer, 2 * j, 4 + k:5 + k],
                                            ALU.mult, ALU.add)
                read(ins, f"{name}hT1")

            def residual(name, n, after):
                for c in range(2):
                    cols = slice(c * HALF, (c + 1) * HALF)
                    ps = full_lin(dve, f"{name}y{c}")
                    g = gmod[:, n, cols].unsqueeze(1).broadcast_to([P, NT, HALF])
                    read(dve.tensor_tensor(hs[:, :, cols], ps, g, ALU.mult), f"{name}y{c}")
                    dve.wait_ge(*read_of(f"{name}y{c}"))
                    step(dve.scalar_tensor_tensor(x[:, :, cols], x[:, :, cols], ALPHA, hs[:, :, cols],
                                                  ALU.mult, ALU.add))
                    for i in range(NT):
                        ins = dve.bn_stats(bns[:, i, c, :], x[:, i, cols])
                step(ins)
                for i in range(NT):
                    ins = dve.bn_aggr(mv[:, i, :], bns[:, i, :, :])
                step(ins)
                dve.tensor_scalar(mv[:, :, 1], mv[:, :, 1], LN_EPS, None, ALU.add).then_inc(S(f"{name}lnvar"), 1)
                rsqrt(f"{name}ln", mv[:, :, 1], st[:, 2, :, 0], st[:, 0, :, 0])
                dve.wait_ge(S("lnp_landed"), 32 * (n + 2))
                for i in range(NT):
                    step(dve.tensor_scalar(x[:, i, :], x[:, i, :], mv[:, i, 0:1], st[:, 2, i, 0:1],
                                           ALU.subtract, ALU.mult))
                for i in range(NT):
                    step(dve.tensor_tensor(x[:, i, :], x[:, i, :], lnp[:, 0, :], ALU.mult))
                for i in range(NT):
                    ins = dve.tensor_tensor(x[:, i, :], x[:, i, :], lnp[:, 1, :], ALU.add)
                ins.then_inc(S(f"{after}x"), 1)

            def mlp(name, layer, n, after):
                mixed(name, layer, 1)
                for g in range(8):
                    dve.wait_ge(*read_of(f"{name}u{g}"))
                    dve.tensor_tensor(flat(hb[g % 2]), flat(hb[g % 2]), flat(hb[g % 2]), ALU.mult
                                      ).then_inc(S(f"{name}act"), 1)
                residual(name, n, after)

            def biased(i, g, a):
                return Mbias[:, 4 * g + a:4 * g + 4:2, 0:P * (i + 1)][:, :, ::-1]

            mixed("s0", 0, 0)
            dve.wait_ge(S("s0css"), 1)
            dve.tensor_scalar(st[:, 1, :, 0], st[:, 0, :, 0], 1.0 / T, LN_EPS, ALU.mult, ALU.add
                              ).then_inc(S("s0cvar"), 1)
            rsqrt("s0c", st[:, 1, :, 0], st[:, 2, :, 0], st[:, 0, :, 0])
            for i in range(NT):
                ins = dve.tensor_scalar(ckv[:, i, :], ckv[:, i, :], st[:, 2, i, 0:1], None, ALU.mult)
            ins.then_inc(S("s0ckvn"), 1)
            for i in range(NT):
                for g in range(2):
                    n = 2 * i + g
                    W = P * (i + 1)
                    dve.wait_ge(*read_of(f"s0idx{i}{g}"))
                    for s in range(QUAD):
                        head = 4 * g + 2 * (s % 2) + s // 2
                        r, v = Pq[n % 2][:, s, 0:W], iw[:, i, head:head + 1]
                        if g == 0 and s == 0:
                            ins = dve.tensor_scalar(isc[:, i, 0:W], r, v, None, ALU.mult)
                        else:
                            ins = dve.scalar_tensor_tensor(isc[:, i, 0:W], r, v, isc[:, i, 0:W], ALU.mult, ALU.add)
                        if s < QUAD - 1:
                            step(ins)
                    ins.then_inc(S("s0idx_used"), 1)
                    dve.wait_ge(S("s0idx_used"), n + 1)
            turned("s0ckvT", ckvT, [colB[:, r:r + 1] for r in range(2)])
            dve.wait_ge(S("s0causal"), 1)
            for i in range(NT):
                W = P * (i + 1)
                for n in range(TOPK // 8):
                    src = isc if n == 0 else iwk
                    step(dve.max(top8[:], src[:, i, 0:W]))
                    step(dve.match_replace(iwk[:, i, 0:W], top8[:], src[:, i, 0:W], LOWEST))
                step(dve.tensor_tensor(isc[:, i, 0:W], isc[:, i, 0:W], iwk[:, i, 0:W], ALU.is_equal))
                step(dve.tensor_scalar(isc[:, i, 0:W], isc[:, i, 0:W], NEG, None, ALU.mult))
            quads = [(i, g) for i in range(NT) for g in range(4)]
            dve.wait_ge(S("Mbias"), 16)

            def total_s0(n):
                i, g = quads[n]
                dve.wait_ge(S("s0exp"), n + 1)
                dve.reciprocal(by_slot(rden[:, i, 4 * g:4 * g + 4]), slots(qst[:, n, 2, :])
                               ).then_inc(S("s0prob"), 1)

            def scaled_out(i):
                dve.wait_ge(S("s0prob"), 4 * i + 4)
                ps = full_lin(dve, f"s0o{i}")
                read(dve.tensor_tensor(hs[:, i, :].rearrange("p (h d) -> p h d", h=16),
                                       flat(ps).rearrange("p (h d) -> p h d", h=16),
                                       rden[:, i, :].unsqueeze(2).broadcast_to([P, 16, HD]), ALU.mult), f"s0o{i}")

            for n, (i, g) in enumerate(quads):
                W = P * (i + 1)
                scores = softmax("s0", n, quads, biased)
                step(dve.tensor_tensor(scores, scores, isc[:, i, 0:W].unsqueeze(1).broadcast_to([P, QUAD, W]), ALU.add))
                maximum("s0", n, g, scores)
                if n >= 1:
                    total_s0(n - 1)
                if n == 6:
                    scaled_out(0)
            total_s0(7)
            scaled_out(1)
            for h in range(2):
                ps = full_tmp(dve, f"s0oT{h}")
                read(dve.tensor_copy(flat(hT[:, 4 * h:4 * h + 4, :]), flat(ps)), f"s0oT{h}")
            residual("s0", 0, "s1")
            mlp("s1", 0, 1, "s2")
            mixed("s2", 1, 0)

            def combine(n):
                i, g = quads[n]
                W = P * (i + 1)
                dve.wait_ge(S("s2exp"), n + 1)
                step(dve.reciprocal(qst[:, n, 3, :], qst[:, n, 2, :]))
                step(dve.tensor_scalar(qst[:, n, 3, 2:4], qst[:, n, 3, 2:4], lams[:, 3:4], None, ALU.mult))
                for j in range(2):
                    ins = dve.tensor_scalar(Pq[n % 2][:, j, 0:W], Pq[n % 2][:, j, 0:W], qst[:, n, 3, j:j + 1],
                                            None, ALU.mult)
                step(ins)
                for j in range(2):
                    ins = dve.scalar_tensor_tensor(Pq[n % 2][:, j, 0:W], Pq[n % 2][:, 2 + j, 0:W],
                                                   qst[:, n, 3, 2 + j:3 + j], Pq[n % 2][:, j, 0:W], ALU.mult, ALU.add)
                ins.then_inc(S("s2prob"), 1)

            def raw_out(i):
                ps = full_lin(dve, f"s2o{i}")
                read(dve.tensor_copy(hs[:, i, :], flat(ps)), f"s2o{i}")

            for n, (i, g) in enumerate(quads):
                scores = softmax("s2", n, quads, biased)
                maximum("s2", n, g, scores)
                if n >= 1:
                    combine(n - 1)
                if n == 6:
                    raw_out(0)
            combine(7)
            raw_out(1)
            dve.wait_ge(S("s2osq"), 1)
            dve.tensor_reduce(st[:, 0], osq.rearrange("p i (h d) -> p i h d", h=8), AX.X, ALU.add
                              ).then_inc(S("s2hss"), 1)
            variance("s2h", st[:, 0], st[:, 1], P, LN_EPS)
            rsqrt("s2h", st[:, 1], st[:, 2], st[:, 0])
            for i in range(NT):
                o = hs[:, i, :].rearrange("p (h d) -> p h d", h=8)
                ins = dve.tensor_tensor(o, o, st[:, 2, i, :].unsqueeze(2).broadcast_to([P, 8, P]), ALU.mult)
            ins.then_inc(S("s2o"), 1)
            for h in range(2):
                turned(f"s2oT{h}", hT[:, 4 * h:4 * h + 4, :], [colB[:, 2:3]] * 4, 1.0 - LAM_INIT)
            residual("s2", 2, "s3")
            mlp("s3", 1, 3, "s4")


_INS = ["x", "positions", "norm_w", "w_in", "attn_sinks", "hgrn_norm_w", "w_up_attn", "w_up_hgrn", "w_out",
        "lb_logits", "final_norm_w", "c_2", "rel_bias_2", "ada_w_2", "ada_b_2", "ln_g_2", "ln_b_2", "a_w_in_2",
        "a_kv_norm_2", "a_w_uk_2", "a_w_uv_2", "a_w_o_2", "b_w_in_2", "b_lambda_2", "b_subln_2", "b_w_o_2",
        "mlp_w1_2", "mlp_w2_2"]


def kernel(**inputs):
    import concourse.bacc as _bacc
    from concourse.bass_utils import run_bass_kernel_spmd as _run

    nc = _bacc.Bacc("TRN2", target_bir_lowering=False, num_devices=1)
    arrays, args = {}, {}
    for name in _INS:
        a = np.ascontiguousarray(inputs[name])
        arrays[f"in_{name}"] = a
        args[name] = nc.dram_tensor(f"in_{name}", a.shape, mybir.dt.from_np(a.dtype), kind="ExternalInput").ap()
    onehot = bucket_onehot()
    arrays["onehot_table"] = onehot
    args["onehot"] = nc.dram_tensor("onehot_table", onehot.shape, F32, kind="ExternalInput").ap()
    out = nc.dram_tensor("out_0", (1, T, D), F32, kind="ExternalOutput").ap()
    build_program(nc, args, out)
    r = _run(nc, [arrays], core_ids=[0])
    return r.results[0]["out_0"]
```

```python
from contextlib import ExitStack

import numpy as np

import concourse.bass as bass
from concourse import mybir

ALU = mybir.AluOpType
ACT = mybir.ActivationFunctionType
AX = mybir.AxisListType
F32 = mybir.dt.float32
F32R = mybir.dt.float32r
I32 = mybir.dt.int32

P = 128
T = 256
NT = T // P
D = 1024
KT = D // P
HD = 64
HALF = 512
EPS = 1e-6
LN_EPS = 1e-5
NEG = -1e30
LOWEST = -3e38
TOPK = 64
ALPHA = 4 ** 0.25
LAM_INIT = 0.8 - 0.6 * float(np.exp(-0.3))
RING = 4
PARTS = 3
NBUCKET = 32
DIST = 3 * P - 1
ROPE_HALF = 8
QUAD = 4
LEVELS = 8
CHUNK = 64
ARENA = 65
TURN = float(2 * np.pi)
TURN_PARTS = [6.28125, 0.0019350051879882812, 3.0199159819567e-07]
ROUNDER = 1.5 * 2.0 ** 23
SIN_MAX = 3.1415925
ADA_START = [[(0, 0)], [(0, 8)]]
ADA_WINDOW = [{1: [(0, 1)], 2: [(0, 2)], 3: [(0, 3)], 4: [(0, 4)]}, {1: [(0, 9)], 2: [(0, 10)], 3: [(0, 11)], 4: [(1, 0)]}]
ADA_GATED = [[(0, 5), (0, 6)], [(1, 1), (1, 2)]]
ADA_MERGE = [[(0, 7)], [(1, 3)]]
ADA_SPARSE = {n: [(1, 5 + n)] for n in range(1, 5)}
ADA_DIFF = {1: [(1, 4)], 2: [(1, 5)], 3: [(1, 10)], 4: [(1, 11)]}
Q0, K0, V0, Z0, QH0, F0, I0, G0, GA0, GH0 = 0, 512, 640, 768, 1280, 1792, 2304, 2816, 3328, 4352


def bucket_onehot():
    edges = list(range(16)) + [int(np.ceil(16 * 8 ** (k / 16) - 1e-9)) for k in range(16)] + [T]
    table = np.zeros((NBUCKET + 1, DIST), np.float32)
    for b in range(NBUCKET):
        table[b, edges[b] + P - 1:edges[b + 1] + P - 1] = 1.0
    table[0, :P - 1] = 1.0
    table[NBUCKET, :P - 1] = NEG
    return table


def build_program(nc, I, out):
    with ExitStack() as ctx:
        def sb(name, shape, dt=F32):
            return ctx.enter_context(nc.sbuf_tensor(name, shape, dt))

        sems = {}

        def S(name):
            if name not in sems:
                sems[name] = ctx.enter_context(nc.semaphore(name))
            return sems[name]

        lin_ps = ctx.enter_context(nc.psum_tensor("lin_ps", [P, 4, HALF], F32))
        tmp_ps = ctx.enter_context(nc.psum_tensor("tmp_ps", [P, 4, HALF], F32))

        ring = sb("ring", [P, RING, 4, HALF])
        x = sb("x", [P, NT, D])
        whi = sb("whi", [P, PARTS, 2, HALF], F32R)
        wlo = sb("wlo", [P, PARTS, 2, HALF], F32R)
        hThi = sb("hThi", [P, KT, T], F32R)
        hTlo = sb("hTlo", [P, KT, T], F32R)
        hbhi = sb("hbhi", [P, 2, QUAD, T], F32R)
        hblo = sb("hblo", [P, 2, QUAD, T], F32R)
        ident = sb("ident", [P, P])
        band = sb("band", [P, T])
        levelmask = sb("levelmask", [P, LEVELS, P])
        chunkmask = sb("chunkmask", [P, 4 * T])
        stackA = sb("stackA", [P, P])
        stackB = sb("stackB", [5, P])
        colA = sb("colA", [P, P])
        colB = sb("colB", [P, 5])
        sinks = sb("sinks", [P, 16])
        lamb = sb("lamb", [P, 4, HD])
        posi = sb("posi", [P, NT], I32)
        posf = sb("posf", [P, NT])
        invf = sb("invf", [P, ROPE_HALF])
        ang = sb("ang", [P, NT, 2, ROPE_HALF])
        angk = sb("angk", [P, NT, 2, ROPE_HALF])
        trig = sb("trig", [P, NT, 2, ROPE_HALF])
        lbw = sb("lbw", [P, 6, 4])
        lams = sb("lams", [P, 8])
        csil = sb("csil", [P, KT])
        csb = sb("csb", [P, KT, P])
        modc = sb("modc", [P, 2, 4, KT])
        gmod = sb("gmod", [P, 2, D])
        relT = sb("relT", [NBUCKET + 1, 16])
        lnp = sb("lnp", [P, 2, D])
        st = sb("st", [P, 3, 2, 8])
        bns = sb("bns", [P, NT, 2, 6])
        mv = sb("mv", [P, NT, 2])
        qst = sb("qst", [P, 8, 6, QUAD])
        rden = sb("rden", [P, NT, 16])
        ropet = sb("ropet", [P, 4, 10, ROPE_HALF])
        hs = sb("hs", [P, NT, D])
        iw = sb("iw", [P, NT, 8])
        top8 = sb("top8", [P, 8])
        arena = sb("arena", [P, ARENA * 1024 // 4])
        scratch = nc.dram_tensor("relvec_dram", (16, DIST), F32).ap()

        def at(k, *shape):
            n = int(np.prod(shape))
            v = arena[:, int(k * 1024):int(k * 1024) + n]
            names = " ".join(f"d{j}" for j in range(len(shape)))
            return v if len(shape) == 1 else v.rearrange(
                f"p ({names}) -> p {names}", **{f"d{j}": s for j, s in enumerate(shape)})

        qkv = at(0, NT, 768)
        zs = at(1.5, NT, HALF)
        ga = at(2.5, NT, D)
        gh = at(4.5, NT, D)
        vh = at(6.5, NT, HALF)
        zg = at(7.5, NT, HALF)
        qin = at(8.5, 4, T)
        kin = at(9.5, 4, T)
        G = at(10.5, 4, T)
        decay = [at(11.5, 4, T), at(12.5, 4, T)]
        scor = at(13.5, 8, P)
        cross = at(14.5, 4, P)
        kdup = at(15, NT, 2, 2, HD)
        kTd = at(15.5, 2, T)
        Pq_first = [decay[0], decay[1]]
        pT_first = [at(9.5, QUAD * T), at(10.5, QUAD * T)]
        qTa = qin
        onehot, relvec = at(2, DIST)[0:NBUCKET + 1], at(2.5, DIST)[0:16]
        pairx = at(3, 2, P).bitcast(I32)
        levelge = at(0, LEVELS + 1, P)
        gate_min, gate_max, gate_p, gate_n, gate_lnsum = decay[0], decay[1], at(13.5, 4, T), kin, G
        qT = at(0, KT, T)
        kT = at(2, KT, T)
        vv = at(4, NT, D)
        iqT = at(6, 4, T)
        ikT = at(7, T)
        ckvT = at(7.25, 2, T)
        wukT = at(7.75, 2, D)
        isc = at(9.75, NT, T)
        Mbias = at(10.25, 16, T)
        Pq_second = [at(14.25, QUAD, T), at(15.25, QUAD, T)]
        pT_second = [at(7.75, QUAD * T), at(8.75, QUAD * T)]
        hidden = [at(6, QUAD, T), at(7, QUAD, T)]
        osq = at(6, NT, D)
        iwk, ckv = hs[:, :, T:2 * T], hs[:, :, 2 * T:3 * T]

        done = {}
        turn_tmp, turn_lin = {}, {}
        units, halves, halves_at = [], [], {}
        count = {}

        def bump(name, n=1):
            count[name] = count.get(name, 0) + n
            return count[name]

        def read_of(name):
            if name in turn_tmp:
                n = turn_tmp[name]
                return S(f"tmp_read{n % 2}"), n // 2 + 1
            half, n = turn_lin[name]
            return S(f"lin_read{half}"), n + 1

        def win(w, c0, n, k0=0):
            return w[k0 * P:(k0 + 4) * P, c0:c0 + n].rearrange("(k p) n -> p k n", p=P)

        hT = (hThi, hTlo)

        block = ctx.enter_context(nc.Block())

        @block.tensor
        def _(pe):
            pending = [0]
            lin_last, lin_turns = [1], [0, 0]

            def unit(parts, split):
                n = len(units)
                landed = 16 * len(parts) + (units[n - RING]["landed"] if n >= RING else 0)
                units.append({"parts": parts, "landed": landed})
                if split is None:
                    pending[0] += 1
                else:
                    units[n]["release"] = (S("low_formed"), len(halves) + 2)
                    halves.extend((n, h, split) for h in range(2))
                return n

            def take(*parts):
                n = unit(parts, None)
                pe.wait_ge(S(f"w_landed{n % RING}"), units[n]["landed"])
                return ring[:, n % RING]

            def used(ins):
                n, pending[0] = pending[0], 0
                ins.then_inc(S("w_used"), n)
                value = bump("w_used", n)
                for u in units:
                    if "release" not in u:
                        u["release"] = (S("w_used"), value)
                return S("w_used"), value

            def take_halves(width, *parts):
                first = len(halves)
                unit(parts, width)
                for h in range(2):
                    pe.wait_ge(S("low_formed"), first + h + 1)
                    slot = (first + h) % PARTS
                    yield 2 * h, whi[:, slot], wlo[:, slot]

            def half_used(ins, *names):
                ins.then_inc(S("half_used"), 1)
                value = bump("half_used")
                for name in names:
                    finished(name, (S("half_used"), value))

            def finished(name, event):
                done[name] = event
                halves_at[name] = count.get("half_used", 0), count.get("w_used", 0)

            def wait_read(*names):
                for name in names:
                    pe.wait_ge(*read_of(name))

            def open_tmp(name):
                n = len(turn_tmp)
                turn_tmp[name] = n
                if n >= 2:
                    pe.wait_ge(S(f"tmp_read{n % 2}"), n // 2)
                return tmp_ps[:, 2 * (n % 2):2 * (n % 2) + 2, :]

            def close_tmp(ins, name):
                ins.then_inc(S("tmp_full"), 1)
                finished(name, (S("tmp_full"), bump("tmp_full")))

            def open_lin(name, half=None):
                half = 1 - lin_last[0] if half is None else half
                lin_last[0] = half
                n = lin_turns[half]
                lin_turns[half] += 1
                turn_lin[name] = (half, n)
                if n:
                    pe.wait_ge(S(f"lin_read{half}"), n)
                return lin_ps[:, 2 * half:2 * half + 2, :]

            def product_tok(ps, src, k, i, hi, lo, first, last):
                xh, xl = (v[:, k, i * P:(i + 1) * P] for v in src)
                pe.matmul(ps, xh, hi, start=first, stop=False, skip_group_check=True)
                pe.matmul(ps, xh, lo, start=False, stop=False, skip_group_check=True)
                return pe.matmul(ps, xl, hi, start=False, stop=last, skip_group_check=True)

            def product_feat(ps, src, k, hi, lo, first, last):
                xh, xl = (v[:, k, :] for v in src)
                pe.matmul(ps, hi, xh, start=first, stop=False, skip_group_check=True)
                pe.matmul(ps, hi, xl, start=False, stop=False, skip_group_check=True)
                return pe.matmul(ps, lo, xh, start=False, stop=last, skip_group_check=True)

            def linear_tok(name, w, c0, n, src, kts=KT, k_src=0):
                ps = open_lin(name)
                for k0 in range(0, kts, 4):
                    for r, hi, lo in take_halves(n, (slice(0, n), win(w, c0, n, k0))):
                        for k in range(2):
                            kk = k0 + r + k
                            for i in range(NT):
                                mm = product_tok(ps[:, i, 0:n], src, k_src + kk, i, hi[:, k, 0:n], lo[:, k, 0:n],
                                                 kk == 0, kk == kts - 1)
                        half_used(mm, name)

            def feat_units(name, ps, w, c0, src):
                for k0 in (0, 4):
                    for r, hi, lo in take_halves(HALF, (slice(0, HALF), win(w, c0, HALF, k0))):
                        for k in range(2):
                            kk = k0 + r + k
                            for c in range(4):
                                cols = slice(c * P, (c + 1) * P)
                                mm = product_feat(ps[:, c // 2, (c % 2) * T:(c % 2) * T + T], src, kk,
                                                  hi[:, k, cols], lo[:, k, cols], kk == 0 and c % 2 == 0,
                                                  kk == KT - 1)
                        half_used(mm, name)

            def linear_feat(name, w, c0, src):
                feat_units(name, open_lin(name), w, c0, src)

            def transposes(name, pieces):
                ps = open_tmp(name).rearrange("p a b -> p (a b)")
                for n, piece in enumerate(pieces):
                    mm = pe.transpose(ps[:, n * P:(n + 1) * P], piece, ident[:])
                close_tmp(mm, name)

            def feature_major(name, src, kts=KT):
                for h in range(kts // 4):
                    transposes(f"{name}{h}", [src[:, i, k * P:(k + 1) * P]
                                              for k in range(4 * h, 4 * h + 4) for i in range(NT)])

            def ada(layer, n, half=None):
                name = f"ada{layer}_{n}"
                ps = open_lin(name, half)
                w = I["ada_w_2"][layer]
                if n // 2 in (2, 5):
                    for k0 in (0, 4):
                        slot = take((slice(0, HALF), win(w, n * HALF, HALF, k0)))
                        for k in range(4):
                            mm = pe.matmul(ps[:, 0, :], csb[:, k0 + k, :], slot[:, k, :],
                                           start=(k0 + k == 0), stop=(k0 + k == KT - 1))
                        finished(name, used(mm))
                    return
                for k0 in (0, 4):
                    slot = take((slice(0, HALF), win(w, n * HALF, HALF, k0)))
                    for k in range(4):
                        for c in range(4):
                            mm = pe.matmul(ps[:, 0, c:c + 1], slot[:, k, c * P:(c + 1) * P],
                                           csil[:, k0 + k:k0 + k + 1], start=(k0 + k == 0 and c == 0),
                                           stop=(k0 + k == KT - 1), skip_group_check=True)
                    finished(name, used(mm))

            def attention(name, quads, q, k, v, vw, per, ocols, bufs, fills):
                def scores(n):
                    i, g = quads[n]
                    W = P * (i + 1)
                    ps = open_tmp(f"{name}s{n}")
                    for j in range(2):
                        for a in range(2):
                            mm = pe.matmul(ps[:, a, j * W:(j + 1) * W], q(g, j, a)[:, i * P:(i + 1) * P],
                                           k(g, j, a)[:, 0:W], start=True, stop=True)
                    close_tmp(mm, f"{name}s{n}")

                def turned(n):
                    i, g = quads[n]
                    pe.wait_ge(S(f"{name}prob"), n + 1)
                    transposes(f"{name}p{n}", [bufs[0][n % 2][:, s, b * P:(b + 1) * P]
                                               for s in range(per) for b in range(i + 1)])

                def product(n):
                    i, g = quads[n]
                    wait_read(f"{name}p{n}")
                    if g == 0 and i == 1 and ocols == D:
                        product.ps = open_lin(f"{name}o1", 1 - turn_lin[f"{name}o0"][0])
                    ps = product.ps
                    for s in range(per):
                        head = g * per + (2 * (s % 2) + s // 2 if per == QUAD else s)
                        o = ps[:, i, head * vw:(head + 1) * vw] if ocols == HALF else \
                            ps.rearrange("p a b -> p (a b)")[:, head * vw:(head + 1) * vw]
                        for b in range(i + 1):
                            blk = s * (i + 1) + b
                            mm = pe.matmul(o, bufs[1][n % 2][:, blk * P:(blk + 1) * P], v(b, head),
                                           start=(b == 0), stop=(b == i))
                    mm.then_inc(S("att_pv"), 1)
                    event = (S("att_pv"), bump("att_pv"))
                    finished(f"{name}o{i}", event)
                    finished(f"{name}pv{n}", event)

                product.ps = open_lin(f"{name}o0")
                for n in range(len(quads) + 2):
                    if n < len(quads):
                        scores(n)
                    for layer, m in fills.get(n, ()):
                        ada(layer, m, 1 - turn_lin[f"{name}o0"][0])
                    if 1 <= n <= len(quads):
                        turned(n - 1)
                    if n >= 2:
                        product(n - 2)

            pe.wait_ge(S("ident"), 1)
            pe.wait_ge(S("small_landed"), 16 * 8)
            ps = open_tmp("cols")
            pe.transpose(ps[:, 0, 0:P], stackA[:], ident[:])
            close_tmp(pe.transpose(ps[:, 0, P:P + 5], stackB[:], ident[0:5, 0:5]), "cols")
            ps = open_tmp("relvec")
            pe.wait_ge(S("rel_landed"), 32)
            close_tmp(pe.matmul(ps[0:16, 0, 0:DIST], relT[:], onehot[:], start=True, stop=True), "relvec")

            def fill(*chunks):
                for layer, m in chunks:
                    ada(layer, m)

            pe.wait_ge(S("cond_ready"), 1)
            quads_a = [(i, g) for i in range(NT) for g in range(2)]
            for L in range(2):
                w = I["w_in"][L]
                fill(*ADA_START[L])
                pe.wait_ge(S("f_scaled"), L + 1)
                feature_major(f"f{L}hT", hs)
                wait_read(f"f{L}hT0", f"f{L}hT1")
                linear_feat(f"f{L}f", w, F0, hT)
                linear_feat(f"f{L}qh", w, QH0, hT)
                linear_tok(f"f{L}kv", w, K0, 256, hT)
                linear_tok(f"f{L}q", w, Q0, HALF, hT)
                linear_tok(f"f{L}i", w, I0, HALF, hT)
                pe.wait_ge(S("f_rope"), L + 1)
                transposes(f"f{L}kT", [kdup[:, i, g].rearrange("p a d -> p (a d)") for g in range(2) for i in range(NT)])
                linear_tok(f"f{L}z", w, Z0, HALF, hT)
                linear_tok(f"f{L}g", w, G0, HALF, hT)
                for lv in range(LEVELS + 1):
                    name = f"f{L}lv{lv}"
                    ps = open_tmp(name).rearrange("p a b -> p (a b)")
                    pe.wait_ge(S("level_ready"), (LEVELS + 1) * L + lv + 1)
                    left, right = (kin, qin) if lv == 0 else (decay[lv % 2], decay[lv % 2])
                    for n in range(4 if lv == LEVELS else 8):
                        if lv == LEVELS:
                            a, b = left[:, n, 0:P], right[:, n, P:T]
                        else:
                            cut = slice((n % 2) * P, (n % 2) * P + P)
                            a, b = left[:, n // 2, cut], right[:, n // 2, cut]
                        mm = pe.matmul(ps[:, n * P:(n + 1) * P], a, b, start=True, stop=True)
                    close_tmp(mm, name)
                    if lv in (2, 4, 6, 7):
                        c = {2: (GA0, "ga0"), 4: (GA0 + HALF, "ga1"), 6: (GH0, "gh0"), 7: (GH0 + HALF, "gh1")}[lv]
                        linear_tok(f"f{L}{c[1]}", w, c[0], HALF, hT)
                transposes(f"f{L}qT", [qkv[:, i, k * P:(k + 1) * P] for k in range(4) for i in range(NT)])
                ps = open_lin(f"f{L}ho")
                wait_read(f"f{L}lv{LEVELS - 1}", f"f{L}lv{LEVELS}")
                for h in range(4):
                    cols = slice(h * P, (h + 1) * P)
                    pe.matmul(ps[:, 0, cols], scor[:, 2 * h, :], vh[:, 0, cols], start=True, stop=True)
                    pe.matmul(ps[:, 1, cols], cross[:, h, :], vh[:, 0, cols], start=True, stop=False)
                    mm = pe.matmul(ps[:, 1, cols], scor[:, 2 * h + 1, :], vh[:, 1, cols], start=False, stop=True)
                mm.then_inc(S("hgrn_out"), 1)
                finished(f"f{L}ho", (S("hgrn_out"), bump("hgrn_out")))
                wait_read(f"f{L}kT", f"f{L}qT")
                attention(f"f{L}a", quads_a,
                          lambda g, j, a: qTa[a * HD:(a + 1) * HD, 2 * g + j, :],
                          lambda g, j, a: kTd[a * HD:(a + 1) * HD, g, :],
                          lambda b, head: qkv[:, b, 640 + (head // 4) * HD:640 + (head // 4 + 1) * HD],
                          HD, QUAD, HALF, (Pq_first, pT_first), ADA_WINDOW[L])
                fill(*ADA_GATED[L])
                pe.wait_ge(S("f_b"), L + 1)
                feature_major(f"f{L}bT", hs[:, :, HALF:D], 4)
                pe.wait_ge(S("f_a"), L + 1)
                feature_major(f"f{L}aT", hs[:, :, 0:HALF], 4)
                wait_read(f"f{L}bT0", f"f{L}aT0")
                for c in range(2):
                    linear_tok(f"f{L}ua{c}", I["w_up_attn"][L], c * HALF, HALF, hT, kts=4)
                    linear_tok(f"f{L}uh{c}", I["w_up_hgrn"][L], c * HALF, HALF, hT, kts=4, k_src=4)
                fill(*ADA_MERGE[L])
                pe.wait_ge(S("f_merged"), L + 1)
                feature_major(f"f{L}mT", hs)
                wait_read(f"f{L}mT0", f"f{L}mT1")
                for c in range(2):
                    linear_tok(f"f{L}out{c}", I["w_out"][L], c * HALF, HALF, hT)

            def mixed(name):
                pe.wait_ge(S(f"{name}x"), 1)
                feature_major(f"{name}hT", x)
                pe.wait_ge(S("mixed_low"), bump("mixed", 2))

            def project(name, w):
                feature_major(f"{name}oT", hs)
                wait_read(f"{name}oT0", f"{name}oT1")
                for c in range(2):
                    linear_tok(f"{name}y{c}", w, c * HALF, HALF, hT)

            def mlp(name, w1, w2):
                mixed(name)
                groups = 8
                ys = None
                for g in range(groups + 1):
                    if g < groups:
                        feat_units(f"{name}u{g}", open_tmp(f"{name}u{g}"), w1, g * HALF, hT)
                    if g == 1:
                        ys = [open_lin(f"{name}y{c}") for c in range(2)]
                    if g >= 1:
                        pe.wait_ge(S(f"{name}act"), g)
                        b = (g - 1) % 2
                        for c in range(2):
                            for r, hi, lo in take_halves(HALF, (slice(0, HALF), win(w2, c * HALF, HALF, 4 * (g - 1)))):
                                for k in range(2):
                                    for i in range(NT):
                                        mm = product_tok(ys[c][:, i, :], (hbhi[:, b], hblo[:, b]), r + k, i,
                                                         hi[:, k, :], lo[:, k, :], g == 1 and r + k == 0,
                                                         g == groups and r + k == 3)
                                half_used(mm, f"{name}y{c}", f"{name}hb{g - 1}")

            quads_16 = [(i, g) for i in range(NT) for g in range(4)]

            w = I["a_w_in_2"][0]
            mixed("s0")
            ps = open_lin("s0misc")
            psk = open_tmp("s0ik")
            for k0 in (0, 4):
                for r, hi, lo in take_halves(392, (slice(0, T), win(w, 1024, T, k0)),
                                             (slice(T, T + 8), win(w, 1856, 8, k0)),
                                             (slice(264, 328), win(w, 1792, HD, k0)),
                                             (slice(328, 392), win(w, 1792, HD, k0))):
                    for k in range(2):
                        kk = k0 + r + k
                        for i in range(NT):
                            product_tok(ps[:, i, 0:T + 8], hT, kk, i, hi[:, k, 0:T + 8], lo[:, k, 0:T + 8],
                                        kk == 0, kk == KT - 1)
                        mm = product_feat(psk[:, 0, 0:T], hT, kk, hi[:, k, 264:392], lo[:, k, 264:392],
                                          kk == 0, kk == KT - 1)
                    half_used(mm, "s0misc", "s0ik")
            linear_feat("s0iq", w, 1280, hT)
            wait_read("s0ik", "s0iq")
            for i in range(NT):
                for g in range(2):
                    W = P * (i + 1)
                    ps = open_tmp(f"s0idx{i}{g}")
                    for j in range(2):
                        for a in range(2):
                            rows = slice(a * HD, (a + 1) * HD)
                            mm = pe.matmul(ps[:, a, j * W:(j + 1) * W], iqT[rows, 2 * g + j, i * P:(i + 1) * P],
                                           ikT[rows, 0:W], start=True, stop=True)
                    close_tmp(mm, f"s0idx{i}{g}")
                if i == 0:
                    linear_feat("s0q0", w, 0, hT)
            linear_feat("s0q1", w, HALF, hT)
            pe.wait_ge(S("s0ckvn"), 1)
            transposes("s0ckvT", [ckv[:, i, r * P:(r + 1) * P] for r in range(2) for i in range(NT)])
            slot = take((slice(0, HALF), I["a_w_uk_2"][0].rearrange("h d r -> (h d) r").rearrange(
                "(k p) r -> p k r", p=P)))
            uk = slot.rearrange("p a b -> p (a b)").rearrange("p (k r) -> p k r", k=KT)
            for r in range(2):
                ps = open_tmp(f"s0wuk{r}").rearrange("p a b -> p (a b)")
                for k in range(KT):
                    mm = pe.transpose(ps[:, k * P:(k + 1) * P], uk[:, k, r * P:(r + 1) * P], ident[:])
                close_tmp(mm, f"s0wuk{r}")
            wait_read("s0ckvT")
            slot = take((0, "wuv"), (1, "wuv"))
            uv = slot.rearrange("p a b -> p (a b)").rearrange("p (r n) -> p r n", r=2)
            for i in range(NT):
                ps = open_lin(f"s0v{i}")
                for c in range(2):
                    for r in range(2):
                        mm = pe.matmul(ps[:, c, :], ckvT[:, r, i * P:(i + 1) * P], uv[:, r, c * HALF:(c + 1) * HALF],
                                       start=(r == 0), stop=(r == 1))
                if i == 0:
                    mm.then_inc(S("s0v0_full"), 1)
                    finished("s0v0", (S("s0v0_full"), 1))
                else:
                    finished("s0v1", used(mm))
            wait_read("s0wuk0", "s0wuk1")
            for h in range(2):
                ps = open_tmp(f"s0k{h}")
                for c in range(4):
                    for r in range(2):
                        mm = pe.matmul(ps[:, c // 2, (c % 2) * T:(c % 2) * T + T],
                                       wukT[:, r, (4 * h + c) * P:(4 * h + c + 1) * P], ckvT[:, r, :],
                                       start=(r == 0), stop=(r == 1))
                close_tmp(mm, f"s0k{h}")
            wait_read("s0q0", "s0q1", "s0k0", "s0k1", "s0v0", "s0v1")
            heads = (lambda t: lambda g, j, a: t[a * HD:(a + 1) * HD, 2 * g + j, :])
            attention("s0", quads_16, heads(qT), heads(kT),
                      lambda b, head: vv[:, b, head * HD:(head + 1) * HD], HD, QUAD, D,
                      (Pq_second, pT_second), ADA_SPARSE)
            wait_read("s0o0", "s0o1")
            project("s0", I["a_w_o_2"][0])
            mlp("s1", I["mlp_w1_2"][0], I["mlp_w2_2"][0])

            w = I["b_w_in_2"][0]
            mixed("s2")
            for n in range(2):
                linear_feat(f"s2q{n}", w, n * HALF, hT)
                linear_feat(f"s2k{n}", w, D + n * HALF, hT)
            for n in range(2):
                linear_tok(f"s2v{n}", w, 2 * D + n * HALF, HALF, hT)
            wait_read(*(f"s2{part}{n}" for part in "qkv" for n in range(2)))
            attention("s2", quads_16, heads(qT), heads(kT),
                      lambda b, head: vv[:, b, head * P:(head + 1) * P], P, 2, D,
                      (Pq_second, pT_second), ADA_DIFF)
            pe.wait_ge(S("s2o"), 1)
            project("s2", I["b_w_o_2"][0])
            mlp("s3", I["mlp_w1_2"][1], I["mlp_w2_2"][1])

        def full_tmp_of(eng, name):
            eng.wait_ge(*done[name])
            n = turn_tmp[name]
            return tmp_ps[:, 2 * (n % 2):2 * (n % 2) + 2, :]

        def full_lin_of(eng, name):
            eng.wait_ge(*done[name])
            half = turn_lin[name][0]
            return lin_ps[:, 2 * half:2 * half + 2, :]

        def read(ins, name):
            ins.then_inc(read_of(name)[0], 1)

        def flat(v):
            return v.rearrange("p a b -> p (a b)")

        @block.sync
        def _(sp):
            for n, unit in enumerate(units):
                if n >= RING:
                    sp.wait_ge(*units[n - RING]["release"])
                slot = ring[:, n % RING]
                for cols, src in unit["parts"]:
                    if isinstance(src, str):
                        r = cols
                        dst = slot.rearrange("p a b -> p (a b)")[:, r * D:(r + 1) * D].rearrange(
                            "p (h d) -> p h d", h=16)
                        sp.dma_start(dst, I["a_w_uv_2"][0, :, r * P:(r + 1) * P, :].rearrange(
                            "h p d -> p h d")).then_inc(S(f"w_landed{n % RING}"), 16)
                    elif src.shape[1] == KT:
                        sp.dma_start(slot.rearrange("p a b -> p (a b)").rearrange("p (k r) -> p k r", k=KT),
                                     src).then_inc(S(f"w_landed{n % RING}"), 16)
                    else:
                        sp.dma_start(slot[:, :, cols], src).then_inc(S(f"w_landed{n % RING}"), 16)
            sp.wait_ge(S("s4x"), 1)
            sp.dma_start(out.rearrange("b (i p) d -> p (b i) d", p=P), x[:]).then_inc(S("out_written"), 16)
            sp.wait_ge(S("out_written"), 16)

        @block.gpsimd
        def _(pool):
            def step(ins):
                ins.then_inc(S("pool_step"), 1)
                pool.wait_ge(S("pool_step"), bump("pool_step"))

            step(pool.memset(ident[:], 0.0))
            pool.affine_select(out=ident[:], in_=ident[:], compare_op=ALU.not_equal, fill=1.0, base=0,
                               pattern=[[-1, P]], channel_multiplier=1).then_inc(S("ident"), 1)
            step(pool.memset(band[:], 0.0))
            step(pool.affine_select(out=band[:, 0:P], in_=band[:, 0:P], compare_op=ALU.is_gt, fill=NEG, base=0,
                                    pattern=[[1, P]], channel_multiplier=-1))
            pool.affine_select(out=band[:, P:T], in_=band[:, P:T], compare_op=ALU.is_ge, fill=NEG, base=0,
                               pattern=[[-1, P]], channel_multiplier=1).then_inc(S("band"), 1)
            step(pool.iota(pairx[:, 0, :], pattern=[[0, P]], base=0, channel_multiplier=1))
            pool.iota(pairx[:, 1, :], pattern=[[1, P]], base=0, channel_multiplier=0).then_inc(S("pairs"), 1)
            step(pool.memset(chunkmask[:], 1.0))
            pool.memset(chunkmask[:].rearrange("p (c t) -> p c t", t=CHUNK)[:, :, 0:1], 0.0).then_inc(S("chunkmask"), 1)
            for j in range(ROPE_HALF):
                ins = pool.memset(invf[:, j:j + 1], float(np.float32(500000.0) ** np.float32(-j * 0.125)))
            ins.then_inc(S("invf"), 1)
            pool.memset(relT[:], 1.0).then_inc(S("relT_ones"), 1)
            pool.wait_ge(S("levels_both"), 1)
            pool.affine_select(out=levelmask[:, 1:, :], in_=levelmask[:, 1:, :], compare_op=ALU.is_gt, fill=0.0,
                               base=0, pattern=[[0, LEVELS - 1], [1, P]], channel_multiplier=-1
                               ).then_inc(S("levels"), 1)
            for n, (u, h, width) in enumerate(halves):
                pool.wait_ge(S("high_formed"), n + 1)
                pool.tensor_tensor(wlo[:, n % PARTS, :, 0:width], ring[:, u % RING, 2 * h:2 * h + 2, 0:width],
                                   whi[:, n % PARTS, :, 0:width].bitcast(F32), ALU.subtract
                                   ).then_inc(S("low_formed"), 1)

        @block.scalar
        def _(act):
            def step(ins):
                ins.then_inc(S("act_step"), 1)
                act.wait_ge(S("act_step"), bump("act_step"))

            act.dma_start(x[:], I["x"].rearrange("b (i p) d -> p (b i) d", p=P)).then_inc(S("x_landed"), 16)
            rows = 0
            for v in (I["norm_w"].rearrange("l (k p) -> (l k) p", p=P),
                      I["lb_logits"].rearrange("l (k p) -> (l k) p", p=P),
                      I["ada_b_2"].rearrange("l (k p) -> (l k) p", p=P),
                      I["c_2"].rearrange("b (k p) -> (b k) p", p=P)):
                act.dma_start(stackA[rows:rows + v.shape[0], :], v).then_inc(S("small_landed"), 16)
                rows += v.shape[0]
            rows = 0
            for v in (I["a_kv_norm_2"].rearrange("l (k p) -> (l k) p", p=P), I["b_subln_2"], I["hgrn_norm_w"]):
                act.dma_start(stackB[rows:rows + v.shape[0], :], v).then_inc(S("small_landed"), 16)
                rows += v.shape[0]
            act.dma_start(posi[:], I["positions"].rearrange("b (i p) -> p (b i)", p=P),
                          allow_slow_non_contiguous=True).then_inc(S("small_landed"), 16)
            act.dma_start(sinks[:], I["attn_sinks"].rearrange("l h -> (l h)").partition_broadcast(P)
                          ).then_inc(S("sinks_landed"), 16)
            act.dma_start(lamb[:].rearrange("p a d -> p (a d)"),
                          I["b_lambda_2"].rearrange("l a d -> (l a d)").partition_broadcast(P)
                          ).then_inc(S("lamb_landed"), 16)

            def gate_bias(layer, j):
                section = (2, 5)[j]
                act.dma_start(gmod[:, j, :], I["ada_b_2"][layer, section * D:(section + 1) * D].partition_broadcast(P)
                              ).then_inc(S(f"gbias_landed{j}"), 16)

            formed = [0]

            def high_parts(end, plain):
                for n in range(formed[0], min(end, len(halves))):
                    u, h, width = halves[n]
                    if any(event[0] is S("w_used") and event[1] > plain
                           for event in (v["release"] for v in units[max(0, u - 2 * RING):max(0, u - RING + 1)])):
                        return
                    act.wait_ge(S(f"w_landed{u % RING}"), units[u]["landed"])
                    if n >= PARTS:
                        act.wait_ge(S("half_used"), n - PARTS + 1)
                    act.copy(whi[:, n % PARTS, :, 0:width], ring[:, u % RING, 2 * h:2 * h + 2, 0:width]
                             ).then_inc(S("high_formed"), 1)
                    formed[0] = n + 1

            def ahead(name):
                high_parts(halves_at[name][0] + PARTS, halves_at[name][1])

            def full_tmp(name):
                ahead(name)
                return full_tmp_of(act, name)

            def full_lin(name):
                ahead(name)
                return full_lin_of(act, name)

            def high_of(name, k0, cols=None):
                ps = flat(full_tmp(name))
                if cols is None:
                    ins = act.copy(flat(hThi[:, k0:k0 + 4, :]), ps)
                elif isinstance(cols, list):
                    for k, col in enumerate(cols):
                        ins = act.activation(hThi[:, k0 + k, :], ps[:, k * T:(k + 1) * T], ACT.Copy, scale=col)
                else:
                    ins = act.activation(flat(hThi[:, k0:k0 + 4, :]), ps, ACT.Copy, scale=cols)
                ins.then_inc(S("operand_high"), 1)

            def squares(name, ready, after=None):
                if after:
                    ahead(after)
                act.wait_ge(*ready)
                for i in range(NT):
                    ins = act.activation(hs[:, i, :], x[:, i, :], ACT.Square, accum_out=st[:, 0, i, 0:1])
                ins.then_inc(S(f"{name}ss"), 1)

            def rough_rsqrt(name, v, y, after=None):
                if after:
                    ahead(after)
                act.wait_ge(S(f"{name}var"), 1)
                step(act.activation(y, v, ACT.Ln))
                act.activation(y, y, ACT.Exp, scale=-0.5).then_inc(S(f"{name}rough"), 1)

            def exps(name, n, W, Pq):
                ahead(f"{name}s{n}")
                act.wait_ge(S(f"{name}max"), n + 1)
                for s in range(QUAD):
                    ins = act.activation(Pq[n % 2][:, s, 0:W], Pq[n % 2][:, s, 0:W], ACT.Exp,
                                         bias=qst[:, n, 1, s:s + 1], accum_out=qst[:, n, 2, s:s + 1])
                return ins

            def attention(name, quads, per, bufs, sink=False):
                Pq, pT = bufs
                for n in range(len(quads) + 1):
                    if n < len(quads):
                        ins = exps(name, n, P * (quads[n][0] + 1), Pq)
                        if sink:
                            ins = act.activation(qst[:, n, 3, :], qst[:, n, 4, :], ACT.Exp)
                        ins.then_inc(S(f"{name}exp"), 1)
                    if n >= 1:
                        m = n - 1
                        ps = full_tmp(f"{name}p{m}")
                        if m >= 2:
                            act.wait_ge(*done[f"{name}pv{m - 2}"])
                        w = per * (quads[m][0] + 1) * P
                        read(act.copy(pT[m % 2][:, 0:w], flat(ps)[:, 0:w]), f"{name}p{m}")

            act.wait_ge(S("relT_ones"), 1)
            act.dma_start(relT[0:NBUCKET, :], I["rel_bias_2"]).then_inc(S("rel_landed"), 16)
            act.dma_start(onehot, I["onehot"]).then_inc(S("rel_landed"), 16)
            act.dma_start(lnp[:, 0, :], I["final_norm_w"].partition_broadcast(P)).then_inc(S("lnp_landed"), 32)
            act.wait_ge(*read_of("cols"))
            act.activation(csil[:], colA[:, 120:128], ACT.Silu).then_inc(S("csil"), 1)
            act.wait_ge(S("angles"), 1)
            act.activation(trig[:], ang[:], ACT.Sin).then_inc(S("trig"), 1)
            act.wait_ge(S("lb_max"), 1)
            act.activation(lbw[:, 0:2, :], lbw[:, 0:2, :], ACT.Exp).then_inc(S("lb_exp"), 1)
            act.wait_ge(S("lam_dots"), 1)
            act.activation(lams[:, 0:2], lams[:, 0:2], ACT.Exp).then_inc(S("lam_exp"), 1)

            act.wait_ge(*read_of("relvec"))
            act.dma_start(scratch, relvec).then_inc(S("scratch_written"), 16)
            for L in range(2):
                if L == 0:
                    for j in range(2):
                        gate_bias(0, j)
                    squares("f0", (S("x_landed"), 16))
                else:
                    squares("f1", read_of("f0out1"), "f0out1")
                rough_rsqrt(f"f{L}", st[:, 1, :, 0], st[:, 2, :, 0])
                for h in range(2):
                    high_of(f"f{L}hT{h}", 4 * h, [colA[:, 8 * L + k:8 * L + k + 1] for k in range(4 * h, 4 * h + 4)])
                ahead(f"f{L}f")
                act.wait_ge(*read_of(f"f{L}f"))
                act.activation(gate_p[:], gate_min[:], ACT.Exp)
                act.activation(gate_n[:], gate_max[:], ACT.Exp, scale=-1.0).then_inc(S("f_pn"), 1)
                act.wait_ge(S("f_sum"), L + 1)
                ins = act.activation(gate_lnsum[:], gate_lnsum[:], ACT.Ln)
                if L == 1:
                    ins = act.activation(gate_p[:], gate_p[:], ACT.Ln)
                ins.then_inc(S("f_ln"), 1)
                act.wait_ge(S("f_kexp"), L + 1)
                act.activation(kin[:], gate_max[:], ACT.Exp, scale=-1.0).then_inc(S("f_kin"), 1)
                ps = full_lin(f"f{L}qh")
                read(act.activation(flat(qin), flat(ps), ACT.Silu), f"f{L}qh")
                ps = full_lin(f"f{L}kv")
                read(act.copy(qkv[:, :, K0:K0 + 256], ps[:, :, 0:256]), f"f{L}kv")
                ps = full_lin(f"f{L}q")
                read(act.mul(qkv[:, :, 0:HALF], ps, HD ** -0.5), f"f{L}q")
                ps = full_lin(f"f{L}i")
                read(act.copy(vh[:], ps), f"f{L}i")
                ps = full_lin(f"f{L}z")
                read(act.activation(zs[:], ps, ACT.Silu), f"f{L}z")
                ps = full_lin(f"f{L}g")
                read(act.activation(zg[:], ps, ACT.Silu), f"f{L}g")
                for lv in range(1, LEVELS + 1):
                    if lv >= 3:
                        ahead(f"f{L}lv{lv - 2}")
                    act.wait_ge(S("level_diff"), LEVELS * L + lv)
                    act.activation(decay[lv % 2][:], decay[lv % 2][:], ACT.Exp).then_inc(S("level_exp"), 1)
                    if L == 0 and lv == 3:
                        act.wait_ge(S("scratch_written"), 16)
                    if lv in (3, 5, 7, 8):
                        g, c = {3: (ga, "ga0"), 5: (ga, "ga1"), 7: (gh, "gh0"), 8: (gh, "gh1")}[lv]
                        ps = full_lin(f"f{L}{c}")
                        half = slice(0, HALF) if c[-1] == "0" else slice(HALF, D)
                        read(act.activation(g[:, :, half], ps, ACT.Sigmoid), f"f{L}{c}")
                name = f"f{L}lv{LEVELS}"
                ps = full_tmp(name)
                read(act.copy(flat(cross), flat(ps)[:, 0:HALF]), name)
                ps = full_tmp(f"f{L}qT")
                act.wait_ge(S("level_ready"), (LEVELS + 1) * (L + 1))
                read(act.copy(flat(qTa), flat(ps)), f"f{L}qT")
                ps = full_lin(f"f{L}ho")
                act.activation(hs[:, :, 0:HALF], ps, ACT.Square).then_inc(S("f_hsq"), 1)
                rough_rsqrt(f"f{L}h", st[:, 1], st[:, 2])
                attention(f"f{L}a", [(i, g) for i in range(NT) for g in range(2)], QUAD,
                          (Pq_first, pT_first), sink=True)
                high_of(f"f{L}bT0", 4, colB[:, 3 + L:4 + L])
                high_of(f"f{L}aT0", 0)
                for h in range(2):
                    high_of(f"f{L}mT{h}", 4 * h)

            squares("n", read_of("f1out1"), "f1out1")
            act.wait_ge(S("scratch_written"), 16)
            act.dma_start(Mbias, bass.AP(scratch.tensor, 0, [[1, P], [DIST, 16], [1, T]])).then_inc(S("Mbias"), 16)
            rough_rsqrt("n", st[:, 1, :, 0], st[:, 2, :, 0])

            def mixed(name, layer, j):
                for h in range(2):
                    ps = flat(full_tmp(f"{name}hT{h}"))
                    act.wait_ge(*read_of(f"ada{layer}_{(3, 9)[j]}"))
                    for k in range(4):
                        kk = 4 * h + k
                        ins = act.activation(flat(hs)[:, kk * T:(kk + 1) * T], ps[:, k * T:(k + 1) * T], ACT.Identity,
                                             bias=modc[:, layer, 2 * j, kk:kk + 1],
                                             scale=modc[:, layer, 2 * j + 1, kk:kk + 1])
                    read(ins, f"{name}hT{h}")

            def norm_weights(n):
                for k, v in enumerate((I["ln_g_2"], I["ln_b_2"])):
                    act.dma_start(lnp[:, k, :], v[n // 2, n % 2].partition_broadcast(P)
                                  ).then_inc(S("lnp_landed"), 16)

            def mlp(name, layer):
                mixed(name, layer, 1)
                norm_weights(2 * layer + 1)
                if layer == 0:
                    gate_bias(1, 0)
                for g in range(8):
                    ps = full_tmp(f"{name}u{g}")
                    if g >= 2:
                        act.wait_ge(S(f"{name}act"), g - 1)
                    read(act.activation(flat(hidden[g % 2]), flat(ps), ACT.Relu), f"{name}u{g}")
                rough_rsqrt(f"{name}ln", mv[:, :, 1], st[:, 2, :, 0], f"{name}y1")

            mixed("s0", 0, 0)
            norm_weights(0)
            ps = full_tmp("s0ik")
            read(act.copy(ikT[:], ps[:, 0, 0:T]), "s0ik")
            ps = full_lin("s0misc")
            act.copy(ckv[:], ps[:, :, 0:T]).then_inc(S("s0ckv"), 1)
            read(act.mul(iw[:], ps[:, :, T:T + 8], 8 ** -0.5 * HD ** -0.5), "s0misc")
            act.wait_ge(S("s0ckv"), 1)
            for i in range(NT):
                ins = act.activation(hs[:, i, 0:T], ckv[:, i, :], ACT.Square, accum_out=st[:, 0, i, 0:1])
            ins.then_inc(S("s0css"), 1)
            rough_rsqrt("s0c", st[:, 1, :, 0], st[:, 2, :, 0])
            ps = full_lin("s0iq")
            read(act.copy(flat(iqT), flat(ps)), "s0iq")
            for i in range(NT):
                for g in range(2):
                    n = 2 * i + g
                    W = P * (i + 1)
                    ps = full_tmp(f"s0idx{i}{g}")
                    if n >= 2:
                        act.wait_ge(S("s0idx_used"), n - 1)
                    for a in range(2):
                        ins = act.activation(Pq_second[n % 2][:, 2 * a:2 * a + 2, 0:W],
                                             ps[:, a, 0:2 * W].rearrange("p (j w) -> p j w", j=2), ACT.Relu)
                    read(ins, f"s0idx{i}{g}")
                if i == 0:
                    ps = full_lin("s0q0")
                    read(act.mul(flat(qT[:, 0:4, :]), flat(ps), HD ** -0.5), "s0q0")
            ps = full_lin("s0q1")
            read(act.mul(flat(qT[:, 4:8, :]), flat(ps), HD ** -0.5), "s0q1")
            for r in range(2):
                ps = full_tmp(f"s0wuk{r}")
                read(act.copy(wukT[:, r, :], flat(ps)), f"s0wuk{r}")
            for i in range(NT):
                ps = full_lin(f"s0v{i}")
                read(act.copy(vv[:, i, :], flat(ps)), f"s0v{i}")
            for h in range(2):
                ps = full_tmp(f"s0k{h}")
                read(act.copy(flat(kT[:, 4 * h:4 * h + 4, :]), flat(ps)), f"s0k{h}")
            quads = [(i, g) for i in range(NT) for g in range(4)]
            attention("s0", quads, QUAD, (Pq_second, pT_second))
            for h in range(2):
                high_of(f"s0oT{h}", 4 * h)
            rough_rsqrt("s0ln", mv[:, :, 1], st[:, 2, :, 0], "s0y1")
            mlp("s1", 0)
            mixed("s2", 1, 0)
            norm_weights(2)
            gate_bias(1, 1)
            for n in range(2):
                for part, dst, scale in (("q", qT, HD ** -0.5), ("k", kT, 1.0)):
                    ps = full_lin(f"s2{part}{n}")
                    read(act.mul(flat(dst[:, 4 * n:4 * n + 4, :]), flat(ps), scale), f"s2{part}{n}")
            for n in range(2):
                ps = full_lin(f"s2v{n}")
                read(act.copy(vv[:, :, n * HALF:(n + 1) * HALF], ps), f"s2v{n}")
            attention("s2", quads, 2, (Pq_second, pT_second))
            for i in range(NT):
                ahead(f"s2o{i}")
                act.wait_ge(*read_of(f"s2o{i}"))
                ins = act.activation(osq[:, i, :], hs[:, i, :], ACT.Square)
            ins.then_inc(S("s2osq"), 1)
            rough_rsqrt("s2h", st[:, 1], st[:, 2])
            for h in range(2):
                high_of(f"s2oT{h}", 4 * h, lams[:, 4:5])
            rough_rsqrt("s2ln", mv[:, :, 1], st[:, 2, :, 0], "s2y1")
            mlp("s3", 1)

        @block.vector
        def _(dve):
            def step(ins):
                ins.then_inc(S("dve_step"), 1)
                dve.wait_ge(S("dve_step"), bump("dve_step"))

            def rsqrt(name, v, y, w):
                dve.wait_ge(S(f"{name}rough"), 1)
                step(dve.tensor_tensor(w, y, y, ALU.mult))
                step(dve.tensor_tensor(w, w, v, ALU.mult))
                step(dve.tensor_scalar(w, w, -0.5, 1.5, ALU.mult, ALU.add))
                step(dve.tensor_tensor(y, y, w, ALU.mult))

            def variance(name, ss, v, n, eps):
                dve.wait_ge(S(f"{name}ss"), 1)
                dve.tensor_scalar(v, ss, 1.0 / n, eps, ALU.mult, ALU.add).then_inc(S(f"{name}var"), 1)

            def low_of(name, k0, cols=None):
                ps = flat(full_tmp_of(dve, name))
                dve.wait_ge(S("operand_high"), bump("operand_low"))
                hi, lo = hThi[:].bitcast(F32), hTlo
                if cols is None:
                    ins = dve.tensor_tensor(flat(lo[:, k0:k0 + 4, :]), ps, flat(hi[:, k0:k0 + 4, :]), ALU.subtract)
                elif isinstance(cols, list):
                    for k, col in enumerate(cols):
                        ins = dve.scalar_tensor_tensor(lo[:, k0 + k, :], ps[:, k * T:(k + 1) * T], col,
                                                       hi[:, k0 + k, :], ALU.mult, ALU.subtract)
                else:
                    ins = dve.scalar_tensor_tensor(flat(lo[:, k0:k0 + 4, :]), ps, cols, flat(hi[:, k0:k0 + 4, :]),
                                                   ALU.mult, ALU.subtract)
                read(ins, name)

            dve.wait_ge(S("pairs"), 1)
            step(dve.tensor_tensor(pairx[:, 0, :], pairx[:, 0, :], pairx[:, 1, :], ALU.bitwise_xor))
            step(dve.tensor_copy(levelge[:, 0, :], pairx[:, 0, :]))
            for lv in range(1, LEVELS):
                dve.tensor_scalar(levelge[:, lv, :], levelge[:, 0, :], float(2 ** (lv - 1)), None, ALU.is_ge)
            step(dve.memset(levelge[:, LEVELS, :], 0.0))
            dve.tensor_scalar(levelmask[:, 0, :], levelge[:, 0, :], 0.0, None, ALU.is_equal)
            dve.tensor_tensor(levelmask[:, 1:, :], levelge[:, 1:LEVELS, :], levelge[:, 2:, :], ALU.subtract
                              ).then_inc(S("levels_both"), 1)
            ps = full_tmp_of(dve, "cols")
            dve.tensor_copy(colA[:], ps[:, 0, 0:P])
            read(dve.tensor_copy(colB[:], ps[:, 0, P:P + 5]), "cols")
            ps = full_tmp_of(dve, "relvec")
            read(dve.tensor_copy(relvec, ps[0:16, 0, 0:DIST]), "relvec")
            dve.wait_ge(S("small_landed"), 16 * 8)
            dve.wait_ge(S("invf"), 1)
            step(dve.tensor_copy(posf[:], posi[:]))
            for i in range(NT):
                for c in range(2):
                    ins = dve.tensor_scalar(ang[:, i, c, :], invf[:], posf[:, i:i + 1], None, ALU.mult)
            step(ins)
            for c in range(2):
                ins = dve.tensor_scalar(angk[:, :, c, :], ang[:, :, c, :], 1.0 / TURN, 0.25 * c, ALU.mult, ALU.add)
            step(ins)
            step(dve.tensor_scalar(angk[:], angk[:], ROUNDER, None, ALU.add))
            step(dve.tensor_scalar(angk[:], angk[:], -ROUNDER, None, ALU.add))
            for part in TURN_PARTS:
                step(dve.scalar_tensor_tensor(ang[:], angk[:], -part, ang[:], ALU.mult, ALU.add))
            step(dve.tensor_scalar(ang[:, :, 1, :], ang[:, :, 1, :], TURN / 4, None, ALU.add))
            dve.tensor_scalar(ang[:], ang[:], SIN_MAX, -SIN_MAX, ALU.min, ALU.max).then_inc(S("angles"), 1)
            step(dve.tensor_copy(lbw[:, 0:2, :], colA[:, 16:24].rearrange("p (l h) -> p l h", l=2)))
            step(dve.tensor_tensor(lbw[:, 2, :], lbw[:, 0, :], lbw[:, 1, :], ALU.max))
            dve.tensor_tensor(lbw[:, 0:2, :], lbw[:, 0:2, :], lbw[:, 2, :].unsqueeze(1).broadcast_to([P, 2, 4]),
                              ALU.subtract).then_inc(S("lb_max"), 1)
            dve.wait_ge(S("lb_exp"), 1)
            step(dve.tensor_tensor(lbw[:, 2, :], lbw[:, 0, :], lbw[:, 1, :], ALU.add))
            step(dve.reciprocal(lbw[:, 2, :], lbw[:, 2, :]))
            step(dve.tensor_tensor(lbw[:, 0:2, :], lbw[:, 0:2, :], lbw[:, 2, :].unsqueeze(1).broadcast_to([P, 2, 4]),
                                   ALU.mult))
            step(dve.tensor_tensor(lbw[:, 3, :], lbw[:, 0, :], lbw[:, 1, :], ALU.add))
            step(dve.tensor_tensor(lbw[:, 3, :], lbw[:, 3, :], lbw[:, 0, :], ALU.subtract))
            step(dve.tensor_scalar(lbw[:, 4, :], lbw[:, 3, :], -1.0, 1.0, ALU.mult, ALU.add))
            dve.wait_ge(S("lamb_landed"), 16)
            for n in range(2):
                step(dve.tensor_tensor(lamb[:, 2 * n, :], lamb[:, 2 * n, :], lamb[:, 2 * n + 1, :], ALU.mult))
                ins = dve.tensor_reduce(lams[:, n:n + 1], lamb[:, 2 * n, :], AX.X, ALU.add)
            ins.then_inc(S("lam_dots"), 1)
            dve.wait_ge(S("lam_exp"), 1)
            step(dve.tensor_tensor(lams[:, 2:3], lams[:, 1:2], lams[:, 0:1], ALU.subtract))
            step(dve.tensor_scalar(lams[:, 3:4], lams[:, 2:3], -LAM_INIT, None, ALU.add))
            step(dve.tensor_scalar(lams[:, 4:5], colB[:, 2:3], 1.0 - LAM_INIT, None, ALU.mult))
            dve.wait_ge(S("csil"), 1)
            dve.tensor_copy(csb[:], csil[:].unsqueeze(2).broadcast_to([P, KT, P])).then_inc(S("cond_ready"), 1)

            def fill(chunks):
                for layer, m in chunks:
                    section, half = m // 2, m % 2
                    name = f"ada{layer}_{m}"
                    ps = full_lin_of(dve, name)
                    if section in (2, 5):
                        g = gmod[:, section // 4, half * HALF:(half + 1) * HALF]
                        dve.wait_ge(S(f"gbias_landed{section // 4}"), 16 * (layer + 1))
                        ins = dve.scalar_tensor_tensor(g, ps[:, 0, :], 1.0, g, ALU.add, ALU.add)
                    else:
                        bias = colA[:, 24 + 48 * layer + 4 * m:24 + 48 * layer + 4 * m + 4]
                        row = {0: 0, 1: 1, 3: 2, 4: 3}[section]
                        ins = dve.scalar_tensor_tensor(modc[:, layer, row, 4 * half:4 * half + 4], ps[:, 0, 0:4],
                                                       1.0 if section in (1, 4) else 0.0, bias, ALU.add, ALU.add)
                    read(ins, name)

            def softmax(name, n, quads, mask, Pq):
                i, g = quads[n]
                W = P * (i + 1)
                ps = full_tmp_of(dve, f"{name}s{n}")
                if n >= 2:
                    dve.wait_ge(*done[f"{name}p{n - 2}"])
                buf = Pq[n % 2]
                for a in range(2):
                    ins = dve.tensor_tensor(buf[:, 2 * a:2 * a + 2, 0:W],
                                            ps[:, a, 0:2 * W].rearrange("p (j w) -> p j w", j=2),
                                            mask(i, g, a), ALU.add)
                read(ins, f"{name}s{n}")
                dve.wait_ge(*read_of(f"{name}s{n}"))
                return buf[:, :, 0:W]

            def maximum(name, n, g, scores, sink=None):
                step(dve.tensor_reduce(qst[:, n, 0, :], scores, AX.X, ALU.max))
                if sink is not None:
                    step(dve.tensor_tensor(qst[:, n, 0, :], qst[:, n, 0, :], sink, ALU.max))
                    dve.tensor_tensor(qst[:, n, 4, :], sink, qst[:, n, 0, :], ALU.subtract)
                dve.tensor_scalar(qst[:, n, 1, :], qst[:, n, 0, :], -1.0, None, ALU.mult
                                  ).then_inc(S(f"{name}max"), 1)

            def by_slot(v):
                return v.rearrange("p (j a) -> p a j", a=2)

            def slots(v):
                return v.rearrange("p (a j) -> p a j", a=2)

            for L in range(2):
                fill(ADA_START[L])
                variance(f"f{L}", st[:, 0, :, 0], st[:, 1, :, 0], D, EPS)
                rsqrt(f"f{L}", st[:, 1, :, 0], st[:, 2, :, 0], st[:, 0, :, 0])
                for i in range(NT):
                    ins = dve.tensor_scalar(hs[:, i, :], x[:, i, :], st[:, 2, i, 0:1], None, ALU.mult)
                ins.then_inc(S("f_scaled"), 1)
                for h in range(2):
                    low_of(f"f{L}hT{h}", 4 * h,
                           [colA[:, 8 * L + k:8 * L + k + 1] for k in range(4 * h, 4 * h + 4)])
                ps = full_lin_of(dve, f"f{L}f")
                dve.tensor_scalar(flat(gate_min), flat(ps), 0.0, None, ALU.min)
                read(dve.tensor_scalar(flat(gate_max), flat(ps), 0.0, None, ALU.max), f"f{L}f")
                dve.wait_ge(S("f_pn"), L + 1)
                if L == 1:
                    step(dve.tensor_tensor(flat(gate_lnsum), flat(gate_p), flat(gate_n), ALU.add))
                    for h in range(4):
                        ins = dve.scalar_tensor_tensor(gate_p[:, h, :], gate_n[:, h, :], lbw[:, 3, h:h + 1],
                                                       gate_p[:, h, :], ALU.mult, ALU.add)
                    ins.then_inc(S("f_sum"), 1)
                else:
                    dve.tensor_tensor(flat(gate_lnsum), flat(gate_p), flat(gate_n), ALU.add
                                      ).then_inc(S("f_sum"), 1)
                dve.wait_ge(S("f_ln"), L + 1)
                step(dve.tensor_tensor(flat(gate_p), flat(gate_p if L else gate_min), flat(gate_lnsum), ALU.subtract))
                dve.tensor_tensor(flat(gate_max), flat(gate_max), flat(gate_lnsum), ALU.add
                                  ).then_inc(S("f_kexp"), 1)
                dve.wait_ge(S("chunkmask"), 1)
                dve.wait_ge(S("f_kexp"), L + 1)
                step(dve.tensor_tensor_scan(flat(G), chunkmask[:], flat(gate_p), 0.0, ALU.mult, ALU.add))
                dve.wait_ge(S("f_kin"), L + 1)
                ins = dve.memset(flat(scor), 0.0)
                if L == 1:
                    for h in range(4):
                        ins = dve.tensor_scalar(kin[:, h, :], kin[:, h, :], lbw[:, 4, h:h + 1], None, ALU.mult)
                step(ins)
                dve.wait_ge(*read_of(f"f{L}kv"))
                dve.wait_ge(*read_of(f"f{L}q"))
                dve.wait_ge(S("trig"), 1)
                for i in range(NT):
                    heads = qkv[:, i, 0:640].rearrange("p (h d) -> p h d", h=10)
                    x1, x2 = heads[:, :, 0:ROPE_HALF], heads[:, :, ROPE_HALF:2 * ROPE_HALF]
                    sin, cos = (trig[:, i, c, :].unsqueeze(1).broadcast_to([P, 10, ROPE_HALF]) for c in range(2))
                    dve.tensor_tensor(ropet[:, 0], x1, cos, ALU.mult)
                    dve.tensor_tensor(ropet[:, 1], x2, sin, ALU.mult)
                    dve.tensor_tensor(ropet[:, 2], x2, cos, ALU.mult)
                    step(dve.tensor_tensor(ropet[:, 3], x1, sin, ALU.mult))
                    dve.tensor_tensor(x1, ropet[:, 0], ropet[:, 1], ALU.subtract)
                    step(dve.tensor_tensor(x2, ropet[:, 2], ropet[:, 3], ALU.add))
                for i in range(NT):
                    for a in range(2):
                        ins = dve.tensor_copy(kdup[:, i, :, a, :], qkv[:, i, K0:V0].rearrange("p (g d) -> p g d", g=2))
                ins.then_inc(S("f_rope"), 1)
                dve.wait_ge(*read_of(f"f{L}qh"))
                dve.nop().then_inc(S("level_ready"), 1)
                ps = full_tmp_of(dve, f"f{L}kT")
                read(dve.tensor_copy(flat(kTd), flat(ps)[:, 0:2 * T]), f"f{L}kT")

                def differences(lv):
                    buf = decay[lv % 2]
                    if lv >= 3:
                        dve.wait_ge(*done[f"f{L}lv{lv - 2}"])
                    if lv < LEVELS:
                        b = 2 ** (lv - 1)
                        g = flat(G).rearrange("p (n h b) -> p n h b", h=2, b=b)
                        d = flat(buf).rearrange("p (n h b) -> p n h b", h=2, b=b)
                        ref = g[:, :, 0, b - 1:b].broadcast_to([P, 4 * T // (2 * b), b])
                        if 2 * b <= CHUNK:
                            dve.tensor_tensor(d[:, :, 1, :], g[:, :, 1, :], ref, ALU.subtract)
                        else:
                            dve.tensor_copy(d[:, :, 1, :], g[:, :, 1, :])
                        ins = dve.tensor_tensor(d[:, :, 0, :], ref, g[:, :, 0, :], ALU.subtract)
                    else:
                        g = G.rearrange("p h (c t) -> p h c t", c=4)
                        d = buf.rearrange("p h (c t) -> p h c t", c=4)

                        def end(c):
                            return g[:, :, c, CHUNK - 1:CHUNK].broadcast_to([P, 4, CHUNK])

                        dve.tensor_copy(d[:, :, 2, :], g[:, :, 2, :])
                        dve.tensor_tensor(d[:, :, 3, :], g[:, :, 3, :], end(2), ALU.add)
                        dve.tensor_tensor(d[:, :, 1, :], end(1), g[:, :, 1, :], ALU.subtract)
                        step(dve.tensor_tensor(d[:, :, 0, :], end(0), g[:, :, 0, :], ALU.subtract))
                        ins = dve.tensor_tensor(d[:, :, 0, :], d[:, :, 0, :], end(1), ALU.add)
                    ins.then_inc(S("level_diff"), 1)

                def factors(lv):
                    dve.wait_ge(S("level_exp"), LEVELS * L + lv)
                    b = 2 ** (lv - 1)
                    d, q, k = (flat(v).rearrange("p (n h b) -> p n h b", h=2, b=b) for v in (decay[lv % 2], qin, kin))
                    dve.tensor_tensor(d[:, :, 1, :], d[:, :, 1, :], q[:, :, 1, :], ALU.mult)
                    dve.tensor_tensor(d[:, :, 0, :], d[:, :, 0, :], k[:, :, 0, :], ALU.mult
                                      ).then_inc(S("level_ready"), 1)

                def gather(lv):
                    ps = flat(full_tmp_of(dve, f"f{L}lv{lv}"))
                    if lv == 0:
                        dve.wait_ge(S("levels"), 1)
                    else:
                        dve.wait_ge(*read_of(f"f{L}lv{lv - 1}"))
                    read(dve.copy_predicated(scor[:], levelmask[:, lv, :].bitcast(I32).unsqueeze(1).broadcast_to([P, 8, P]),
                                             ps.rearrange("p (n t) -> p n t", n=8)), f"f{L}lv{lv}")

                differences(1)
                for lv in range(1, LEVELS + 1):
                    if lv < LEVELS:
                        differences(lv + 1)
                    factors(lv)
                    gather(lv - 1)
                dve.wait_ge(S("f_hsq"), L + 1)
                if L == 0:
                    dve.memset(st[:, 0, :, 4:8], 1.0)
                dve.tensor_reduce(st[:, 0, :, 0:4], hs[:, :, 0:HALF].rearrange("p i (h d) -> p i h d", h=4),
                                  AX.X, ALU.add).then_inc(S(f"f{L}hss"), 1)
                variance(f"f{L}h", st[:, 0], st[:, 1], P, EPS)
                rsqrt(f"f{L}h", st[:, 1], st[:, 2], st[:, 0])
                ps = full_lin_of(dve, f"f{L}ho")
                for i in range(NT):
                    ins = dve.tensor_tensor(hs[:, i, HALF:D].rearrange("p (h d) -> p h d", h=4),
                                            ps[:, i, :].rearrange("p (h d) -> p h d", h=4),
                                            st[:, 2, i, 0:4].unsqueeze(2).broadcast_to([P, 4, P]), ALU.mult)
                read(ins, f"f{L}ho")
                dve.wait_ge(*read_of(f"f{L}ho"))
                dve.wait_ge(*read_of(f"f{L}g"))
                dve.tensor_tensor(hs[:, :, HALF:D], hs[:, :, HALF:D], zg[:], ALU.mult).then_inc(S("f_b"), 1)
                quads = [(i, g) for i in range(NT) for g in range(2)]
                name = f"f{L}a"
                dve.wait_ge(S("band"), 1)
                dve.wait_ge(S("sinks_landed"), 16)

                def window(i, g, a):
                    m = band[:] if i else band[:, P:T]
                    return m.unsqueeze(1).broadcast_to([P, 2, P * (i + 1)])

                def total(n):
                    i, g = quads[n]
                    dve.wait_ge(S(f"{name}exp"), n + 1)
                    step(dve.tensor_tensor(qst[:, n, 2, :], qst[:, n, 2, :], qst[:, n, 3, :], ALU.add))
                    dve.reciprocal(by_slot(rden[:, i, 4 * g:4 * g + 4]), slots(qst[:, n, 2, :])
                                   ).then_inc(S(f"{name}prob"), 1)

                for n, (i, g) in enumerate(quads):
                    sink = by_slot(sinks[:, 8 * L + 4 * g:8 * L + 4 * g + 4])
                    scores = softmax(name, n, quads, window, Pq_first)
                    maximum(name, n, g, scores, sink)
                    if n >= 1:
                        total(n - 1)
                    fill(ADA_WINDOW[L].get(n, ()))
                total(3)
                fill(ADA_WINDOW[L].get(4, ()))
                dve.wait_ge(S(f"{name}prob"), 4)
                dve.wait_ge(*done[f"{name}o1"])
                ps = full_lin_of(dve, f"{name}o0")
                for i in range(NT):
                    ins = dve.tensor_tensor(hs[:, i, 0:HALF].rearrange("p (h d) -> p h d", h=8),
                                            ps[:, i, :].rearrange("p (h d) -> p h d", h=8),
                                            rden[:, i, 0:8].unsqueeze(2).broadcast_to([P, 8, HD]), ALU.mult)
                read(ins, f"{name}o0")
                dve.wait_ge(*read_of(f"{name}o0"))
                dve.wait_ge(*read_of(f"f{L}z"))
                dve.tensor_tensor(hs[:, :, 0:HALF], hs[:, :, 0:HALF], zs[:], ALU.mult).then_inc(S("f_a"), 1)
                fill(ADA_GATED[L])
                low_of(f"f{L}bT0", 4, colB[:, 3 + L:4 + L])
                low_of(f"f{L}aT0", 0)
                dve.wait_ge(*read_of(f"f{L}gh0"))
                dve.wait_ge(*read_of(f"f{L}gh1"))
                for c in range(2):
                    cols = slice(c * HALF, (c + 1) * HALF)
                    ps = full_lin_of(dve, f"f{L}ua{c}")
                    read(dve.tensor_tensor(hs[:, :, cols], ps, ga[:, :, cols], ALU.mult), f"f{L}ua{c}")
                    ps = full_lin_of(dve, f"f{L}uh{c}")
                    read(dve.tensor_tensor(gh[:, :, cols], ps, gh[:, :, cols], ALU.mult), f"f{L}uh{c}")
                    dve.wait_ge(*read_of(f"f{L}ua{c}"))
                    dve.wait_ge(*read_of(f"f{L}uh{c}"))
                    ins = dve.tensor_tensor(hs[:, :, cols], hs[:, :, cols], gh[:, :, cols], ALU.add)
                ins.then_inc(S("f_merged"), 1)
                fill(ADA_MERGE[L])
                for h in range(2):
                    low_of(f"f{L}mT{h}", 4 * h)
                for c in range(2):
                    cols = slice(c * HALF, (c + 1) * HALF)
                    ps = full_lin_of(dve, f"f{L}out{c}")
                    read(dve.tensor_tensor(x[:, :, cols], x[:, :, cols], ps, ALU.add), f"f{L}out{c}")

            variance("n", st[:, 0, :, 0], st[:, 1, :, 0], D, EPS)
            rsqrt("n", st[:, 1, :, 0], st[:, 2, :, 0], st[:, 0, :, 0])
            dve.wait_ge(S("lnp_landed"), 32)
            for i in range(NT):
                ins = dve.scalar_tensor_tensor(x[:, i, :], x[:, i, :], st[:, 2, i, 0:1], lnp[:, 0, :],
                                               ALU.mult, ALU.mult)
            ins.then_inc(S("s0x"), 1)

            def mixed(name):
                for h in range(2):
                    dve.wait_ge(*read_of(f"{name}hT{h}"))
                    whole = flat(hs)[:, 4 * h * T:4 * (h + 1) * T]
                    step(dve.tensor_copy(flat(hThi[:, 4 * h:4 * h + 4, :]), whole))
                    dve.tensor_tensor(flat(hTlo[:, 4 * h:4 * h + 4, :]), whole,
                                      flat(hThi[:, 4 * h:4 * h + 4, :].bitcast(F32)), ALU.subtract
                                      ).then_inc(S("mixed_low"), 1)

            def residual(name, n, after):
                for c in range(2):
                    cols = slice(c * HALF, (c + 1) * HALF)
                    ps = full_lin_of(dve, f"{name}y{c}")
                    g = gmod[:, n % 2, cols].unsqueeze(1).broadcast_to([P, NT, HALF])
                    read(dve.tensor_tensor(hs[:, :, cols], ps, g, ALU.mult), f"{name}y{c}")
                    dve.wait_ge(*read_of(f"{name}y{c}"))
                    step(dve.scalar_tensor_tensor(x[:, :, cols], x[:, :, cols], ALPHA, hs[:, :, cols],
                                                  ALU.mult, ALU.add))
                    for i in range(NT):
                        ins = dve.bn_stats(bns[:, i, c, :], x[:, i, cols])
                step(ins)
                for i in range(NT):
                    ins = dve.bn_aggr(mv[:, i, :], bns[:, i, :, :])
                step(ins)
                dve.tensor_scalar(mv[:, :, 1], mv[:, :, 1], LN_EPS, None, ALU.add).then_inc(S(f"{name}lnvar"), 1)
                rsqrt(f"{name}ln", mv[:, :, 1], st[:, 2, :, 0], st[:, 0, :, 0])
                dve.wait_ge(S("lnp_landed"), 32 * (n + 2))
                for i in range(NT):
                    step(dve.tensor_scalar(x[:, i, :], x[:, i, :], mv[:, i, 0:1], st[:, 2, i, 0:1],
                                           ALU.subtract, ALU.mult))
                for i in range(NT):
                    step(dve.tensor_tensor(x[:, i, :], x[:, i, :], lnp[:, 0, :], ALU.mult))
                for i in range(NT):
                    ins = dve.tensor_tensor(x[:, i, :], x[:, i, :], lnp[:, 1, :], ALU.add)
                ins.then_inc(S(f"{after}x"), 1)

            def mlp(name, n, after):
                mixed(name)
                for g in range(8):
                    dve.wait_ge(*read_of(f"{name}u{g}"))
                    if g >= 2:
                        dve.wait_ge(*done[f"{name}hb{g - 2}"])
                    h = flat(hidden[g % 2])
                    step(dve.tensor_tensor(h, h, h, ALU.mult))
                    step(dve.tensor_copy(flat(hbhi[:, g % 2]), h))
                    dve.tensor_tensor(flat(hblo[:, g % 2]), h, flat(hbhi[:, g % 2].bitcast(F32)), ALU.subtract
                                      ).then_inc(S(f"{name}act"), 1)
                residual(name, n, after)

            def biased(i, g, a):
                return Mbias[:, 4 * g + a:4 * g + 4:2, 0:P * (i + 1)][:, :, ::-1]

            mixed("s0")
            dve.wait_ge(S("s0css"), 1)
            dve.tensor_scalar(st[:, 1, :, 0], st[:, 0, :, 0], 1.0 / T, LN_EPS, ALU.mult, ALU.add
                              ).then_inc(S("s0cvar"), 1)
            rsqrt("s0c", st[:, 1, :, 0], st[:, 2, :, 0], st[:, 0, :, 0])
            for i in range(NT):
                ins = dve.tensor_scalar(ckv[:, i, :], ckv[:, i, :], st[:, 2, i, 0:1], None, ALU.mult)
            ins.then_inc(S("s0ckvn"), 1)
            for i in range(NT):
                for g in range(2):
                    n = 2 * i + g
                    W = P * (i + 1)
                    dve.wait_ge(*read_of(f"s0idx{i}{g}"))
                    for s in range(QUAD):
                        head = 4 * g + 2 * (s % 2) + s // 2
                        r, v = Pq_second[n % 2][:, s, 0:W], iw[:, i, head:head + 1]
                        if g == 0 and s == 0:
                            ins = dve.tensor_scalar(isc[:, i, 0:W], r, v, None, ALU.mult)
                        else:
                            ins = dve.scalar_tensor_tensor(isc[:, i, 0:W], r, v, isc[:, i, 0:W], ALU.mult, ALU.add)
                        if s < QUAD - 1:
                            step(ins)
                    ins.then_inc(S("s0idx_used"), 1)
                    dve.wait_ge(S("s0idx_used"), n + 1)
            ps = flat(full_tmp_of(dve, "s0ckvT"))
            for r in range(2):
                ins = dve.tensor_scalar(ckvT[:, r, :], ps[:, r * T:(r + 1) * T], colB[:, r:r + 1], None, ALU.mult)
            read(ins, "s0ckvT")
            dve.wait_ge(S("band"), 1)
            for i in range(NT):
                v = isc[:, i, i * P:(i + 1) * P]
                ins = dve.tensor_tensor(v, v, band[:, P:T], ALU.add)
            step(ins)
            for i in range(NT):
                W = P * (i + 1)
                for n in range(TOPK // 8):
                    src = isc if n == 0 else iwk
                    step(dve.max(top8[:], src[:, i, 0:W]))
                    step(dve.match_replace(iwk[:, i, 0:W], top8[:], src[:, i, 0:W], LOWEST))
                step(dve.tensor_tensor(isc[:, i, 0:W], isc[:, i, 0:W], iwk[:, i, 0:W], ALU.is_equal))
                step(dve.tensor_scalar(isc[:, i, 0:W], isc[:, i, 0:W], NEG, None, ALU.mult))
            quads = [(i, g) for i in range(NT) for g in range(4)]
            dve.wait_ge(S("Mbias"), 16)

            def total_s0(n):
                i, g = quads[n]
                dve.wait_ge(S("s0exp"), n + 1)
                dve.reciprocal(by_slot(rden[:, i, 4 * g:4 * g + 4]), slots(qst[:, n, 2, :])
                               ).then_inc(S("s0prob"), 1)

            def scaled_out(i):
                dve.wait_ge(S("s0prob"), 4 * i + 4)
                ps = full_lin_of(dve, f"s0o{i}")
                read(dve.tensor_tensor(hs[:, i, :].rearrange("p (h d) -> p h d", h=16),
                                       flat(ps).rearrange("p (h d) -> p h d", h=16),
                                       rden[:, i, :].unsqueeze(2).broadcast_to([P, 16, HD]), ALU.mult), f"s0o{i}")

            for n, (i, g) in enumerate(quads):
                W = P * (i + 1)
                scores = softmax("s0", n, quads, biased, Pq_second)
                step(dve.tensor_tensor(scores, scores, isc[:, i, 0:W].unsqueeze(1).broadcast_to([P, QUAD, W]), ALU.add))
                maximum("s0", n, g, scores)
                if n >= 1:
                    total_s0(n - 1)
                fill(ADA_SPARSE.get(n, ()))
                if n == 6:
                    scaled_out(0)
            total_s0(7)
            scaled_out(1)
            for h in range(2):
                low_of(f"s0oT{h}", 4 * h)
            residual("s0", 0, "s1")
            mlp("s1", 1, "s2")
            mixed("s2")

            def combine(n):
                i, g = quads[n]
                W = P * (i + 1)
                dve.wait_ge(S("s2exp"), n + 1)
                step(dve.reciprocal(qst[:, n, 3, :], qst[:, n, 2, :]))
                step(dve.tensor_scalar(qst[:, n, 3, 2:4], qst[:, n, 3, 2:4], lams[:, 3:4], None, ALU.mult))
                for j in range(2):
                    ins = dve.tensor_scalar(Pq_second[n % 2][:, j, 0:W], Pq_second[n % 2][:, j, 0:W], qst[:, n, 3, j:j + 1],
                                            None, ALU.mult)
                step(ins)
                for j in range(2):
                    ins = dve.scalar_tensor_tensor(Pq_second[n % 2][:, j, 0:W], Pq_second[n % 2][:, 2 + j, 0:W],
                                                   qst[:, n, 3, 2 + j:3 + j], Pq_second[n % 2][:, j, 0:W], ALU.mult, ALU.add)
                ins.then_inc(S("s2prob"), 1)

            def raw_out(i):
                ps = full_lin_of(dve, f"s2o{i}")
                read(dve.tensor_copy(hs[:, i, :], flat(ps)), f"s2o{i}")

            for n, (i, g) in enumerate(quads):
                scores = softmax("s2", n, quads, biased, Pq_second)
                maximum("s2", n, g, scores)
                if n >= 1:
                    combine(n - 1)
                fill(ADA_DIFF.get(n, ()))
                if n == 6:
                    raw_out(0)
            combine(7)
            raw_out(1)
            dve.wait_ge(S("s2osq"), 1)
            dve.tensor_reduce(st[:, 0], osq.rearrange("p i (h d) -> p i h d", h=8), AX.X, ALU.add
                              ).then_inc(S("s2hss"), 1)
            variance("s2h", st[:, 0], st[:, 1], P, LN_EPS)
            rsqrt("s2h", st[:, 1], st[:, 2], st[:, 0])
            for i in range(NT):
                o = hs[:, i, :].rearrange("p (h d) -> p h d", h=8)
                ins = dve.tensor_tensor(o, o, st[:, 2, i, :].unsqueeze(2).broadcast_to([P, 8, P]), ALU.mult)
            ins.then_inc(S("s2o"), 1)
            for h in range(2):
                low_of(f"s2oT{h}", 4 * h, lams[:, 4:5])
            residual("s2", 2, "s3")
            mlp("s3", 3, "s4")


_INS = ["x", "positions", "norm_w", "w_in", "attn_sinks", "hgrn_norm_w", "w_up_attn", "w_up_hgrn", "w_out",
        "lb_logits", "final_norm_w", "c_2", "rel_bias_2", "ada_w_2", "ada_b_2", "ln_g_2", "ln_b_2", "a_w_in_2",
        "a_kv_norm_2", "a_w_uk_2", "a_w_uv_2", "a_w_o_2", "b_w_in_2", "b_lambda_2", "b_subln_2", "b_w_o_2",
        "mlp_w1_2", "mlp_w2_2"]


def kernel(**inputs):
    import concourse.bacc as _bacc
    from concourse.bass_utils import run_bass_kernel_spmd as _run

    nc = _bacc.Bacc("TRN2", target_bir_lowering=False, num_devices=1)
    arrays, args = {}, {}
    for name in _INS:
        a = np.ascontiguousarray(inputs[name])
        arrays[f"in_{name}"] = a
        args[name] = nc.dram_tensor(f"in_{name}", a.shape, mybir.dt.from_np(a.dtype), kind="ExternalInput").ap()
    onehot = bucket_onehot()
    arrays["onehot_table"] = onehot
    args["onehot"] = nc.dram_tensor("onehot_table", onehot.shape, F32, kind="ExternalInput").ap()
    out = nc.dram_tensor("out_0", (1, T, D), F32, kind="ExternalOutput").ap()
    build_program(nc, args, out)
    r = _run(nc, [arrays], core_ids=[0])
    return r.results[0]["out_0"]
```

```python
from contextlib import ExitStack

import numpy as np

import concourse.bass as bass
from concourse import mybir

ALU = mybir.AluOpType
ACT = mybir.ActivationFunctionType
AX = mybir.AxisListType
F32 = mybir.dt.float32
F32R = mybir.dt.float32r
I32 = mybir.dt.int32

P = 128
T = 256
NT = T // P
D = 1024
KT = D // P
HD = 64
HALF = 512
EPS = 1e-6
LN_EPS = 1e-5
NEG = -1e30
LOWEST = -3e38
TOPK = 64
ALPHA = 4 ** 0.25
LAM_INIT = 0.8 - 0.6 * float(np.exp(-0.3))
RING = 4
PARTS = 3
NBUCKET = 32
DIST = 3 * P - 1
ROPE_HALF = 8
QUAD = 4
LEVELS = 8
CHUNK = 64
ARENA = 65
TURN = float(2 * np.pi)
TURN_PARTS = [6.28125, 0.0019350051879882812, 3.0199159819567e-07]
ROUNDER = 1.5 * 2.0 ** 23
SIN_MAX = 3.1415925
ADA = [(0, m) for m in range(12)] + [(1, m) for m in range(12)]
ADA_LEVELS = (2, 6)
Q0, K0, V0, Z0, QH0, F0, I0, G0, GA0, GH0 = 0, 512, 640, 768, 1280, 1792, 2304, 2816, 3328, 4352


def bucket_onehot():
    edges = list(range(16)) + [int(np.ceil(16 * 8 ** (k / 16) - 1e-9)) for k in range(16)] + [T]
    table = np.zeros((NBUCKET + 1, DIST), np.float32)
    for b in range(NBUCKET):
        table[b, edges[b] + P - 1:edges[b + 1] + P - 1] = 1.0
    table[0, :P - 1] = 1.0
    table[NBUCKET, :P - 1] = NEG
    return table


def build_program(nc, I, out):
    with ExitStack() as ctx:
        def sb(name, shape, dt=F32):
            return ctx.enter_context(nc.sbuf_tensor(name, shape, dt))

        sems = {}

        def S(name):
            if name not in sems:
                sems[name] = ctx.enter_context(nc.semaphore(name))
            return sems[name]

        lin_ps = ctx.enter_context(nc.psum_tensor("lin_ps", [P, 4, HALF], F32))
        tmp_ps = ctx.enter_context(nc.psum_tensor("tmp_ps", [P, 4, HALF], F32))

        ring = sb("ring", [P, RING, 4, HALF])
        x = sb("x", [P, NT, D])
        whi = sb("whi", [P, PARTS, 2, HALF], F32R)
        wlo = sb("wlo", [P, PARTS, 2, HALF], F32R)
        hThi = sb("hThi", [P, KT, T], F32R)
        hTlo = sb("hTlo", [P, KT, T], F32R)
        hbhi = sb("hbhi", [P, 2, QUAD, T], F32R)
        hblo = sb("hblo", [P, 2, QUAD, T], F32R)
        ident = sb("ident", [P, P])
        band = sb("band", [P, T])
        levelmask = sb("levelmask", [P, LEVELS, P])
        chunkmask = sb("chunkmask", [P, 4 * T])
        stackA = sb("stackA", [P, P])
        stackB = sb("stackB", [5, P])
        colA = sb("colA", [P, P])
        colB = sb("colB", [P, 5])
        sinks = sb("sinks", [P, 16])
        lamb = sb("lamb", [P, 4, HD])
        posi = sb("posi", [P, NT], I32)
        posf = sb("posf", [P, NT])
        invf = sb("invf", [P, ROPE_HALF])
        ang = sb("ang", [P, NT, 2, ROPE_HALF])
        angk = sb("angk", [P, NT, 2, ROPE_HALF])
        trig = sb("trig", [P, NT, 2, ROPE_HALF])
        lbw = sb("lbw", [P, 6, 4])
        lams = sb("lams", [P, 8])
        csil = sb("csil", [P, KT])
        ones = sb("ones", [P, P])
        adasum = sb("adasum", [P, 2, HALF])
        modc = sb("modc", [P, 2, 4, KT])
        gmod = sb("gmod", [P, 2, D])
        relT = sb("relT", [NBUCKET + 1, 16])
        lnp = sb("lnp", [P, 2, D])
        st = sb("st", [P, 3, 2, 8])
        bns = sb("bns", [P, NT, 2, 6])
        mv = sb("mv", [P, NT, 2])
        qst = sb("qst", [P, 8, 6, QUAD])
        rden = sb("rden", [P, NT, 16])
        ropet = sb("ropet", [P, 4, 10, ROPE_HALF])
        hs = sb("hs", [P, NT, D])
        iw = sb("iw", [P, NT, 8])
        top8 = sb("top8", [P, 8])
        arena = sb("arena", [P, ARENA * 1024 // 4])
        scratch = nc.dram_tensor("relvec_dram", (16, DIST), F32).ap()

        def at(k, *shape):
            n = int(np.prod(shape))
            v = arena[:, int(k * 1024):int(k * 1024) + n]
            names = " ".join(f"d{j}" for j in range(len(shape)))
            return v if len(shape) == 1 else v.rearrange(
                f"p ({names}) -> p {names}", **{f"d{j}": s for j, s in enumerate(shape)})

        qkv = at(0, NT, 768)
        zs = at(1.5, NT, HALF)
        ga = at(2.5, NT, D)
        gh = at(4.5, NT, D)
        vh = at(6.5, NT, HALF)
        zg = at(7.5, NT, HALF)
        qin = at(8.5, 4, T)
        kin = at(9.5, 4, T)
        G = at(10.5, 4, T)
        decay = [at(11.5, 4, T), at(12.5, 4, T)]
        scor = at(13.5, 8, P)
        cross = at(14.5, 4, P)
        kdup = at(15, NT, 2, 2, HD)
        kTd = at(15.5, 2, T)
        Pq_first = [decay[0], decay[1]]
        pT_first = [at(9.5, QUAD * T), at(10.5, QUAD * T)]
        qTa = qin
        onehot, relvec = at(2, DIST)[0:NBUCKET + 1], at(2.5, DIST)[0:16]
        pairx = at(3, 2, P).bitcast(I32)
        levelge = at(0, LEVELS + 1, P)
        gate_min, gate_max, gate_p, gate_n, gate_lnsum = decay[0], decay[1], at(13.5, 4, T), kin, G
        qT = at(0, KT, T)
        kT = at(2, KT, T)
        vv = at(4, NT, D)
        iqT = at(6, 4, T)
        ikT = at(7, T)
        ckvT = at(7.25, 2, T)
        wukT = at(7.75, 2, D)
        isc = at(9.75, NT, T)
        Mbias = at(10.25, 16, T)
        Pq_second = [at(14.25, QUAD, T), at(15.25, QUAD, T)]
        pT_second = [at(7.75, QUAD * T), at(8.75, QUAD * T)]
        hidden = [at(6, QUAD, T), at(7, QUAD, T)]
        osq = at(6, NT, D)
        iwk, ckv = hs[:, :, T:2 * T], hs[:, :, 2 * T:3 * T]

        done = {}
        turn_tmp, turn_lin = {}, {}
        units, halves, halves_at = [], [], {}
        ada_units = []
        count = {}

        def bump(name, n=1):
            count[name] = count.get(name, 0) + n
            return count[name]

        def read_of(name):
            if name in turn_tmp:
                n = turn_tmp[name]
                return S(f"tmp_read{n % 2}"), n // 2 + 1
            half, n = turn_lin[name]
            return S(f"lin_read{half}"), n + 1

        def win(w, c0, n, k0=0):
            return w[k0 * P:(k0 + 4) * P, c0:c0 + n].rearrange("(k p) n -> p k n", p=P)

        hT = (hThi, hTlo)

        block = ctx.enter_context(nc.Block())

        @block.tensor
        def _(pe):
            pending = [0]
            lin_last, lin_turns = [1], [0, 0]

            def unit(parts, split):
                n = len(units)
                landed = 16 * len(parts) + (units[n - RING]["landed"] if n >= RING else 0)
                units.append({"parts": parts, "landed": landed})
                if split is None:
                    pending[0] += 1
                elif split != "ada":
                    units[n]["release"] = (S("low_formed"), len(halves) + 2)
                    halves.extend((n, h, split) for h in range(2))
                return n

            def take(*parts):
                n = unit(parts, None)
                pe.wait_ge(S(f"w_landed{n % RING}"), units[n]["landed"])
                return ring[:, n % RING]

            def used(ins):
                n, pending[0] = pending[0], 0
                ins.then_inc(S("w_used"), n)
                value = bump("w_used", n)
                for u in units:
                    if "release" not in u:
                        u["release"] = (S("w_used"), value)
                return S("w_used"), value

            def take_halves(width, *parts):
                first = len(halves)
                unit(parts, width)
                for h in range(2):
                    pe.wait_ge(S("low_formed"), first + h + 1)
                    slot = (first + h) % PARTS
                    yield 2 * h, whi[:, slot], wlo[:, slot]

            def half_used(ins, *names):
                ins.then_inc(S("half_used"), 1)
                value = bump("half_used")
                for name in names:
                    finished(name, (S("half_used"), value))

            def finished(name, event):
                done[name] = event
                halves_at[name] = count.get("half_used", 0), (count.get("w_used", 0), 2 * len(ada_units))

            def wait_read(*names):
                for name in names:
                    pe.wait_ge(*read_of(name))

            rest = []

            def operand_ready(first, second):
                pe.wait_ge(*first)
                rest.append(second)

            def operand(k0):
                if k0 and rest:
                    pe.wait_ge(*rest.pop())

            def open_tmp(name):
                n = len(turn_tmp)
                turn_tmp[name] = n
                if n >= 2:
                    pe.wait_ge(S(f"tmp_read{n % 2}"), n // 2)
                return tmp_ps[:, 2 * (n % 2):2 * (n % 2) + 2, :]

            def close_tmp(ins, name):
                ins.then_inc(S("tmp_full"), 1)
                finished(name, (S("tmp_full"), bump("tmp_full")))

            def open_lin(name, half=None):
                half = 1 - lin_last[0] if half is None else half
                lin_last[0] = half
                n = lin_turns[half]
                lin_turns[half] += 1
                turn_lin[name] = (half, n)
                if n:
                    pe.wait_ge(S(f"lin_read{half}"), n)
                return lin_ps[:, 2 * half:2 * half + 2, :]

            def product_tok(ps, src, k, i, hi, lo, first, last):
                xh, xl = (v[:, k, i * P:(i + 1) * P] for v in src)
                pe.matmul(ps, xh, hi, start=first, stop=False, skip_group_check=True)
                pe.matmul(ps, xh, lo, start=False, stop=False, skip_group_check=True)
                return pe.matmul(ps, xl, hi, start=False, stop=last, skip_group_check=True)

            def product_feat(ps, src, k, hi, lo, first, last):
                xh, xl = (v[:, k, :] for v in src)
                pe.matmul(ps, hi, xh, start=first, stop=False, skip_group_check=True)
                pe.matmul(ps, hi, xl, start=False, stop=False, skip_group_check=True)
                return pe.matmul(ps, lo, xh, start=False, stop=last, skip_group_check=True)

            opened = {}

            def linear_part(name, w, c0, n, src, k0, kts=KT, k_src=0, half=None,
                            mid=None):
                if k0 == 0:
                    opened[name] = open_lin(name, half)
                ps = opened[name]
                operand(k0)
                for r, hi, lo in take_halves(n, (slice(0, n), win(w, c0, n, k0))):
                    for k in range(2):
                        kk = k0 + r + k
                        for i in range(NT):
                            mm = product_tok(ps[:, i, 0:n], src, k_src + kk, i, hi[:, k, 0:n], lo[:, k, 0:n],
                                             kk == 0, kk == kts - 1)
                    half_used(mm, name)
                    if r == 0 and mid:
                        mid()

            def linear_tok(name, w, c0, n, src, kts=KT, k_src=0):
                for k0 in range(0, kts, 4):
                    linear_part(name, w, c0, n, src, k0, kts, k_src)

            def feat_units(name, ps, w, c0, src):
                for k0 in (0, 4):
                    operand(k0)
                    for r, hi, lo in take_halves(HALF, (slice(0, HALF), win(w, c0, HALF, k0))):
                        for k in range(2):
                            kk = k0 + r + k
                            for c in range(4):
                                cols = slice(c * P, (c + 1) * P)
                                mm = product_feat(ps[:, c // 2, (c % 2) * T:(c % 2) * T + T], src, kk,
                                                  hi[:, k, cols], lo[:, k, cols], kk == 0 and c % 2 == 0,
                                                  kk == KT - 1)
                        half_used(mm, name)

            def linear_feat(name, w, c0, src):
                feat_units(name, open_lin(name), w, c0, src)

            def transposes(name, pieces):
                ps = open_tmp(name).rearrange("p a b -> p (a b)")
                for n, piece in enumerate(pieces):
                    mm = pe.transpose(ps[:, n * P:(n + 1) * P], piece, ident[:])
                close_tmp(mm, name)

            def feature_major(name, src, kts=KT):
                for h in range(kts // 4):
                    transposes(f"{name}{h}", [src[:, i, k * P:(k + 1) * P]
                                              for k in range(4 * h, 4 * h + 4) for i in range(NT)])

            def ada_end():
                n = len(ada_units) - 1
                layer, m = ADA[n]
                name = f"ada{layer}_{m}"
                ps = open_tmp(name)
                pe.wait_ge(S("ada_read"), 2 * n + 2)
                if m // 2 in (2, 5):
                    mm = pe.matmul(ps[:, 0, :], ones[:], adasum[:, n % 2, :], start=True, stop=True)
                else:
                    for c in range(4):
                        mm = pe.matmul(ps[:, 0, c:c + 1], adasum[:, n % 2, c * P:(c + 1) * P], ones[:, 0:1],
                                       start=(c == 0), stop=True, skip_group_check=True)
                close_tmp(mm, name)

            def ada_start():
                layer, m = ADA[len(ada_units)]
                first = len(units)
                for u in range(2):
                    unit([(slice(0, HALF), win(I["ada_w_2"][layer], m * HALF, HALF, 4 * u))], "ada")
                    units[-1]["release"] = (S("ada_read"), 2 * len(ada_units) + u + 1)
                ada_units.append(first)

            def attention(name, quads, q, k, v, vw, per, ocols, bufs, fills=None, lag=1, half=None):
                def scores(n):
                    i, g = quads[n]
                    W = P * (i + 1)
                    ps = open_tmp(f"{name}s{n}")
                    for j in range(2):
                        for a in range(2):
                            mm = pe.matmul(ps[:, a, j * W:(j + 1) * W], q(g, j, a)[:, i * P:(i + 1) * P],
                                           k(g, j, a)[:, 0:W], start=True, stop=True)
                    close_tmp(mm, f"{name}s{n}")

                def turned(n):
                    i, g = quads[n]
                    pe.wait_ge(S(f"{name}{'exp' if per == QUAD else 'prob'}"), n + 1)
                    transposes(f"{name}p{n}", [bufs[0][n % 2][:, s, b * P:(b + 1) * P]
                                               for s in range(per) for b in range(i + 1)])

                def product(n):
                    i, g = quads[n]
                    wait_read(f"{name}p{n}")
                    if n == 0:
                        product.ps = open_lin(f"{name}o0", half)
                    if g == 0 and i == 1 and ocols == D:
                        product.ps = open_lin(f"{name}o1", 1 - half)
                    ps = product.ps
                    for s in range(per):
                        head = g * per + (2 * (s % 2) + s // 2 if per == QUAD else s)
                        o = ps[:, i, head * vw:(head + 1) * vw] if ocols == HALF else \
                            ps.rearrange("p a b -> p (a b)")[:, head * vw:(head + 1) * vw]
                        for b in range(i + 1):
                            blk = s * (i + 1) + b
                            mm = pe.matmul(o, bufs[1][n % 2][:, blk * P:(blk + 1) * P], v(b, head),
                                           start=(b == 0), stop=(b == i))
                    mm.then_inc(S("att_pv"), 1)
                    event = (S("att_pv"), bump("att_pv"))
                    finished(f"{name}o{i}", event)
                    finished(f"{name}pv{n}", event)

                half = 1 - lin_last[0] if half is None else half
                for n in range(len(quads) + lag + 1):
                    if n < len(quads):
                        scores(n)
                    for part in (fills or {}).get(n, ()):
                        part(1 - half)
                    if lag <= n < len(quads) + lag:
                        turned(n - lag)
                    if n > lag:
                        product(n - lag - 1)

            pe.wait_ge(S("ones"), 1)
            pe.wait_ge(S("ident"), 1)
            pe.wait_ge(S("small_landed"), 16 * 8)
            ps = open_tmp("cols")
            pe.transpose(ps[:, 0, 0:P], stackA[:], ident[:])
            close_tmp(pe.transpose(ps[:, 0, P:P + 5], stackB[:], ident[0:5, 0:5]), "cols")
            ps = open_tmp("relvec")
            pe.wait_ge(S("rel_landed"), 32)
            close_tmp(pe.matmul(ps[0:16, 0, 0:DIST], relT[:], onehot[:], start=True, stop=True), "relvec")

            quads_a = [(i, g) for i in range(NT) for g in range(2)]
            for L in range(2):
                w = I["w_in"][L]
                pe.wait_ge(S("f_scaled"), L + 1)
                feature_major(f"f{L}hT", hs)
                operand_ready(read_of(f"f{L}hT0"), read_of(f"f{L}hT1"))
                linear_feat(f"f{L}f", w, F0, hT)
                linear_feat(f"f{L}qh", w, QH0, hT)
                linear_tok(f"f{L}kv", w, K0, 256, hT)
                if L:
                    ada_end()
                ada_start()
                linear_tok(f"f{L}q", w, Q0, HALF, hT)
                parts = [(c, first, k0) for c, first in
                         (("i", I0), ("z", Z0), ("g", G0), ("ga0", GA0), ("ga1", GA0 + HALF)) for k0 in (0, 4)]
                for lv in range(LEVELS + 1):
                    name = f"f{L}lv{lv}"
                    ps = open_tmp(name).rearrange("p a b -> p (a b)")
                    pe.wait_ge(S("level_ready"), (LEVELS + 1) * L + lv + 1)
                    left, right = (kin, qin) if lv == 0 else (decay[lv % 2], decay[lv % 2])
                    for n in range(4 if lv == LEVELS else 8):
                        if lv == LEVELS:
                            a, b = left[:, n, 0:P], right[:, n, P:T]
                        else:
                            cut = slice((n % 2) * P, (n % 2) * P + P)
                            a, b = left[:, n // 2, cut], right[:, n // 2, cut]
                        mm = pe.matmul(ps[:, n * P:(n + 1) * P], a, b, start=True, stop=True)
                    close_tmp(mm, name)
                    if lv in ADA_LEVELS:
                        ada_end()
                        ada_start()
                    c, first, k0 = parts[lv]
                    linear_part(f"f{L}{c}", w, first, HALF, hT, k0)
                pe.wait_ge(S("f_rope"), L + 1)
                transposes(f"f{L}kT", [kdup[:, i, g].rearrange("p a d -> p (a d)") for g in range(2) for i in range(NT)])
                transposes(f"f{L}qT", [qkv[:, i, k * P:(k + 1) * P] for k in range(4) for i in range(NT)])
                ps = open_lin(f"f{L}ho")
                wait_read(f"f{L}lv{LEVELS - 1}", f"f{L}lv{LEVELS}")
                for h in range(4):
                    cols = slice(h * P, (h + 1) * P)
                    pe.matmul(ps[:, 0, cols], scor[:, 2 * h, :], vh[:, 0, cols], start=True, stop=True)
                    pe.matmul(ps[:, 1, cols], cross[:, h, :], vh[:, 0, cols], start=True, stop=False)
                    mm = pe.matmul(ps[:, 1, cols], scor[:, 2 * h + 1, :], vh[:, 1, cols], start=False, stop=True)
                mm.then_inc(S("hgrn_out"), 1)
                finished(f"f{L}ho", (S("hgrn_out"), bump("hgrn_out")))
                def gates(name, first, k0):
                    return lambda half: linear_part(f"f{L}{name}", w, first, HALF, hT, k0, half=half)

                def turn_b(half):
                    pe.wait_ge(S("f_b"), L + 1)
                    feature_major(f"f{L}bT", hs[:, :, HALF:D], 4)

                wait_read(f"f{L}kT", f"f{L}qT")
                attention(f"f{L}a", quads_a,
                          lambda g, j, a: qTa[a * HD:(a + 1) * HD, 2 * g + j, :],
                          lambda g, j, a: kTd[a * HD:(a + 1) * HD, g, :],
                          lambda b, head: qkv[:, b, 640 + (head // 4) * HD:640 + (head // 4 + 1) * HD],
                          HD, QUAD, HALF, (Pq_first, pT_first),
                          {0: [gates("ga1", GA0 + HALF, 4)], 1: [gates("gh0", GH0, 0)], 2: [gates("gh0", GH0, 4)],
                           3: [gates("gh1", GH0 + HALF, 0)], 4: [gates("gh1", GH0 + HALF, 4), turn_b]},
                          half=turn_lin[f"f{L}ho"][0])
                ada_end()
                ada_start()
                pe.wait_ge(S("f_a"), L + 1)
                feature_major(f"f{L}aT", hs[:, :, 0:HALF], 4)
                wait_read(f"f{L}bT0")
                for c in range(2):
                    linear_tok(f"f{L}uh{c}", I["w_up_hgrn"][L], c * HALF, HALF, hT, kts=4, k_src=4)
                wait_read(f"f{L}aT0")
                def merged(h):
                    pe.wait_ge(S("f_merged"), 2 * L + h + 1)
                    transposes(f"f{L}mT{h}", [hs[:, i, k * P:(k + 1) * P]
                                              for k in range(4 * h, 4 * h + 4) for i in range(NT)])

                for c in range(2):
                    linear_part(f"f{L}ua{c}", I["w_up_attn"][L], c * HALF, HALF, hT, 0, kts=4,
                                mid=(lambda: merged(0)) if c else None)
                w_out = I["w_out"][L]
                for h in range(2):
                    wait_read(f"f{L}mT{h}")
                    for c in range(2):
                        linear_part(f"f{L}out{c}", w_out, c * HALF, HALF, hT, 4 * h, k_src=4 - 8 * h,
                                    mid=(lambda: merged(1)) if h == 0 and c == 0 else None)
                        if h == 0 and c == 1:
                            ada_end()
                            ada_start()

            def mixed(name):
                pe.wait_ge(S(f"{name}x"), 1)
                feature_major(f"{name}hT", x)
                operand_ready((S("mixed_low"), bump("mixed")), (S("mixed_low"), bump("mixed")))

            def project(name, w):
                feature_major(f"{name}oT", hs)
                operand_ready(read_of(f"{name}oT0"), read_of(f"{name}oT1"))
                for c in range(2):
                    linear_tok(f"{name}y{c}", w, c * HALF, HALF, hT)
                    if name == "s0" and c == 0:
                        ada_end()

            def mlp(name, w1, w2, chunks):
                mixed(name)
                groups = 8
                ys = None
                for g in range(groups + 1):
                    if g < groups:
                        feat_units(f"{name}u{g}", open_tmp(f"{name}u{g}"), w1, g * HALF, hT)
                    if g == 1:
                        ys = [open_lin(f"{name}y{c}") for c in range(2)]
                    if g >= 1:
                        pe.wait_ge(S(f"{name}act"), g)
                        b = (g - 1) % 2
                        for c in range(2):
                            for r, hi, lo in take_halves(HALF, (slice(0, HALF), win(w2, c * HALF, HALF, 4 * (g - 1)))):
                                for k in range(2):
                                    for i in range(NT):
                                        mm = product_tok(ys[c][:, i, :], (hbhi[:, b], hblo[:, b]), r + k, i,
                                                         hi[:, k, :], lo[:, k, :], g == 1 and r + k == 0,
                                                         g == groups and r + k == 3)
                                half_used(mm, f"{name}y{c}", f"{name}hb{g - 1}")
                    if 1 < g <= min(chunks + 1, 7):
                        ada_end()
                    if 0 < g <= chunks:
                        ada_start()

            quads_16 = [(i, g) for i in range(NT) for g in range(4)]

            w = I["a_w_in_2"][0]
            mixed("s0")
            ps = open_lin("s0misc")
            psk = open_tmp("s0ik")
            for k0 in (0, 4):
                operand(k0)
                for r, hi, lo in take_halves(392, (slice(0, T), win(w, 1024, T, k0)),
                                             (slice(T, T + 8), win(w, 1856, 8, k0)),
                                             (slice(264, 328), win(w, 1792, HD, k0)),
                                             (slice(328, 392), win(w, 1792, HD, k0))):
                    for k in range(2):
                        kk = k0 + r + k
                        for i in range(NT):
                            product_tok(ps[:, i, 0:T + 8], hT, kk, i, hi[:, k, 0:T + 8], lo[:, k, 0:T + 8],
                                        kk == 0, kk == KT - 1)
                        mm = product_feat(psk[:, 0, 0:T], hT, kk, hi[:, k, 264:392], lo[:, k, 264:392],
                                          kk == 0, kk == KT - 1)
                    half_used(mm, "s0misc", "s0ik")
            linear_feat("s0iq", w, 1280, hT)
            wait_read("s0ik", "s0iq")
            for i in range(NT):
                for g in range(2):
                    W = P * (i + 1)
                    ps = open_tmp(f"s0idx{i}{g}")
                    for j in range(2):
                        for a in range(2):
                            rows = slice(a * HD, (a + 1) * HD)
                            mm = pe.matmul(ps[:, a, j * W:(j + 1) * W], iqT[rows, 2 * g + j, i * P:(i + 1) * P],
                                           ikT[rows, 0:W], start=True, stop=True)
                    close_tmp(mm, f"s0idx{i}{g}")
                if i == 0:
                    linear_feat("s0q0", w, 0, hT)
            linear_feat("s0q1", w, HALF, hT)
            pe.wait_ge(S("s0ckvn"), 1)
            transposes("s0ckvT", [ckv[:, i, r * P:(r + 1) * P] for r in range(2) for i in range(NT)])
            slot = take((slice(0, HALF), I["a_w_uk_2"][0].rearrange("h d r -> (h d) r").rearrange(
                "(k p) r -> p k r", p=P)))
            uk = slot.rearrange("p a b -> p (a b)").rearrange("p (k r) -> p k r", k=KT)
            for r in range(2):
                ps = open_tmp(f"s0wuk{r}").rearrange("p a b -> p (a b)")
                for k in range(KT):
                    mm = pe.transpose(ps[:, k * P:(k + 1) * P], uk[:, k, r * P:(r + 1) * P], ident[:])
                close_tmp(mm, f"s0wuk{r}")
            wait_read("s0ckvT")
            slot = take((0, "wuv"), (1, "wuv"))
            uv = slot.rearrange("p a b -> p (a b)").rearrange("p (r n) -> p r n", r=2)
            for i in range(NT):
                ps = open_lin(f"s0v{i}")
                for c in range(2):
                    for r in range(2):
                        mm = pe.matmul(ps[:, c, :], ckvT[:, r, i * P:(i + 1) * P], uv[:, r, c * HALF:(c + 1) * HALF],
                                       start=(r == 0), stop=(r == 1))
                if i == 0:
                    mm.then_inc(S("s0v0_full"), 1)
                    finished("s0v0", (S("s0v0_full"), 1))
                else:
                    finished("s0v1", used(mm))
            wait_read("s0wuk0", "s0wuk1")
            for h in range(2):
                ps = open_tmp(f"s0k{h}")
                for c in range(4):
                    for r in range(2):
                        mm = pe.matmul(ps[:, c // 2, (c % 2) * T:(c % 2) * T + T],
                                       wukT[:, r, (4 * h + c) * P:(4 * h + c + 1) * P], ckvT[:, r, :],
                                       start=(r == 0), stop=(r == 1))
                close_tmp(mm, f"s0k{h}")
            wait_read("s0q0", "s0q1", "s0k0", "s0k1", "s0v0", "s0v1")
            heads = (lambda t: lambda g, j, a: t[a * HD:(a + 1) * HD, 2 * g + j, :])
            attention("s0", quads_16, heads(qT), heads(kT),
                      lambda b, head: vv[:, b, head * HD:(head + 1) * HD], HD, QUAD, D, (Pq_second, pT_second))
            wait_read("s0o0", "s0o1")
            project("s0", I["a_w_o_2"][0])
            mlp("s1", I["mlp_w1_2"][0], I["mlp_w2_2"][0], 7)

            w = I["b_w_in_2"][0]
            mixed("s2")
            for n in range(2):
                for part in range(2):
                    if n or part:
                        ada_end()
                        ada_start()
                    linear_feat(f"s2{'qk'[part]}{n}", w, part * D + n * HALF, hT)
            for n in range(2):
                ada_end()
                ada_start()
                linear_tok(f"s2v{n}", w, 2 * D + n * HALF, HALF, hT)
            ada_end()
            wait_read(*(f"s2{part}{n}" for part in "qkv" for n in range(2)))
            attention("s2", quads_16, heads(qT), heads(kT),
                      lambda b, head: vv[:, b, head * P:(head + 1) * P], P, 2, D, (Pq_second, pT_second), lag=2)
            pe.wait_ge(S("s2o"), 1)
            project("s2", I["b_w_o_2"][0])
            mlp("s3", I["mlp_w1_2"][1], I["mlp_w2_2"][1], 2)

        def full_tmp_of(eng, name):
            eng.wait_ge(*done[name])
            n = turn_tmp[name]
            return tmp_ps[:, 2 * (n % 2):2 * (n % 2) + 2, :]

        def full_lin_of(eng, name):
            eng.wait_ge(*done[name])
            half = turn_lin[name][0]
            return lin_ps[:, 2 * half:2 * half + 2, :]

        def read(ins, name):
            ins.then_inc(read_of(name)[0], 1)

        def flat(v):
            return v.rearrange("p a b -> p (a b)")

        @block.sync
        def _(sp):
            for n, unit in enumerate(units):
                if n >= RING:
                    sp.wait_ge(*units[n - RING]["release"])
                slot = ring[:, n % RING]
                for cols, src in unit["parts"]:
                    if isinstance(src, str):
                        r = cols
                        dst = slot.rearrange("p a b -> p (a b)")[:, r * D:(r + 1) * D].rearrange(
                            "p (h d) -> p h d", h=16)
                        sp.dma_start(dst, I["a_w_uv_2"][0, :, r * P:(r + 1) * P, :].rearrange(
                            "h p d -> p h d")).then_inc(S(f"w_landed{n % RING}"), 16)
                    elif src.shape[1] == KT:
                        sp.dma_start(slot.rearrange("p a b -> p (a b)").rearrange("p (k r) -> p k r", k=KT),
                                     src).then_inc(S(f"w_landed{n % RING}"), 16)
                    else:
                        sp.dma_start(slot[:, :, cols], src).then_inc(S(f"w_landed{n % RING}"), 16)
            sp.wait_ge(S("s4x"), 1)
            sp.dma_start(out.rearrange("b (i p) d -> p (b i) d", p=P), x[:]).then_inc(S("out_written"), 16)
            sp.wait_ge(S("out_written"), 16)

        @block.gpsimd
        def _(pool):
            def step(ins):
                ins.then_inc(S("pool_step"), 1)
                pool.wait_ge(S("pool_step"), bump("pool_step"))

            step(pool.memset(ident[:], 0.0))
            pool.affine_select(out=ident[:], in_=ident[:], compare_op=ALU.not_equal, fill=1.0, base=0,
                               pattern=[[-1, P]], channel_multiplier=1).then_inc(S("ident"), 1)
            pool.memset(ones[:], 1.0).then_inc(S("ones"), 1)
            step(pool.memset(band[:], 0.0))
            step(pool.affine_select(out=band[:, 0:P], in_=band[:, 0:P], compare_op=ALU.is_gt, fill=NEG, base=0,
                                    pattern=[[1, P]], channel_multiplier=-1))
            pool.affine_select(out=band[:, P:T], in_=band[:, P:T], compare_op=ALU.is_ge, fill=NEG, base=0,
                               pattern=[[-1, P]], channel_multiplier=1).then_inc(S("band"), 1)
            step(pool.iota(pairx[:, 0, :], pattern=[[0, P]], base=0, channel_multiplier=1))
            pool.iota(pairx[:, 1, :], pattern=[[1, P]], base=0, channel_multiplier=0).then_inc(S("pairs"), 1)
            step(pool.memset(chunkmask[:], 1.0))
            pool.memset(chunkmask[:].rearrange("p (c t) -> p c t", t=CHUNK)[:, :, 0:1], 0.0).then_inc(S("chunkmask"), 1)
            for j in range(ROPE_HALF):
                ins = pool.memset(invf[:, j:j + 1], float(np.float32(500000.0) ** np.float32(-j * 0.125)))
            ins.then_inc(S("invf"), 1)
            pool.memset(relT[:], 1.0).then_inc(S("relT_ones"), 1)
            pool.wait_ge(S("levels_both"), 1)
            pool.affine_select(out=levelmask[:, 1:, :], in_=levelmask[:, 1:, :], compare_op=ALU.is_gt, fill=0.0,
                               base=0, pattern=[[0, LEVELS - 1], [1, P]], channel_multiplier=-1
                               ).then_inc(S("levels"), 1)
            for n, (u, h, width) in enumerate(halves):
                pool.wait_ge(S("high_formed"), n + 1)
                pool.tensor_tensor(wlo[:, n % PARTS, :, 0:width], ring[:, u % RING, 2 * h:2 * h + 2, 0:width],
                                   whi[:, n % PARTS, :, 0:width].bitcast(F32), ALU.subtract
                                   ).then_inc(S("low_formed"), 1)

        @block.scalar
        def _(act):
            def step(ins):
                ins.then_inc(S("act_step"), 1)
                act.wait_ge(S("act_step"), bump("act_step"))

            act.dma_start(x[:], I["x"].rearrange("b (i p) d -> p (b i) d", p=P)).then_inc(S("x_landed"), 16)
            rows = 0
            for v in (I["norm_w"].rearrange("l (k p) -> (l k) p", p=P),
                      I["lb_logits"].rearrange("l (k p) -> (l k) p", p=P),
                      I["ada_b_2"].rearrange("l (k p) -> (l k) p", p=P),
                      I["c_2"].rearrange("b (k p) -> (b k) p", p=P)):
                act.dma_start(stackA[rows:rows + v.shape[0], :], v).then_inc(S("small_landed"), 16)
                rows += v.shape[0]
            rows = 0
            for v in (I["a_kv_norm_2"].rearrange("l (k p) -> (l k) p", p=P), I["b_subln_2"], I["hgrn_norm_w"]):
                act.dma_start(stackB[rows:rows + v.shape[0], :], v).then_inc(S("small_landed"), 16)
                rows += v.shape[0]
            act.dma_start(posi[:], I["positions"].rearrange("b (i p) -> p (b i)", p=P),
                          allow_slow_non_contiguous=True).then_inc(S("small_landed"), 16)
            act.dma_start(sinks[:], I["attn_sinks"].rearrange("l h -> (l h)").partition_broadcast(P)
                          ).then_inc(S("sinks_landed"), 16)
            act.dma_start(lamb[:].rearrange("p a d -> p (a d)"),
                          I["b_lambda_2"].rearrange("l a d -> (l a d)").partition_broadcast(P)
                          ).then_inc(S("lamb_landed"), 16)

            def gate_bias(layer, j):
                section = (2, 5)[j]
                act.dma_start(gmod[:, j, :], I["ada_b_2"][layer, section * D:(section + 1) * D].partition_broadcast(P)
                              ).then_inc(S(f"gbias_landed{j}"), 16)

            formed = [0]

            def high_parts(end, plain):
                for n in range(formed[0], min(end, len(halves))):
                    u, h, width = halves[n]
                    if any(event[1] > limit and event[0] is S(by) for by, limit in zip(("w_used", "ada_read"), plain)
                           for event in (v["release"] for v in units[max(0, u - 2 * RING):max(0, u - RING + 1)])):
                        return
                    act.wait_ge(S(f"w_landed{u % RING}"), units[u]["landed"])
                    if n >= PARTS:
                        act.wait_ge(S("half_used"), n - PARTS + 1)
                    act.copy(whi[:, n % PARTS, :, 0:width], ring[:, u % RING, 2 * h:2 * h + 2, 0:width]
                             ).then_inc(S("high_formed"), 1)
                    formed[0] = n + 1

            def ahead(name):
                high_parts(halves_at[name][0] + PARTS, halves_at[name][1])

            def full_tmp(name):
                ahead(name)
                return full_tmp_of(act, name)

            def full_lin(name):
                ahead(name)
                return full_lin_of(act, name)

            def high_of(name, k0, cols=None):
                ps = flat(full_tmp(name))
                if cols is None:
                    ins = act.copy(flat(hThi[:, k0:k0 + 4, :]), ps)
                elif isinstance(cols, list):
                    for k, col in enumerate(cols):
                        ins = act.activation(hThi[:, k0 + k, :], ps[:, k * T:(k + 1) * T], ACT.Copy, scale=col)
                else:
                    ins = act.activation(flat(hThi[:, k0:k0 + 4, :]), ps, ACT.Copy, scale=cols)
                ins.then_inc(S("operand_high"), 1)

            def squares(name, ready, after=None):
                if after:
                    ahead(after)
                act.wait_ge(*ready)
                for i in range(NT):
                    ins = act.activation(hs[:, i, :], x[:, i, :], ACT.Square, accum_out=st[:, 0, i, 0:1])
                ins.then_inc(S(f"{name}ss"), 1)

            def rough_rsqrt(name, v, y, after=None):
                if after:
                    ahead(after)
                act.wait_ge(S(f"{name}var"), 1)
                step(act.activation(y, v, ACT.Ln))
                act.activation(y, y, ACT.Exp, scale=-0.5).then_inc(S(f"{name}rough"), 1)

            def exps(name, n, W, Pq):
                ahead(f"{name}s{n}")
                act.wait_ge(S(f"{name}max"), n + 1)
                for s in range(QUAD):
                    ins = act.activation(Pq[n % 2][:, s, 0:W], Pq[n % 2][:, s, 0:W], ACT.Exp,
                                         bias=qst[:, n, 1, s:s + 1], accum_out=qst[:, n, 2, s:s + 1])
                return ins

            def attention(name, quads, per, bufs, sink=False, evacuate={}, lag=1):
                Pq, pT = bufs
                for n in range(len(quads) + lag):
                    if n in evacuate:
                        evacuate[n]()
                    if n < len(quads):
                        ins = exps(name, n, P * (quads[n][0] + 1), Pq)
                        if sink:
                            ins = act.activation(qst[:, n, 3, :], qst[:, n, 4, :], ACT.Exp)
                        ins.then_inc(S(f"{name}exp"), 1)
                    if n >= lag:
                        m = n - lag
                        ps = full_tmp(f"{name}p{m}")
                        if m >= 2:
                            act.wait_ge(*done[f"{name}pv{m - 2}"])
                        w = per * (quads[m][0] + 1) * P
                        read(act.copy(pT[m % 2][:, 0:w], flat(ps)[:, 0:w]), f"{name}p{m}")

            act.wait_ge(S("relT_ones"), 1)
            act.dma_start(relT[0:NBUCKET, :], I["rel_bias_2"]).then_inc(S("rel_landed"), 16)
            act.dma_start(onehot, I["onehot"]).then_inc(S("rel_landed"), 16)
            act.dma_start(lnp[:, 0, :], I["final_norm_w"].partition_broadcast(P)).then_inc(S("lnp_landed"), 32)
            act.wait_ge(*read_of("cols"))
            act.activation(csil[:], colA[:, 120:128], ACT.Silu).then_inc(S("csil"), 1)
            act.wait_ge(S("angles"), 1)
            act.activation(trig[:], ang[:], ACT.Sin).then_inc(S("trig"), 1)
            act.wait_ge(S("lb_max"), 1)
            act.activation(lbw[:, 0:2, :], lbw[:, 0:2, :], ACT.Exp).then_inc(S("lb_exp"), 1)
            act.wait_ge(S("lam_dots"), 1)
            act.activation(lams[:, 0:2], lams[:, 0:2], ACT.Exp).then_inc(S("lam_exp"), 1)

            act.wait_ge(*read_of("relvec"))
            act.dma_start(scratch, relvec).then_inc(S("scratch_written"), 16)
            for L in range(2):
                if L == 0:
                    for j in range(2):
                        gate_bias(0, j)
                    squares("f0", (S("x_landed"), 16))
                else:
                    squares("f1", read_of("f0out1"), "f0out1")
                rough_rsqrt(f"f{L}", st[:, 1, :, 0], st[:, 2, :, 0])
                for h in range(2):
                    high_of(f"f{L}hT{h}", 4 * h, [colA[:, 8 * L + k:8 * L + k + 1] for k in range(4 * h, 4 * h + 4)])
                ahead(f"f{L}f")
                act.wait_ge(*read_of(f"f{L}f"))
                act.activation(gate_p[:], gate_min[:], ACT.Exp)
                act.activation(gate_n[:], gate_max[:], ACT.Exp, scale=-1.0).then_inc(S("f_pn"), 1)
                act.wait_ge(S("f_sum"), L + 1)
                ins = act.activation(gate_lnsum[:], gate_lnsum[:], ACT.Ln)
                if L == 1:
                    ins = act.activation(gate_p[:], gate_p[:], ACT.Ln)
                ins.then_inc(S("f_ln"), 1)
                act.wait_ge(S("f_kexp"), L + 1)
                act.activation(kin[:], gate_max[:], ACT.Exp, scale=-1.0).then_inc(S("f_kin"), 1)
                ps = full_lin(f"f{L}qh")
                read(act.activation(flat(qin), flat(ps), ACT.Silu), f"f{L}qh")
                ps = full_lin(f"f{L}kv")
                read(act.copy(qkv[:, :, K0:K0 + 256], ps[:, :, 0:256]), f"f{L}kv")
                ps = full_lin(f"f{L}q")
                read(act.mul(qkv[:, :, 0:HALF], ps, HD ** -0.5), f"f{L}q")
                for lv in range(1, LEVELS + 1):
                    if lv >= 3:
                        ahead(f"f{L}lv{lv - 2}")
                    act.wait_ge(S("level_diff"), LEVELS * L + lv)
                    act.activation(decay[lv % 2][:], decay[lv % 2][:], ACT.Exp).then_inc(S("level_exp"), 1)
                    if lv % 2 == 0:
                        if lv == LEVELS and L == 0:
                            act.wait_ge(S("scratch_written"), 16)
                        c, dst, func = {2: ("i", vh, ACT.Copy), 4: ("z", zs, ACT.Silu), 6: ("g", zg, ACT.Silu),
                                        8: ("ga0", ga[:, :, 0:HALF], ACT.Sigmoid)}[lv]
                        ps = full_lin(f"f{L}{c}")
                        read(act.activation(dst[:] if c != "ga0" else dst, ps, func), f"f{L}{c}")
                name = f"f{L}lv{LEVELS}"
                ps = full_tmp(name)
                read(act.copy(flat(cross), flat(ps)[:, 0:HALF]), name)
                ps = full_tmp(f"f{L}qT")
                act.wait_ge(S("level_ready"), (LEVELS + 1) * (L + 1))
                read(act.copy(flat(qTa), flat(ps)), f"f{L}qT")
                ps = full_lin(f"f{L}ho")
                act.activation(hs[:, :, 0:HALF], ps, ACT.Square).then_inc(S("f_hsq"), 1)
                rough_rsqrt(f"f{L}h", st[:, 1], st[:, 2])
                def gate(name, dst):
                    ps = full_lin(name)
                    read(act.activation(dst, ps, ACT.Sigmoid), name)

                attention(f"f{L}a", [(i, g) for i in range(NT) for g in range(2)], QUAD,
                          (Pq_first, pT_first), True,
                          {0: lambda: gate(f"f{L}ga1", ga[:, :, HALF:D]),
                           3: lambda: gate(f"f{L}gh0", gh[:, :, 0:HALF]),
                           4: lambda: gate(f"f{L}gh1", gh[:, :, HALF:D])})
                high_of(f"f{L}bT0", 4, colB[:, 3 + L:4 + L])
                high_of(f"f{L}aT0", 0)
                for h in range(2):
                    high_of(f"f{L}mT{h}", 4 - 4 * h)

            squares("n", read_of("f1out1"), "f1out1")
            act.wait_ge(S("scratch_written"), 16)
            act.dma_start(Mbias, bass.AP(scratch.tensor, 0, [[1, P], [DIST, 16], [1, T]])).then_inc(S("Mbias"), 16)
            rough_rsqrt("n", st[:, 1, :, 0], st[:, 2, :, 0])

            def mixed(name, layer, j):
                for h in range(2):
                    ps = flat(full_tmp(f"{name}hT{h}"))
                    act.wait_ge(*read_of(f"ada{layer}_{(3, 9)[j]}"))
                    for k in range(4):
                        kk = 4 * h + k
                        ins = act.activation(flat(hs)[:, kk * T:(kk + 1) * T], ps[:, k * T:(k + 1) * T], ACT.Identity,
                                             bias=modc[:, layer, 2 * j, kk:kk + 1],
                                             scale=modc[:, layer, 2 * j + 1, kk:kk + 1])
                    read(ins, f"{name}hT{h}")

            def norm_weights(n):
                for k, v in enumerate((I["ln_g_2"], I["ln_b_2"])):
                    act.dma_start(lnp[:, k, :], v[n // 2, n % 2].partition_broadcast(P)
                                  ).then_inc(S("lnp_landed"), 16)

            def mlp(name, layer):
                mixed(name, layer, 1)
                norm_weights(2 * layer + 1)
                if layer == 0:
                    gate_bias(1, 0)
                for g in range(8):
                    ps = full_tmp(f"{name}u{g}")
                    if g >= 2:
                        act.wait_ge(S(f"{name}act"), g - 1)
                    read(act.activation(flat(hidden[g % 2]), flat(ps), ACT.Relu), f"{name}u{g}")
                rough_rsqrt(f"{name}ln", mv[:, :, 1], st[:, 2, :, 0], f"{name}y1")

            mixed("s0", 0, 0)
            norm_weights(0)
            ps = full_tmp("s0ik")
            read(act.copy(ikT[:], ps[:, 0, 0:T]), "s0ik")
            ps = full_lin("s0misc")
            act.copy(ckv[:], ps[:, :, 0:T]).then_inc(S("s0ckv"), 1)
            read(act.mul(iw[:], ps[:, :, T:T + 8], 8 ** -0.5 * HD ** -0.5), "s0misc")
            act.wait_ge(S("s0ckv"), 1)
            for i in range(NT):
                ins = act.activation(hs[:, i, 0:T], ckv[:, i, :], ACT.Square, accum_out=st[:, 0, i, 0:1])
            ins.then_inc(S("s0css"), 1)
            rough_rsqrt("s0c", st[:, 1, :, 0], st[:, 2, :, 0])
            ps = full_lin("s0iq")
            read(act.copy(flat(iqT), flat(ps)), "s0iq")
            for i in range(NT):
                for g in range(2):
                    n = 2 * i + g
                    W = P * (i + 1)
                    ps = full_tmp(f"s0idx{i}{g}")
                    if n >= 2:
                        act.wait_ge(S("s0idx_used"), n - 1)
                    for a in range(2):
                        ins = act.activation(Pq_second[n % 2][:, 2 * a:2 * a + 2, 0:W],
                                             ps[:, a, 0:2 * W].rearrange("p (j w) -> p j w", j=2), ACT.Relu)
                    read(ins, f"s0idx{i}{g}")
                if i == 0:
                    ps = full_lin("s0q0")
                    read(act.mul(flat(qT[:, 0:4, :]), flat(ps), HD ** -0.5), "s0q0")
            ps = full_lin("s0q1")
            read(act.mul(flat(qT[:, 4:8, :]), flat(ps), HD ** -0.5), "s0q1")
            for r in range(2):
                ps = full_tmp(f"s0wuk{r}")
                read(act.copy(wukT[:, r, :], flat(ps)), f"s0wuk{r}")
            for i in range(NT):
                ps = full_lin(f"s0v{i}")
                read(act.copy(vv[:, i, :], flat(ps)), f"s0v{i}")
            for h in range(2):
                ps = full_tmp(f"s0k{h}")
                read(act.copy(flat(kT[:, 4 * h:4 * h + 4, :]), flat(ps)), f"s0k{h}")
            quads = [(i, g) for i in range(NT) for g in range(4)]
            attention("s0", quads, QUAD, (Pq_second, pT_second))
            for h in range(2):
                high_of(f"s0oT{h}", 4 * h)
            rough_rsqrt("s0ln", mv[:, :, 1], st[:, 2, :, 0], "s0y1")
            mlp("s1", 0)
            mixed("s2", 1, 0)
            norm_weights(2)
            gate_bias(1, 1)
            for n in range(2):
                for part, dst, scale in (("q", qT, HD ** -0.5), ("k", kT, 1.0)):
                    ps = full_lin(f"s2{part}{n}")
                    read(act.mul(flat(dst[:, 4 * n:4 * n + 4, :]), flat(ps), scale), f"s2{part}{n}")
            for n in range(2):
                ps = full_lin(f"s2v{n}")
                read(act.copy(vv[:, :, n * HALF:(n + 1) * HALF], ps), f"s2v{n}")
            attention("s2", quads, 2, (Pq_second, pT_second), lag=2)
            for i in range(NT):
                ahead(f"s2o{i}")
                act.wait_ge(*read_of(f"s2o{i}"))
                ins = act.activation(osq[:, i, :], hs[:, i, :], ACT.Square)
            ins.then_inc(S("s2osq"), 1)
            rough_rsqrt("s2h", st[:, 1], st[:, 2])
            for h in range(2):
                high_of(f"s2oT{h}", 4 * h, lams[:, 4:5])
            rough_rsqrt("s2ln", mv[:, :, 1], st[:, 2, :, 0], "s2y1")
            mlp("s3", 1)

        @block.vector
        def _(dve):
            def step(ins):
                ins.then_inc(S("dve_step"), 1)
                dve.wait_ge(S("dve_step"), bump("dve_step"))

            def rsqrt(name, v, y, w):
                dve.wait_ge(S(f"{name}rough"), 1)
                step(dve.tensor_tensor(w, y, y, ALU.mult))
                step(dve.tensor_tensor(w, w, v, ALU.mult))
                step(dve.tensor_scalar(w, w, -0.5, 1.5, ALU.mult, ALU.add))
                step(dve.tensor_tensor(y, y, w, ALU.mult))

            def variance(name, ss, v, n, eps):
                dve.wait_ge(S(f"{name}ss"), 1)
                dve.tensor_scalar(v, ss, 1.0 / n, eps, ALU.mult, ALU.add).then_inc(S(f"{name}var"), 1)

            def low_of(name, k0, cols=None):
                ps = flat(full_tmp_of(dve, name))
                dve.wait_ge(S("operand_high"), bump("operand_low"))
                hi, lo = hThi[:].bitcast(F32), hTlo
                if cols is None:
                    ins = dve.tensor_tensor(flat(lo[:, k0:k0 + 4, :]), ps, flat(hi[:, k0:k0 + 4, :]), ALU.subtract)
                elif isinstance(cols, list):
                    for k, col in enumerate(cols):
                        ins = dve.scalar_tensor_tensor(lo[:, k0 + k, :], ps[:, k * T:(k + 1) * T], col,
                                                       hi[:, k0 + k, :], ALU.mult, ALU.subtract)
                else:
                    ins = dve.scalar_tensor_tensor(flat(lo[:, k0:k0 + 4, :]), ps, cols, flat(hi[:, k0:k0 + 4, :]),
                                                   ALU.mult, ALU.subtract)
                read(ins, name)

            dve.wait_ge(S("pairs"), 1)
            step(dve.tensor_tensor(pairx[:, 0, :], pairx[:, 0, :], pairx[:, 1, :], ALU.bitwise_xor))
            step(dve.tensor_copy(levelge[:, 0, :], pairx[:, 0, :]))
            for lv in range(1, LEVELS):
                dve.tensor_scalar(levelge[:, lv, :], levelge[:, 0, :], float(2 ** (lv - 1)), None, ALU.is_ge)
            step(dve.memset(levelge[:, LEVELS, :], 0.0))
            dve.tensor_scalar(levelmask[:, 0, :], levelge[:, 0, :], 0.0, None, ALU.is_equal)
            dve.tensor_tensor(levelmask[:, 1:, :], levelge[:, 1:LEVELS, :], levelge[:, 2:, :], ALU.subtract
                              ).then_inc(S("levels_both"), 1)
            ps = full_tmp_of(dve, "cols")
            dve.tensor_copy(colA[:], ps[:, 0, 0:P])
            read(dve.tensor_copy(colB[:], ps[:, 0, P:P + 5]), "cols")
            ps = full_tmp_of(dve, "relvec")
            read(dve.tensor_copy(relvec, ps[0:16, 0, 0:DIST]), "relvec")
            dve.wait_ge(S("small_landed"), 16 * 8)
            dve.wait_ge(S("invf"), 1)
            step(dve.tensor_copy(posf[:], posi[:]))
            for i in range(NT):
                for c in range(2):
                    ins = dve.tensor_scalar(ang[:, i, c, :], invf[:], posf[:, i:i + 1], None, ALU.mult)
            step(ins)
            for c in range(2):
                ins = dve.tensor_scalar(angk[:, :, c, :], ang[:, :, c, :], 1.0 / TURN, 0.25 * c, ALU.mult, ALU.add)
            step(ins)
            step(dve.tensor_scalar(angk[:], angk[:], ROUNDER, None, ALU.add))
            step(dve.tensor_scalar(angk[:], angk[:], -ROUNDER, None, ALU.add))
            for part in TURN_PARTS:
                step(dve.scalar_tensor_tensor(ang[:], angk[:], -part, ang[:], ALU.mult, ALU.add))
            step(dve.tensor_scalar(ang[:, :, 1, :], ang[:, :, 1, :], TURN / 4, None, ALU.add))
            dve.tensor_scalar(ang[:], ang[:], SIN_MAX, -SIN_MAX, ALU.min, ALU.max).then_inc(S("angles"), 1)
            step(dve.tensor_copy(lbw[:, 0:2, :], colA[:, 16:24].rearrange("p (l h) -> p l h", l=2)))
            step(dve.tensor_tensor(lbw[:, 2, :], lbw[:, 0, :], lbw[:, 1, :], ALU.max))
            dve.tensor_tensor(lbw[:, 0:2, :], lbw[:, 0:2, :], lbw[:, 2, :].unsqueeze(1).broadcast_to([P, 2, 4]),
                              ALU.subtract).then_inc(S("lb_max"), 1)
            dve.wait_ge(S("lb_exp"), 1)
            step(dve.tensor_tensor(lbw[:, 2, :], lbw[:, 0, :], lbw[:, 1, :], ALU.add))
            step(dve.reciprocal(lbw[:, 2, :], lbw[:, 2, :]))
            step(dve.tensor_tensor(lbw[:, 0:2, :], lbw[:, 0:2, :], lbw[:, 2, :].unsqueeze(1).broadcast_to([P, 2, 4]),
                                   ALU.mult))
            step(dve.tensor_tensor(lbw[:, 3, :], lbw[:, 0, :], lbw[:, 1, :], ALU.add))
            step(dve.tensor_tensor(lbw[:, 3, :], lbw[:, 3, :], lbw[:, 0, :], ALU.subtract))
            step(dve.tensor_scalar(lbw[:, 4, :], lbw[:, 3, :], -1.0, 1.0, ALU.mult, ALU.add))
            dve.wait_ge(S("lamb_landed"), 16)
            for n in range(2):
                step(dve.tensor_tensor(lamb[:, 2 * n, :], lamb[:, 2 * n, :], lamb[:, 2 * n + 1, :], ALU.mult))
                ins = dve.tensor_reduce(lams[:, n:n + 1], lamb[:, 2 * n, :], AX.X, ALU.add)
            ins.then_inc(S("lam_dots"), 1)
            dve.wait_ge(S("lam_exp"), 1)
            step(dve.tensor_tensor(lams[:, 2:3], lams[:, 1:2], lams[:, 0:1], ALU.subtract))
            step(dve.tensor_scalar(lams[:, 3:4], lams[:, 2:3], -LAM_INIT, None, ALU.add))
            step(dve.tensor_scalar(lams[:, 4:5], colB[:, 2:3], 1.0 - LAM_INIT, None, ALU.mult))
            dve.wait_ge(S("csil"), 1)
            started = [0]

            def ada_start():
                n = started[0]
                started[0] += 1
                acc = adasum[:, n % 2, :]
                for u in range(2):
                    at_unit = ada_units[n] + u
                    dve.wait_ge(S(f"w_landed{at_unit % RING}"), units[at_unit]["landed"])
                    for k in range(4):
                        w, c = ring[:, at_unit % RING, k, :], csil[:, 4 * u + k:4 * u + k + 1]
                        if u == 0 and k == 0:
                            ins = dve.tensor_scalar(acc, w, c, None, ALU.mult)
                        else:
                            ins = dve.scalar_tensor_tensor(acc, w, c, acc, ALU.mult, ALU.add)
                        if k < 3:
                            step(ins)
                    ins.then_inc(S("ada_read"), 1)
                    if u == 0:
                        dve.wait_ge(S("ada_read"), 2 * n + 1)

            def ada_end(n=None):
                n = started[0] - 1 if n is None else n
                layer, m = ADA[n]
                section, half = m // 2, m % 2
                name = f"ada{layer}_{m}"
                ps = full_tmp_of(dve, name)
                if section in (2, 5):
                    g = gmod[:, section // 4, half * HALF:(half + 1) * HALF]
                    dve.wait_ge(S(f"gbias_landed{section // 4}"), 16 * (layer + 1))
                    ins = dve.scalar_tensor_tensor(g, ps[:, 0, :], 1.0, g, ALU.add, ALU.add)
                else:
                    bias = colA[:, 24 + 48 * layer + 4 * m:24 + 48 * layer + 4 * m + 4]
                    row = {0: 0, 1: 1, 3: 2, 4: 3}[section]
                    ins = dve.scalar_tensor_tensor(modc[:, layer, row, 4 * half:4 * half + 4], ps[:, 0, 0:4],
                                                   1.0 if section in (1, 4) else 0.0, bias, ALU.add, ALU.add)
                read(ins, name)

            def ada_step():
                ada_start()
                ada_end(started[0] - 2)

            def softmax(name, n, quads, mask, Pq):
                i, g = quads[n]
                W = P * (i + 1)
                ps = full_tmp_of(dve, f"{name}s{n}")
                if n >= 2:
                    dve.wait_ge(*done[f"{name}p{n - 2}"])
                buf = Pq[n % 2]
                for a in range(2):
                    ins = dve.tensor_tensor(buf[:, 2 * a:2 * a + 2, 0:W],
                                            ps[:, a, 0:2 * W].rearrange("p (j w) -> p j w", j=2),
                                            mask(i, g, a), ALU.add)
                read(ins, f"{name}s{n}")
                dve.wait_ge(*read_of(f"{name}s{n}"))
                return buf[:, :, 0:W]

            def maximum(name, n, g, scores, sink=None):
                step(dve.tensor_reduce(qst[:, n, 0, :], scores, AX.X, ALU.max))
                if sink is not None:
                    step(dve.tensor_tensor(qst[:, n, 0, :], qst[:, n, 0, :], sink, ALU.max))
                    dve.tensor_tensor(qst[:, n, 4, :], sink, qst[:, n, 0, :], ALU.subtract)
                dve.tensor_scalar(qst[:, n, 1, :], qst[:, n, 0, :], -1.0, None, ALU.mult
                                  ).then_inc(S(f"{name}max"), 1)

            def by_slot(v):
                return v.rearrange("p (j a) -> p a j", a=2)

            def slots(v):
                return v.rearrange("p (a j) -> p a j", a=2)

            for L in range(2):
                variance(f"f{L}", st[:, 0, :, 0], st[:, 1, :, 0], D, EPS)
                rsqrt(f"f{L}", st[:, 1, :, 0], st[:, 2, :, 0], st[:, 0, :, 0])
                for i in range(NT):
                    ins = dve.tensor_scalar(hs[:, i, :], x[:, i, :], st[:, 2, i, 0:1], None, ALU.mult)
                ins.then_inc(S("f_scaled"), 1)
                for h in range(2):
                    low_of(f"f{L}hT{h}", 4 * h,
                           [colA[:, 8 * L + k:8 * L + k + 1] for k in range(4 * h, 4 * h + 4)])
                ps = full_lin_of(dve, f"f{L}f")
                dve.tensor_scalar(flat(gate_min), flat(ps), 0.0, None, ALU.min)
                read(dve.tensor_scalar(flat(gate_max), flat(ps), 0.0, None, ALU.max), f"f{L}f")
                dve.wait_ge(S("f_pn"), L + 1)
                if L == 1:
                    step(dve.tensor_tensor(flat(gate_lnsum), flat(gate_p), flat(gate_n), ALU.add))
                    for h in range(4):
                        ins = dve.scalar_tensor_tensor(gate_p[:, h, :], gate_n[:, h, :], lbw[:, 3, h:h + 1],
                                                       gate_p[:, h, :], ALU.mult, ALU.add)
                    ins.then_inc(S("f_sum"), 1)
                else:
                    dve.tensor_tensor(flat(gate_lnsum), flat(gate_p), flat(gate_n), ALU.add
                                      ).then_inc(S("f_sum"), 1)
                dve.wait_ge(S("f_ln"), L + 1)
                step(dve.tensor_tensor(flat(gate_p), flat(gate_p if L else gate_min), flat(gate_lnsum), ALU.subtract))
                dve.tensor_tensor(flat(gate_max), flat(gate_max), flat(gate_lnsum), ALU.add
                                  ).then_inc(S("f_kexp"), 1)
                dve.wait_ge(S("chunkmask"), 1)
                dve.wait_ge(S("f_kexp"), L + 1)
                step(dve.tensor_tensor_scan(flat(G), chunkmask[:], flat(gate_p), 0.0, ALU.mult, ALU.add))
                dve.wait_ge(S("f_kin"), L + 1)
                ins = dve.memset(flat(scor), 0.0)
                if L == 1:
                    for h in range(4):
                        ins = dve.tensor_scalar(kin[:, h, :], kin[:, h, :], lbw[:, 4, h:h + 1], None, ALU.mult)
                step(ins)
                (ada_step if L else ada_start)()
                dve.wait_ge(*read_of(f"f{L}qh"))
                dve.nop().then_inc(S("level_ready"), 1)

                def differences(lv):
                    buf = decay[lv % 2]
                    if lv >= 3:
                        dve.wait_ge(*done[f"f{L}lv{lv - 2}"])
                    if lv < LEVELS:
                        b = 2 ** (lv - 1)
                        g = flat(G).rearrange("p (n h b) -> p n h b", h=2, b=b)
                        d = flat(buf).rearrange("p (n h b) -> p n h b", h=2, b=b)
                        ref = g[:, :, 0, b - 1:b].broadcast_to([P, 4 * T // (2 * b), b])
                        if 2 * b <= CHUNK:
                            dve.tensor_tensor(d[:, :, 1, :], g[:, :, 1, :], ref, ALU.subtract)
                        else:
                            dve.tensor_copy(d[:, :, 1, :], g[:, :, 1, :])
                        ins = dve.tensor_tensor(d[:, :, 0, :], ref, g[:, :, 0, :], ALU.subtract)
                    else:
                        g = G.rearrange("p h (c t) -> p h c t", c=4)
                        d = buf.rearrange("p h (c t) -> p h c t", c=4)

                        def end(c):
                            return g[:, :, c, CHUNK - 1:CHUNK].broadcast_to([P, 4, CHUNK])

                        dve.tensor_copy(d[:, :, 2, :], g[:, :, 2, :])
                        dve.tensor_tensor(d[:, :, 3, :], g[:, :, 3, :], end(2), ALU.add)
                        dve.tensor_tensor(d[:, :, 1, :], end(1), g[:, :, 1, :], ALU.subtract)
                        step(dve.tensor_tensor(d[:, :, 0, :], end(0), g[:, :, 0, :], ALU.subtract))
                        ins = dve.tensor_tensor(d[:, :, 0, :], d[:, :, 0, :], end(1), ALU.add)
                    ins.then_inc(S("level_diff"), 1)

                def factors(lv):
                    dve.wait_ge(S("level_exp"), LEVELS * L + lv)
                    b = 2 ** (lv - 1)
                    d, q, k = (flat(v).rearrange("p (n h b) -> p n h b", h=2, b=b) for v in (decay[lv % 2], qin, kin))
                    dve.tensor_tensor(d[:, :, 1, :], d[:, :, 1, :], q[:, :, 1, :], ALU.mult)
                    dve.tensor_tensor(d[:, :, 0, :], d[:, :, 0, :], k[:, :, 0, :], ALU.mult
                                      ).then_inc(S("level_ready"), 1)

                def gather(lv):
                    ps = flat(full_tmp_of(dve, f"f{L}lv{lv}"))
                    if lv == 0:
                        dve.wait_ge(S("levels"), 1)
                    else:
                        dve.wait_ge(*read_of(f"f{L}lv{lv - 1}"))
                    read(dve.copy_predicated(scor[:], levelmask[:, lv, :].bitcast(I32).unsqueeze(1).broadcast_to([P, 8, P]),
                                             ps.rearrange("p (n t) -> p n t", n=8)), f"f{L}lv{lv}")

                def rotate():
                    dve.wait_ge(*read_of(f"f{L}kv"))
                    dve.wait_ge(*read_of(f"f{L}q"))
                    dve.wait_ge(S("trig"), 1)
                    for i in range(NT):
                        heads = qkv[:, i, 0:640].rearrange("p (h d) -> p h d", h=10)
                        x1, x2 = heads[:, :, 0:ROPE_HALF], heads[:, :, ROPE_HALF:2 * ROPE_HALF]
                        sin, cos = (trig[:, i, c, :].unsqueeze(1).broadcast_to([P, 10, ROPE_HALF]) for c in range(2))
                        dve.tensor_tensor(ropet[:, 0], x1, cos, ALU.mult)
                        dve.tensor_tensor(ropet[:, 1], x2, sin, ALU.mult)
                        dve.tensor_tensor(ropet[:, 2], x2, cos, ALU.mult)
                        step(dve.tensor_tensor(ropet[:, 3], x1, sin, ALU.mult))
                        dve.tensor_tensor(x1, ropet[:, 0], ropet[:, 1], ALU.subtract)
                        step(dve.tensor_tensor(x2, ropet[:, 2], ropet[:, 3], ALU.add))
                    for i in range(NT):
                        for a in range(2):
                            ins = dve.tensor_copy(kdup[:, i, :, a, :], qkv[:, i, K0:V0].rearrange("p (g d) -> p g d", g=2))
                    ins.then_inc(S("f_rope"), 1)

                differences(1)
                for lv in range(1, LEVELS + 1):
                    if lv < LEVELS:
                        differences(lv + 1)
                    factors(lv)
                    gather(lv - 1)
                    if lv - 1 in ADA_LEVELS:
                        ada_step()
                    if lv == 5:
                        rotate()
                ps = full_tmp_of(dve, f"f{L}kT")
                read(dve.tensor_copy(flat(kTd), flat(ps)[:, 0:2 * T]), f"f{L}kT")
                dve.wait_ge(S("f_hsq"), L + 1)
                if L == 0:
                    dve.memset(st[:, 0, :, 4:8], 1.0)
                dve.tensor_reduce(st[:, 0, :, 0:4], hs[:, :, 0:HALF].rearrange("p i (h d) -> p i h d", h=4),
                                  AX.X, ALU.add).then_inc(S(f"f{L}hss"), 1)
                variance(f"f{L}h", st[:, 0], st[:, 1], P, EPS)
                rsqrt(f"f{L}h", st[:, 1], st[:, 2], st[:, 0])
                ps = full_lin_of(dve, f"f{L}ho")
                for i in range(NT):
                    ins = dve.tensor_tensor(hs[:, i, HALF:D].rearrange("p (h d) -> p h d", h=4),
                                            ps[:, i, :].rearrange("p (h d) -> p h d", h=4),
                                            st[:, 2, i, 0:4].unsqueeze(2).broadcast_to([P, 4, P]), ALU.mult)
                read(ins, f"f{L}ho")
                dve.wait_ge(*read_of(f"f{L}ho"))
                dve.wait_ge(*read_of(f"f{L}g"))
                dve.tensor_tensor(hs[:, :, HALF:D], hs[:, :, HALF:D], zg[:], ALU.mult).then_inc(S("f_b"), 1)
                quads = [(i, g) for i in range(NT) for g in range(2)]
                name = f"f{L}a"
                dve.wait_ge(S("band"), 1)
                dve.wait_ge(S("sinks_landed"), 16)

                def window(i, g, a):
                    m = band[:] if i else band[:, P:T]
                    return m.unsqueeze(1).broadcast_to([P, 2, P * (i + 1)])

                def total(n):
                    i, g = quads[n]
                    dve.wait_ge(S(f"{name}exp"), n + 1)
                    step(dve.tensor_tensor(qst[:, n, 2, :], qst[:, n, 2, :], qst[:, n, 3, :], ALU.add))
                    dve.reciprocal(by_slot(rden[:, i, 4 * g:4 * g + 4]), slots(qst[:, n, 2, :])
                                   ).then_inc(S(f"{name}prob"), 1)

                for n, (i, g) in enumerate(quads):
                    sink = by_slot(sinks[:, 8 * L + 4 * g:8 * L + 4 * g + 4])
                    scores = softmax(name, n, quads, window, Pq_first)
                    maximum(name, n, g, scores, sink)
                    if n >= 1:
                        total(n - 1)
                total(3)
                low_of(f"f{L}bT0", 4, colB[:, 3 + L:4 + L])
                dve.wait_ge(S(f"{name}prob"), 4)
                dve.wait_ge(*done[f"{name}o1"])
                ps = full_lin_of(dve, f"{name}o0")
                for i in range(NT):
                    ins = dve.tensor_tensor(hs[:, i, 0:HALF].rearrange("p (h d) -> p h d", h=8),
                                            ps[:, i, :].rearrange("p (h d) -> p h d", h=8),
                                            rden[:, i, 0:8].unsqueeze(2).broadcast_to([P, 8, HD]), ALU.mult)
                read(ins, f"{name}o0")
                dve.wait_ge(*read_of(f"{name}o0"))
                dve.wait_ge(*read_of(f"f{L}z"))
                dve.tensor_tensor(hs[:, :, 0:HALF], hs[:, :, 0:HALF], zs[:], ALU.mult).then_inc(S("f_a"), 1)
                ada_step()
                low_of(f"f{L}aT0", 0)
                dve.wait_ge(*read_of(f"f{L}gh0"))
                dve.wait_ge(*read_of(f"f{L}gh1"))
                for c in range(2):
                    ps = full_lin_of(dve, f"f{L}uh{c}")
                    cols = slice(c * HALF, (c + 1) * HALF)
                    read(dve.tensor_tensor(gh[:, :, cols], ps, gh[:, :, cols], ALU.mult), f"f{L}uh{c}")
                for c in range(2):
                    cols = slice(c * HALF, (c + 1) * HALF)
                    ps = full_lin_of(dve, f"f{L}ua{c}")
                    read(dve.tensor_tensor(hs[:, :, cols], ps, ga[:, :, cols], ALU.mult), f"f{L}ua{c}")
                    dve.wait_ge(*read_of(f"f{L}ua{c}"))
                    dve.wait_ge(*read_of(f"f{L}uh{c}"))
                    dve.tensor_tensor(hs[:, :, cols], hs[:, :, cols], gh[:, :, cols], ALU.add
                                      ).then_inc(S("f_merged"), 1)
                    low_of(f"f{L}mT{c}", 4 - 4 * c)
                ada_step()
                for c in range(2):
                    cols = slice(c * HALF, (c + 1) * HALF)
                    ps = full_lin_of(dve, f"f{L}out{c}")
                    read(dve.tensor_tensor(x[:, :, cols], x[:, :, cols], ps, ALU.add), f"f{L}out{c}")

            variance("n", st[:, 0, :, 0], st[:, 1, :, 0], D, EPS)
            rsqrt("n", st[:, 1, :, 0], st[:, 2, :, 0], st[:, 0, :, 0])
            dve.wait_ge(S("lnp_landed"), 32)
            for i in range(NT):
                ins = dve.scalar_tensor_tensor(x[:, i, :], x[:, i, :], st[:, 2, i, 0:1], lnp[:, 0, :],
                                               ALU.mult, ALU.mult)
            ins.then_inc(S("s0x"), 1)

            def mixed(name):
                for h in range(2):
                    dve.wait_ge(*read_of(f"{name}hT{h}"))
                    whole = flat(hs)[:, 4 * h * T:4 * (h + 1) * T]
                    step(dve.tensor_copy(flat(hThi[:, 4 * h:4 * h + 4, :]), whole))
                    dve.tensor_tensor(flat(hTlo[:, 4 * h:4 * h + 4, :]), whole,
                                      flat(hThi[:, 4 * h:4 * h + 4, :].bitcast(F32)), ALU.subtract
                                      ).then_inc(S("mixed_low"), 1)

            def residual(name, n, after):
                for c in range(2):
                    cols = slice(c * HALF, (c + 1) * HALF)
                    ps = full_lin_of(dve, f"{name}y{c}")
                    g = gmod[:, n % 2, cols].unsqueeze(1).broadcast_to([P, NT, HALF])
                    read(dve.tensor_tensor(hs[:, :, cols], ps, g, ALU.mult), f"{name}y{c}")
                    dve.wait_ge(*read_of(f"{name}y{c}"))
                    step(dve.scalar_tensor_tensor(x[:, :, cols], x[:, :, cols], ALPHA, hs[:, :, cols],
                                                  ALU.mult, ALU.add))
                    for i in range(NT):
                        ins = dve.bn_stats(bns[:, i, c, :], x[:, i, cols])
                step(ins)
                for i in range(NT):
                    ins = dve.bn_aggr(mv[:, i, :], bns[:, i, :, :])
                step(ins)
                dve.tensor_scalar(mv[:, :, 1], mv[:, :, 1], LN_EPS, None, ALU.add).then_inc(S(f"{name}lnvar"), 1)
                rsqrt(f"{name}ln", mv[:, :, 1], st[:, 2, :, 0], st[:, 0, :, 0])
                dve.wait_ge(S("lnp_landed"), 32 * (n + 2))
                for i in range(NT):
                    step(dve.tensor_scalar(x[:, i, :], x[:, i, :], mv[:, i, 0:1], st[:, 2, i, 0:1],
                                           ALU.subtract, ALU.mult))
                for i in range(NT):
                    step(dve.tensor_tensor(x[:, i, :], x[:, i, :], lnp[:, 0, :], ALU.mult))
                for i in range(NT):
                    ins = dve.tensor_tensor(x[:, i, :], x[:, i, :], lnp[:, 1, :], ALU.add)
                ins.then_inc(S(f"{after}x"), 1)

            def mlp(name, n, after, chunks):
                mixed(name)
                for g in range(8):
                    dve.wait_ge(*read_of(f"{name}u{g}"))
                    if g >= 2:
                        dve.wait_ge(*done[f"{name}hb{g - 2}"])
                    h = flat(hidden[g % 2])
                    step(dve.tensor_tensor(h, h, h, ALU.mult))
                    step(dve.tensor_copy(flat(hbhi[:, g % 2]), h))
                    dve.tensor_tensor(flat(hblo[:, g % 2]), h, flat(hbhi[:, g % 2].bitcast(F32)), ALU.subtract
                                      ).then_inc(S(f"{name}act"), 1)
                    if g == 1:
                        ada_start()
                    elif 1 < g <= chunks:
                        ada_step()
                    elif g == chunks + 1:
                        ada_end()
                residual(name, n, after)

            def biased(i, g, a):
                return Mbias[:, 4 * g + a:4 * g + 4:2, 0:P * (i + 1)][:, :, ::-1]

            mixed("s0")
            dve.wait_ge(S("s0css"), 1)
            dve.tensor_scalar(st[:, 1, :, 0], st[:, 0, :, 0], 1.0 / T, LN_EPS, ALU.mult, ALU.add
                              ).then_inc(S("s0cvar"), 1)
            rsqrt("s0c", st[:, 1, :, 0], st[:, 2, :, 0], st[:, 0, :, 0])
            for i in range(NT):
                ins = dve.tensor_scalar(ckv[:, i, :], ckv[:, i, :], st[:, 2, i, 0:1], None, ALU.mult)
            ins.then_inc(S("s0ckvn"), 1)
            for i in range(NT):
                for g in range(2):
                    n = 2 * i + g
                    W = P * (i + 1)
                    dve.wait_ge(*read_of(f"s0idx{i}{g}"))
                    for s in range(QUAD):
                        head = 4 * g + 2 * (s % 2) + s // 2
                        r, v = Pq_second[n % 2][:, s, 0:W], iw[:, i, head:head + 1]
                        if g == 0 and s == 0:
                            ins = dve.tensor_scalar(isc[:, i, 0:W], r, v, None, ALU.mult)
                        else:
                            ins = dve.scalar_tensor_tensor(isc[:, i, 0:W], r, v, isc[:, i, 0:W], ALU.mult, ALU.add)
                        if s < QUAD - 1:
                            step(ins)
                    ins.then_inc(S("s0idx_used"), 1)
                    dve.wait_ge(S("s0idx_used"), n + 1)
            ps = flat(full_tmp_of(dve, "s0ckvT"))
            for r in range(2):
                ins = dve.tensor_scalar(ckvT[:, r, :], ps[:, r * T:(r + 1) * T], colB[:, r:r + 1], None, ALU.mult)
            read(ins, "s0ckvT")
            dve.wait_ge(S("band"), 1)
            for i in range(NT):
                v = isc[:, i, i * P:(i + 1) * P]
                ins = dve.tensor_tensor(v, v, band[:, P:T], ALU.add)
            step(ins)
            for i in range(NT):
                W = P * (i + 1)
                for n in range(TOPK // 8):
                    src = isc if n == 0 else iwk
                    step(dve.max(top8[:], src[:, i, 0:W]))
                    step(dve.match_replace(iwk[:, i, 0:W], top8[:], src[:, i, 0:W], LOWEST))
                step(dve.tensor_tensor(isc[:, i, 0:W], isc[:, i, 0:W], iwk[:, i, 0:W], ALU.is_equal))
                step(dve.tensor_scalar(isc[:, i, 0:W], isc[:, i, 0:W], NEG, None, ALU.mult))
            quads = [(i, g) for i in range(NT) for g in range(4)]
            dve.wait_ge(S("Mbias"), 16)

            def total_s0(n):
                i, g = quads[n]
                dve.wait_ge(S("s0exp"), n + 1)
                dve.reciprocal(by_slot(rden[:, i, 4 * g:4 * g + 4]), slots(qst[:, n, 2, :])
                               ).then_inc(S("s0prob"), 1)

            def scaled_out(i):
                dve.wait_ge(S("s0prob"), 4 * i + 4)
                ps = full_lin_of(dve, f"s0o{i}")
                read(dve.tensor_tensor(hs[:, i, :].rearrange("p (h d) -> p h d", h=16),
                                       flat(ps).rearrange("p (h d) -> p h d", h=16),
                                       rden[:, i, :].unsqueeze(2).broadcast_to([P, 16, HD]), ALU.mult), f"s0o{i}")

            for n, (i, g) in enumerate(quads):
                W = P * (i + 1)
                scores = softmax("s0", n, quads, biased, Pq_second)
                step(dve.tensor_tensor(scores, scores, isc[:, i, 0:W].unsqueeze(1).broadcast_to([P, QUAD, W]), ALU.add))
                maximum("s0", n, g, scores)
                if n >= 1:
                    total_s0(n - 1)
                if n == 6:
                    scaled_out(0)
            total_s0(7)
            scaled_out(1)
            for h in range(2):
                low_of(f"s0oT{h}", 4 * h)
            ada_end()
            residual("s0", 0, "s1")
            mlp("s1", 1, "s2", 7)
            mixed("s2")
            for _ in range(5):
                ada_step()
            ada_end()

            def combine(n):
                i, g = quads[n]
                W = P * (i + 1)
                dve.wait_ge(S("s2exp"), n + 1)
                step(dve.reciprocal(qst[:, n, 3, :], qst[:, n, 2, :]))
                step(dve.tensor_scalar(qst[:, n, 3, 2:4], qst[:, n, 3, 2:4], lams[:, 3:4], None, ALU.mult))
                for j in range(2):
                    ins = dve.tensor_scalar(Pq_second[n % 2][:, j, 0:W], Pq_second[n % 2][:, j, 0:W], qst[:, n, 3, j:j + 1],
                                            None, ALU.mult)
                step(ins)
                for j in range(2):
                    ins = dve.scalar_tensor_tensor(Pq_second[n % 2][:, j, 0:W], Pq_second[n % 2][:, 2 + j, 0:W],
                                                   qst[:, n, 3, 2 + j:3 + j], Pq_second[n % 2][:, j, 0:W], ALU.mult, ALU.add)
                ins.then_inc(S("s2prob"), 1)

            def raw_out(i):
                ps = full_lin_of(dve, f"s2o{i}")
                read(dve.tensor_copy(hs[:, i, :], flat(ps)), f"s2o{i}")

            for n, (i, g) in enumerate(quads):
                scores = softmax("s2", n, quads, biased, Pq_second)
                maximum("s2", n, g, scores)
                if n >= 1:
                    combine(n - 1)
                if n == 6:
                    raw_out(0)
            combine(7)
            raw_out(1)
            dve.wait_ge(S("s2osq"), 1)
            dve.tensor_reduce(st[:, 0], osq.rearrange("p i (h d) -> p i h d", h=8), AX.X, ALU.add
                              ).then_inc(S("s2hss"), 1)
            variance("s2h", st[:, 0], st[:, 1], P, LN_EPS)
            rsqrt("s2h", st[:, 1], st[:, 2], st[:, 0])
            for i in range(NT):
                o = hs[:, i, :].rearrange("p (h d) -> p h d", h=8)
                ins = dve.tensor_tensor(o, o, st[:, 2, i, :].unsqueeze(2).broadcast_to([P, 8, P]), ALU.mult)
            ins.then_inc(S("s2o"), 1)
            for h in range(2):
                low_of(f"s2oT{h}", 4 * h, lams[:, 4:5])
            residual("s2", 2, "s3")
            mlp("s3", 3, "s4", 2)


_INS = ["x", "positions", "norm_w", "w_in", "attn_sinks", "hgrn_norm_w", "w_up_attn", "w_up_hgrn", "w_out",
        "lb_logits", "final_norm_w", "c_2", "rel_bias_2", "ada_w_2", "ada_b_2", "ln_g_2", "ln_b_2", "a_w_in_2",
        "a_kv_norm_2", "a_w_uk_2", "a_w_uv_2", "a_w_o_2", "b_w_in_2", "b_lambda_2", "b_subln_2", "b_w_o_2",
        "mlp_w1_2", "mlp_w2_2"]


def kernel(**inputs):
    import concourse.bacc as _bacc
    from concourse.bass_utils import run_bass_kernel_spmd as _run

    nc = _bacc.Bacc("TRN2", target_bir_lowering=False, num_devices=1)
    arrays, args = {}, {}
    for name in _INS:
        a = np.ascontiguousarray(inputs[name])
        arrays[f"in_{name}"] = a
        args[name] = nc.dram_tensor(f"in_{name}", a.shape, mybir.dt.from_np(a.dtype), kind="ExternalInput").ap()
    onehot = bucket_onehot()
    arrays["onehot_table"] = onehot
    args["onehot"] = nc.dram_tensor("onehot_table", onehot.shape, F32, kind="ExternalInput").ap()
    out = nc.dram_tensor("out_0", (1, T, D), F32, kind="ExternalOutput").ap()
    build_program(nc, args, out)
    r = _run(nc, [arrays], core_ids=[0])
    return r.results[0]["out_0"]
```
